# Optimizing a Trainium2 kernel written in Bass

```python
import math
import numpy as np
import jax
import jax.numpy as jnp
from jax import lax

D_MODEL = 1024
BATCH = 1
SEQ = 512
DEPTH = 1

HEAD_DIM = 64
DIFF_WIDTH = D_MODEL // 2
NSA_WIDTH = D_MODEL - DIFF_WIDTH
DIFF_HEADS = DIFF_WIDTH // (2 * HEAD_DIM)
DIFF_V_DIM = 2 * HEAD_DIM
NSA_HEADS = NSA_WIDTH // HEAD_DIM
NSA_KV_HEADS = 2
NSA_GROUP = NSA_HEADS // NSA_KV_HEADS
CMP_BLOCK = 32
CMP_STRIDE = 16
CMP_HIDDEN = 2 * HEAD_DIM
SLC_BLOCK = 64
SLC_TOP = 16
WINDOW = 512
Q_BLOCK = 128
N_GROUPS = 8
EXPERTS_PER_GROUP = 8
N_EXPERTS = N_GROUPS * EXPERTS_PER_GROUP
TOP_K = 2
D_EXPERT = D_MODEL // 2
MOE_BLOCK = 128
NEG = -1e30
FORCE_BONUS = 1e4
EPS = 1e-6

IN_SPLITS = (DIFF_HEADS * 2 * HEAD_DIM, DIFF_HEADS * 2 * HEAD_DIM, DIFF_HEADS * DIFF_V_DIM,
             NSA_HEADS * HEAD_DIM) + (NSA_KV_HEADS * HEAD_DIM,) * 6 + (3 * NSA_HEADS,)
IN_COLS = sum(IN_SPLITS)

kernel_name = 'hymba_diffattn_nsa_hiermoe_block'

def rmsnorm(x, g):
    xf = x.astype(jnp.float32)
    y = xf * lax.rsqrt(jnp.mean(xf * xf, axis=-1, keepdims=True) + EPS)
    return (y * g.astype(jnp.float32)).astype(x.dtype)

def masked_softmax(s, mask):
    s = jnp.where(mask, s.astype(jnp.float32), NEG)
    m = jnp.max(s, axis=-1, keepdims=True)
    e = jnp.where(mask, jnp.exp(s - m), 0.0)
    return e / jnp.maximum(jnp.sum(e, axis=-1, keepdims=True), 1e-30)

def alibi_slopes(n):
    return np.array([2.0 ** (-8.0 * (i + 1) / n) for i in range(n)], dtype=np.float32)

def diff_attention(q, k, v, lam_q1, lam_k1, lam_q2, lam_k2, g_subln, lambda_init):
    B, S = q.shape[0], q.shape[1]
    nblk = S // Q_BLOCK
    scale = HEAD_DIM ** -0.5
    f32 = jnp.float32
    lam = (jnp.exp(jnp.sum(lam_q1.astype(f32) * lam_k1.astype(f32)))
           - jnp.exp(jnp.sum(lam_q2.astype(f32) * lam_k2.astype(f32))) + lambda_init)
    slopes = jnp.asarray(alibi_slopes(DIFF_HEADS))[:, None, None, None]
    qb = q.reshape(B, nblk, Q_BLOCK, DIFF_HEADS, 2, HEAD_DIM).transpose(1, 0, 3, 4, 2, 5)
    kt = k.transpose(0, 2, 3, 1, 4)
    vt = v.transpose(0, 2, 1, 3)
    kpos = jnp.arange(S)

    def block(args):
        q_blk, i = args
        qpos = i * Q_BLOCK + jnp.arange(Q_BLOCK)
        dist = qpos[:, None] - kpos[None, :]
        s = jnp.einsum('bhcqd,bhckd->bhcqk', q_blk, kt).astype(f32) * scale
        s = s - slopes * dist.astype(f32)
        p = masked_softmax(s, dist >= 0)
        a = p[:, :, 0] - lam * p[:, :, 1]
        return jnp.einsum('bhqk,bhkd->bhqd', a.astype(vt.dtype), vt)

    o = lax.map(block, (qb, jnp.arange(nblk)))
    o = o.transpose(1, 0, 3, 2, 4).reshape(B, S, DIFF_HEADS, DIFF_V_DIM)
    o = rmsnorm(o, g_subln) * (1.0 - lambda_init)
    return o.reshape(B, S, DIFF_WIDTH)

def nsa_attention(q, k_cmp, v_cmp, k_slc, v_slc, k_win, v_win, gates,
                  pos_k, pos_v, w1_k, w1_v, w2_k, w2_v):
    B, S = q.shape[0], q.shape[1]
    nblk = S // Q_BLOCK
    scale = HEAD_DIM ** -0.5
    f32 = jnp.float32
    slopes = jnp.asarray(alibi_slopes(NSA_HEADS).reshape(NSA_KV_HEADS, NSA_GROUP))[None, :, :, None, None]

    n_cmp = (S - CMP_BLOCK) // CMP_STRIDE + 1
    cidx = np.arange(n_cmp)[:, None] * CMP_STRIDE + np.arange(CMP_BLOCK)[None, :]
    cend = jnp.asarray(cidx[:, -1])

    def compress(t, pos, w1, w2):
        blocks = t[:, cidx] + pos[None, None, :, None, :]
        flat = blocks.transpose(0, 1, 3, 2, 4).reshape(B, n_cmp, NSA_KV_HEADS, CMP_BLOCK * HEAD_DIM)
        return jax.nn.gelu(flat @ w1) @ w2

    kc = compress(k_cmp, pos_k, w1_k, w2_k)
    vc = compress(v_cmp, pos_v, w1_v, w2_v)

    n_slc = S // SLC_BLOCK
    n_top = min(SLC_TOP, n_slc)
    cstart = cidx[:, 0]
    sstart = np.arange(n_slc) * SLC_BLOCK
    overlap = jnp.asarray(((cstart[:, None] < sstart[None, :] + SLC_BLOCK)
                           & (cstart[:, None] + CMP_BLOCK > sstart[None, :])).astype(np.float32))
    jblk = jnp.arange(n_slc)
    slc_kt = k_slc.transpose(0, 2, 1, 3)
    slc_vt = v_slc.transpose(0, 2, 1, 3)
    bi = jnp.arange(B)[:, None, None, None]
    hi = jnp.arange(NSA_KV_HEADS)[None, :, None, None]

    pad = ((0, 0), (WINDOW, 0), (0, 0), (0, 0))
    kw_pad = jnp.pad(k_win, pad)
    vw_pad = jnp.pad(v_win, pad)

    qb = q.reshape(B, nblk, Q_BLOCK, NSA_KV_HEADS, NSA_GROUP, HEAD_DIM).transpose(1, 0, 2, 3, 4, 5)
    gb = gates.reshape(B, nblk, Q_BLOCK, NSA_KV_HEADS, NSA_GROUP, 3).transpose(1, 0, 2, 3, 4, 5)

    def block(args):
        q_blk, g_blk, i = args
        q0 = i * Q_BLOCK
        qpos = q0 + jnp.arange(Q_BLOCK)
        dc = qpos[:, None] - cend[None, :]
        s = jnp.einsum('bqhgd,bkhd->bhgqk', q_blk, kc).astype(f32) * scale - slopes * dc.astype(f32)
        p_c = masked_softmax(s, dc >= 0)
        o_c = jnp.einsum('bhgqk,bkhd->bqhgd', p_c.astype(vc.dtype), vc)
        imp = jnp.einsum('bhgqk,kj->bhqj', p_c, overlap)
        cur = qpos[:, None] // SLC_BLOCK
        forced = (jblk[None, :] == 0) | (jblk[None, :] == cur) | (jblk[None, :] == cur - 1)
        valid = jblk[None, :] * SLC_BLOCK <= qpos[:, None]
        score = jnp.where(valid, imp + FORCE_BONUS * forced.astype(f32), NEG)
        _, top = lax.top_k(score, n_top)
        tok = (top[..., None] * SLC_BLOCK + jnp.arange(SLC_BLOCK)).reshape(
            B, NSA_KV_HEADS, Q_BLOCK, n_top * SLC_BLOCK)
        k_sel = slc_kt[bi, hi, tok]
        v_sel = slc_vt[bi, hi, tok]
        ds = qpos[None, None, :, None] - tok
        s = (jnp.einsum('bqhgd,bhqnd->bhgqn', q_blk, k_sel).astype(f32) * scale
             - slopes * ds[:, :, None].astype(f32))
        p_s = masked_softmax(s, (ds >= 0)[:, :, None])
        o_s = jnp.einsum('bhgqn,bhqnd->bqhgd', p_s.astype(v_sel.dtype), v_sel)
        kw = lax.dynamic_slice_in_dim(kw_pad, q0, WINDOW + Q_BLOCK, axis=1)
        vw = lax.dynamic_slice_in_dim(vw_pad, q0, WINDOW + Q_BLOCK, axis=1)
        wpos = q0 - WINDOW + jnp.arange(WINDOW + Q_BLOCK)
        dw = qpos[:, None] - wpos[None, :]
        s = jnp.einsum('bqhgd,bkhd->bhgqk', q_blk, kw).astype(f32) * scale - slopes * dw.astype(f32)
        p_w = masked_softmax(s, (dw >= 0) & (dw < WINDOW) & (wpos[None, :] >= 0))
        o_w = jnp.einsum('bhgqk,bkhd->bqhgd', p_w.astype(vw.dtype), vw)
        return g_blk[..., 0:1] * o_c + g_blk[..., 1:2] * o_s + g_blk[..., 2:3] * o_w

    o = lax.map(block, (qb, gb, jnp.arange(nblk)))
    return o.transpose(1, 0, 2, 3, 4, 5).reshape(B, S, NSA_WIDTH)

def hier_moe(h, w_rg, b_rg, w_re, b_re, w_gate, w_up, w_down):
    B, S, D = h.shape
    f32 = jnp.float32
    t = h.reshape(-1, D)
    T = t.shape[0]
    lg = (t @ w_rg).astype(f32) + b_rg.astype(f32)
    pg = jax.nn.softmax(lg, axis=-1)
    grp = jnp.argmax(lg, axis=-1)
    p_grp = jnp.take_along_axis(pg, grp[:, None], axis=-1)
    le = ((t @ w_re).astype(f32) + b_re.astype(f32)).reshape(T, N_GROUPS, EXPERTS_PER_GROUP)
    le = jnp.take_along_axis(le, grp[:, None, None], axis=1)[:, 0]
    top_v, top_i = lax.top_k(le, TOP_K)
    wts = jax.nn.softmax(top_v, axis=-1) * p_grp
    eidx = grp[:, None] * EXPERTS_PER_GROUP + top_i

    A = T * TOP_K
    flat_e = eidx.reshape(-1)
    order = jnp.argsort(flat_e)
    sorted_e = flat_e[order]
    counts = jnp.zeros((N_EXPERTS,), jnp.int32).at[flat_e].add(1)
    padded = (counts + MOE_BLOCK - 1) // MOE_BLOCK * MOE_BLOCK
    pad_end = jnp.cumsum(padded)
    pad_start = pad_end - padded
    start = jnp.cumsum(counts) - counts
    dest = pad_start[sorted_e] + (jnp.arange(A) - start[sorted_e])
    n_blocks = -(-A // MOE_BLOCK) + N_EXPERTS
    R = n_blocks * MOE_BLOCK
    xbuf = jnp.zeros((R, D), t.dtype).at[dest].set(t[order // TOP_K])
    blk_e = jnp.minimum(jnp.searchsorted(pad_end, jnp.arange(n_blocks) * MOE_BLOCK, side='right'),
                        N_EXPERTS - 1)

    def expert_block(args):
        xb, e = args
        hid = jax.nn.silu(xb @ w_gate[e]) * (xb @ w_up[e])
        return hid @ w_down[e]

    ybuf = lax.map(expert_block, (xbuf.reshape(n_blocks, MOE_BLOCK, D), blk_e)).reshape(R, D)
    y = jnp.zeros((A, D), ybuf.dtype).at[order].set(ybuf[dest])
    out = jnp.einsum('tkd,tk->td', y.reshape(T, TOP_K, D), wts.astype(y.dtype))
    return out.reshape(B, S, D)

def setup_inputs(seed: int = 0) -> dict:
    key = jax.random.key(seed)
    ks = jax.random.split(key, 32)
    f32 = jnp.float32
    L, D = DEPTH, D_MODEL

    def nrm(k, shape, scale):
        return jax.random.normal(k, shape, f32) * scale

    return {
        'x': nrm(ks[0], (BATCH, SEQ, D), 1.0),
        'c': nrm(ks[1], (BATCH, D), 1.0),
        'w_ada': nrm(ks[2], (L, D, 6 * D), 0.5 * D ** -0.5),
        'b_ada': nrm(ks[3], (L, 6 * D), 0.02),
        'g_pre_mix': 1.0 + nrm(ks[4], (L, D), 0.05),
        'g_post_mix': 1.0 + nrm(ks[5], (L, D), 0.05),
        'g_pre_ffn': 1.0 + nrm(ks[6], (L, D), 0.05),
        'g_post_ffn': 1.0 + nrm(ks[7], (L, D), 0.05),
        'w_in': nrm(ks[8], (L, D, IN_COLS), D ** -0.5),
        'lam_q1': nrm(ks[9], (L, HEAD_DIM), 0.1),
        'lam_k1': nrm(ks[10], (L, HEAD_DIM), 0.1),
        'lam_q2': nrm(ks[11], (L, HEAD_DIM), 0.1),
        'lam_k2': nrm(ks[12], (L, HEAD_DIM), 0.1),
        'g_subln': 1.0 + nrm(ks[13], (L, DIFF_V_DIM), 0.05),
        'cmp_pos_k': nrm(ks[14], (L, CMP_BLOCK, HEAD_DIM), 0.1),
        'cmp_pos_v': nrm(ks[15], (L, CMP_BLOCK, HEAD_DIM), 0.1),
        'cmp_w1_k': nrm(ks[16], (L, CMP_BLOCK * HEAD_DIM, CMP_HIDDEN), (CMP_BLOCK * HEAD_DIM) ** -0.5),
        'cmp_w1_v': nrm(ks[17], (L, CMP_BLOCK * HEAD_DIM, CMP_HIDDEN), (CMP_BLOCK * HEAD_DIM) ** -0.5),
        'cmp_w2_k': nrm(ks[18], (L, CMP_HIDDEN, HEAD_DIM), CMP_HIDDEN ** -0.5),
        'cmp_w2_v': nrm(ks[19], (L, CMP_HIDDEN, HEAD_DIM), CMP_HIDDEN ** -0.5),
        'w_out': nrm(ks[20], (L, D, D), D ** -0.5),
        'w_router_grp': nrm(ks[21], (L, D, N_GROUPS), D ** -0.5),
        'b_router_grp': nrm(ks[22], (L, N_GROUPS), 0.01),
        'w_router_exp': nrm(ks[23], (L, D, N_EXPERTS), D ** -0.5),
        'b_router_exp': nrm(ks[24], (L, N_EXPERTS), 0.01),
        'w_exp_gate': nrm(ks[25], (L, N_EXPERTS, D, D_EXPERT), D ** -0.5),
        'w_exp_up': nrm(ks[26], (L, N_EXPERTS, D, D_EXPERT), D ** -0.5),
        'w_exp_down': nrm(ks[27], (L, N_EXPERTS, D_EXPERT, D), D_EXPERT ** -0.5),
    }

def reference(x, c, w_ada, b_ada, g_pre_mix, g_post_mix, g_pre_ffn, g_post_ffn, w_in,
              lam_q1, lam_k1, lam_q2, lam_k2, g_subln, cmp_pos_k, cmp_pos_v,
              cmp_w1_k, cmp_w1_v, cmp_w2_k, cmp_w2_v, w_out,
              w_router_grp, b_router_grp, w_router_exp, b_router_exp,
              w_exp_gate, w_exp_up, w_exp_down):
    B, S = x.shape[0], x.shape[1]
    split_at = np.cumsum(IN_SPLITS)[:-1].tolist()
    for l in range(DEPTH):
        lambda_init = 0.8 - 0.6 * math.exp(-0.3 * l)
        mod = jax.nn.silu(c) @ w_ada[l] + b_ada[l]
        sh_a, sc_a, gt_a, sh_f, sc_f, gt_f = jnp.split(mod, 6, axis=-1)

        h = rmsnorm(x, g_pre_mix[l]) * (1.0 + sc_a[:, None, :]) + sh_a[:, None, :]
        u = jnp.einsum('bsd,de->bse', h, w_in[l])
        dq, dk, dv, nq, ck, cv, sk, sv, wk, wv, ng = jnp.split(u, split_at, axis=-1)
        kvs = (B, S, NSA_KV_HEADS, HEAD_DIM)
        o_a = diff_attention(dq.reshape(B, S, DIFF_HEADS, 2, HEAD_DIM),
                             dk.reshape(B, S, DIFF_HEADS, 2, HEAD_DIM),
                             dv.reshape(B, S, DIFF_HEADS, DIFF_V_DIM),
                             lam_q1[l], lam_k1[l], lam_q2[l], lam_k2[l], g_subln[l], lambda_init)
        gates = jax.nn.sigmoid(ng.astype(jnp.float32)).astype(u.dtype).reshape(B, S, NSA_HEADS, 3)
        o_b = nsa_attention(nq.reshape(B, S, NSA_HEADS, HEAD_DIM),
                            ck.reshape(kvs), cv.reshape(kvs), sk.reshape(kvs), sv.reshape(kvs),
                            wk.reshape(kvs), wv.reshape(kvs), gates,
                            cmp_pos_k[l], cmp_pos_v[l], cmp_w1_k[l], cmp_w1_v[l],
                            cmp_w2_k[l], cmp_w2_v[l])
        mix = jnp.concatenate([o_a, o_b], axis=-1) @ w_out[l]
        x = x + gt_a[:, None, :] * rmsnorm(mix, g_post_mix[l])

        h = rmsnorm(x, g_pre_ffn[l]) * (1.0 + sc_f[:, None, :]) + sh_f[:, None, :]
        f = hier_moe(h, w_router_grp[l], b_router_grp[l], w_router_exp[l], b_router_exp[l],
                     w_exp_gate[l], w_exp_up[l], w_exp_down[l])
        x = x + gt_f[:, None, :] * rmsnorm(f, g_post_ffn[l])
    return x


_drawn_inputs = setup_inputs


def setup_inputs(seed=0):
    import zlib

    import numpy as np

    out = dict(_drawn_inputs(seed))
    spreads = {}
    factors = {'g_post_ffn': 4.106,
     'lam_q1': 6.487,
     'lam_k1': 4.659,
     'cmp_pos_k': 8.0,
     'b_router_exp': 2.929}
    for name, (base, spread) in spreads.items():
        noise = np.random.default_rng([zlib.crc32(name.encode()), seed]).standard_normal(out[name].shape)
        drawn = base * np.exp(spread * noise) if base else spread * noise
        out[name] = jnp.asarray(drawn.astype(out[name].dtype))
    for name, factor in factors.items():
        out[name] = (out[name] * factor).astype(out[name].dtype)
    return out
```

```python
from contextlib import ExitStack

import concourse.bass as bass
from concourse import mybir

F32 = mybir.dt.float32
I32 = mybir.dt.int32
ALU = mybir.AluOpType
ACT = mybir.ActivationFunctionType
AX = mybir.AxisListType.X

P = 128
D = 1024
SEQ = 512
DC = D // P
NT = SEQ // P
HD = 64
NJ = 4
NSA_HEADS = 8
NCMP = 31
NCP = 32
CMP_BLOCK = 32
CMP_STRIDE = 16
NEG = -1e30
MAX_FLOOR = -1e20
SUM_FLOOR = 1e-30
EPS = 1e-6
LAMBDA_INIT = 0.8 - 0.6
SCALE = HD ** -0.5
NG = 8
NE = 64
NR = NG + NE
F = 512
CAP = 64
MAX_EXTRA = 2 * SEQ // (CAP + 1)
NCOL = NE + MAX_EXTRA + 1
NCMPR = SEQ // CAP - 1
NO_ROW = 1 << 14

C_DQ, C_DK, C_DV, C_NQ, C_KV = 0, 512, 1024, 1536, 2048
N_KV = 792
LEN = [P * (i + 1) for i in range(NT)]
QOFF = [P * i * (i + 1) // 2 for i in range(NT)]
TLEN = [SEQ - P * k for k in range(NT)]
TOFF = [sum(TLEN[:k]) for k in range(NT)]
NS = sum(LEN)

STEP_USES = (("A0", NT), ("A1", NT), ("CMP", 1), ("S0", NT), ("DQ", 1), ("S1", NT), ("DK", 1), ("W0", NT),
             ("SUB", 1), ("DV", 1), ("W1", NT), ("NQ", 1), ("ADA0", 1), ("ADA1", 1))


def first_uses(last):
    at, u = {}, 0
    for name, uses in STEP_USES:
        if not (last and name in ("DQ", "DK", "DV", "NQ")):
            at[name] = u
            u += uses
    return at, u


USE, USES = first_uses(False)
LAST_USE, LAST_USES = first_uses(True)
PRE_USES = 20
ALL_USES = PRE_USES + (NJ - 1) * USES + LAST_USES
PRE_PROJ = 14
NBANK = 4
PRE_T = 10
T_USES = 22
N_SMALL = 16
N_CONST = 14
V_LOOP = 40
AHEAD = 1
OVF = 400


def build(nc, x, c, w_ada, b_ada, g_pre_mix, g_post_mix, g_pre_ffn, g_post_ffn, w_in,
          lam_q1, lam_k1, lam_q2, lam_k2, g_subln, cmp_pos_k, cmp_pos_v, cmp_w1_k, cmp_w1_v,
          cmp_w2_k, cmp_w2_v, w_out, w_router_grp, b_router_grp, w_router_exp, b_router_exp,
          w_exp_gate, w_exp_up, w_exp_down, out):
    with ExitStack() as ctx:
        def sb(name, shape, dt=F32):
            return ctx.enter_context(nc.sbuf_tensor(name, shape, dt))

        def sem(name):
            return ctx.enter_context(nc.semaphore(name))

        exp_w = sb("exp_w", [P, 2, 3 * 4096])
        stream = sb("stream", [P, 2, 4096])
        ov = sb("ov", [P, 8, SEQ])
        mods = sb("mods", [P, NJ, D])
        modsf = mods[:, :, :].rearrange("p a b -> p (a b)")
        xs = sb("xs", [P, NT, D])
        qdn = sb("qdn", [P, 4, SEQ])
        qd = qdn[:, 0:2, :]
        qn = qdn[:, 2:4, :]
        kd = sb("kd", [P, SEQ])
        vd = sb("vd", [P, NT, P])
        ident = sb("ident", [P, P])
        ones = sb("ones", [P, P])
        dist = sb("dist", [P, SEQ])
        dist_c = sb("dist_c", [P, NT, NCP])
        kcp = sb("kcp", [P, NCP])
        vcp = sb("vcp", [P, 2, HD])
        pc = sb("pc", [P, 2, NT, NCP])
        gates = sb("gates", [P, 2, NJ * 3 * NT])
        ada_acc = sb("ada_acc", [P, 2, 512])
        small = sb("small", [P, 512])
        bias_r = sb("bias_r", [P, NR])
        w_r = sb("w_r", [P, DC, NR])

        e1 = exp_w[:, 1, :]
        hT = e1[:, 0:4096].rearrange("p (c t) -> p c t", c=DC)
        prob = e1[:, 4096:4096 + 3 * NS].rearrange("p (b n) -> p b n", b=3)
        probT = e1[:, 7936:7936 + 2 * NS].rearrange("p (b n) -> p b n", b=2)
        vsw = e1[:, 10496:10496 + 2 * SEQ].rearrange("p (w t n) -> p w t n", w=2, t=NT)
        cmp_w1 = e1[:, 4096:8192].rearrange("p (w b n) -> p w b n", w=2, b=16)
        ckp = e1[:, 8192:9216].rearrange("p (w h n) -> p w h n", w=2, h=2)
        cmp_h = e1[:, 9216:9344].rearrange("p (w n) -> p w n", w=2)
        cmp_g = e1[:, 9344:9472].rearrange("p (w n) -> p w n", w=2)
        posT = e1[:, 9472:9504].rearrange("p (w n) -> p w n", w=2)
        cmp_w2 = e1[:, 9504:9632].rearrange("p (w n) -> p w n", w=2)
        pos_in = e1[0:16, 9632:9888].rearrange("p (w n) -> p w n", w=2)
        lam_in = e1[:, 9888:10144].rearrange("p (w n) -> p w n", w=4)
        lam_junk = e1[:, 10144:10272].rearrange("p (w n) -> p w n", w=2)
        sqv = e1[:, 11520:11520 + SEQ]
        mod_row = e1[0:1, 0:2 * D]
        bc_rows = e1[:, 0:7 * D].rearrange("p (r n) -> p r n", r=7)
        w_kv = exp_w[:, 0, 4096:4096 + DC * N_KV].rearrange("p (c n) -> p c n", c=DC)
        ada_early = [exp_w[:, 0, 0:4096], stream[:, 0, :], stream[:, 1, :],
                     mods[:, :, :].rearrange("p a b -> p (a b)")]
        kslc = sb("kslc", [P, SEQ])
        kwin = sb("kwin", [P, SEQ])

        w_slot = stream[:, 0, :].rearrange("p (c n) -> p c n", c=DC)
        ada_slot = stream[:, 1, :].rearrange("p (c n) -> p c n", c=DC)
        wo = stream[:, :, :].rearrange("p a (c n) -> p (a c) n", c=4)

        cs = small[:, 0:8]
        craw = small[:, 8:16]
        cexp = small[:, 16:24]
        shc = small[:, 24:32]
        scc = small[:, 32:40]
        gpc = small[:, 40:48]
        bsh = small[:, 48:56]
        bsc = small[:, 56:64]
        ssq = small[:, 64:68]
        rstd = small[:, 68:72]
        slope = small[:, 72:75]
        qsc = small[:, 75:78]
        sl_r = small[:, 78:81]
        qs_r = small[:, 81:84]
        mx = small[:, 84:108].rearrange("p (m t) -> p m t", m=6)
        nmx = small[:, 108:132].rearrange("p (m t) -> p m t", m=6)
        lsum = small[:, 132:156].rearrange("p (m t) -> p m t", m=6)
        rl = small[:, 156:180].rearrange("p (m t) -> p m t", m=6)
        gcur = small[:, 180:204].rearrange("p (h b t) -> p h b t", h=2, b=3)
        cmx = small[:, 204:212]
        cl = small[:, 212:220]
        lam2 = small[:, 220:222]
        lame = small[:, 222:224]
        nlam = small[:, 224:225]
        gsub = small[:, 225:226]
        gsub2 = small[:, 227:228]
        lamd = small[:, 228:229]
        ssq2 = small[:, 232:240]
        rstd2 = small[:, 240:248]
        wts = small[:, 248:256].rearrange("p (t k) -> p t k", k=2)
        pgrp = small[:, 256:260]
        rt = small[:, 260:292].rearrange("p (a t) -> p a t", t=NT)
        extra_row = small[:, 296:360]
        ssq3 = small[:, 360:364]
        rstd3 = small[:, 364:368]
        key8 = small[:, 368:376]
        addr_f = small[:, 376:384]
        addr_i = sb("addr_i", [P, 8], I32)
        val_i = sb("val_i", [P, 8], I32)
        n_over = sb("n_over", [1, 1], I32)
        over_e = sb("over_e", [1, MAX_EXTRA + 1], I32)
        gidx = sb("gidx", [CAP, NCOL], I32)
        sidx = sb("sidx", [P, NCOL], I32)
        gcol = sb("gcol", [CAP, 2], I32)
        scol = sb("scol", [P, 2], I32)

        ovf = ov[:, :, :].rearrange("p a b -> p (a b)")
        xg = [ovf[0:CAP, b * D:(b + 1) * D] for b in range(2)]
        xT = [ovf[:, 2048 + b * 512:2560 + b * 512] for b in range(2)]
        yb = [ovf[:, 3072 + b * 512:3584 + b * 512] for b in range(2)]
        hbuf = qdn[:, :, :].rearrange("p a b -> p (a b)")[:, 0:1536].rearrange("p (b n) -> p b n", b=2)
        sg = [hbuf[:, b, 0:256] for b in range(2)]
        hid = [hbuf[:, b, 256:512] for b in range(2)]
        hidT = [hbuf[:, b, 512:768] for b in range(2)]
        streamf = stream[:, :, :].rearrange("p a b -> p (a b)")
        h2 = [streamf[:, b * D:(b + 1) * D] for b in range(2)]
        h2T = [streamf[:, (2 + b) * D:(3 + b) * D].rearrange("p (c t) -> p c t", c=DC) for b in range(2)]
        tmpx = ada_acc[:, :, :].rearrange("p a b -> p (a b)")
        sqj = qdn[:, 0:2, :]
        fsqj = tmpx
        list_tmp = tmpx[0:CAP, 0:NCOL]
        ytok = [streamf[:, b * 2 * D:(b + 1) * 2 * D] for b in range(2)]
        lg = qd[:, 0, 0:NT * NR].rearrange("p (t n) -> p t n", t=NT)
        le = qd[:, 1, 0:256].rearrange("p (t e) -> p t e", t=NT)
        eqg = qn[:, 0, 0:32].rearrange("p (t e) -> p t e", t=NT)
        ohg = qn[:, 0, 32:64].rearrange("p (t e) -> p t e", t=NT)
        eg = qn[:, 0, 64:96].rearrange("p (t e) -> p t e", t=NT)
        oh = [qn[:, 1, 0:256].rearrange("p (t e) -> p t e", t=NT),
              qn[:, 1, 256:512].rearrange("p (t e) -> p t e", t=NT)]
        lem = kd[:, 0:256].rearrange("p (t e) -> p t e", t=NT)
        key = kd[:, 256:512].rearrange("p (t e) -> p t e", t=NT)
        sel = vd[:, :, :].rearrange("p t n -> p (t n)")[:, 0:256].rearrange("p (t e) -> p t e", t=NT)
        msum = vd[:, :, :].rearrange("p t n -> p (t n)")[:, 256:512].rearrange("p (t e) -> p t e", t=NT)
        rank = kslc[:, 0:256].rearrange("p (t e) -> p t e", t=NT)
        rblk = kslc[:, 256:512].rearrange("p (t e) -> p t e", t=NT)
        cnt = kwin[:, 0:64]
        cum = kwin[:, 64:128]
        iota_e = kwin[:, 128:192]
        key64 = kwin[:, 192:256]
        base_e = kwin[:, 256:320]
        cmpx = streamf[:, 6 * D:7 * D]
        thr = streamf[:, 7 * D:8 * D]
        tri = dist[:, 0:P]

        ps = ctx.enter_context(nc.psum_tensor("ps", [P, 8, 512], F32))
        SB, TB, OD, ON = 0, 4, 6, 7

        h2_d = nc.dram_tensor("h2_d", (SEQ, D), F32, kind="Internal").ap()
        y_d = nc.dram_tensor("y_d", (2 * 2 * SEQ, D // 2), F32, kind="Internal").ap()
        list_d = nc.dram_tensor("list_d", (CAP * NCOL, 1), I32, kind="Internal").ap()

        d_x, d_c, d_small, d_kv, d_w1 = sem("d_x"), sem("d_c"), sem("d_small"), sem("d_kv"), sem("d_w1")
        d_ada0, d_ada3, d_win, d_ada = sem("d_ada0"), sem("d_ada3"), sem("d_win"), sem("d_ada")
        d_cols, d_wo, d_bc = sem("d_cols"), sem("d_wo"), sem("d_bc")
        d_gu = [sem("d_gu0"), sem("d_gu1")]
        d_wd = [sem("d_wd0"), sem("d_wd1")]
        k_ident, k_zero, k_const, k_router = sem("k_ident"), sem("k_zero"), sem("k_const"), sem("k_router")
        v_step, v_loop, p_step = sem("v_step"), sem("v_loop"), sem("p_step")
        cexp_ready, acc_ready, row_ready = sem("cexp_ready"), sem("acc_ready"), sem("row_ready")
        ssq_ready, ms_ready, rt_ready, rstd_ready, xn_ready = (
            sem("ssq_ready"), sem("ms_ready"), sem("rt_ready"), sem("rstd_ready"), sem("xn_ready"))
        cols_ready, gelu_ready, lam_ready, lame_ready, gexp_ready, loop_vars = (
            sem("cols_ready"), sem("gelu_ready"), sem("lam_ready"), sem("lame_ready"), sem("gexp_ready"),
            sem("loop_vars"))
        bank_full, bank_free = sem("bank_full"), sem("bank_free")
        tbank_full, tbank_free = sem("tbank_full"), sem("tbank_free")
        adacc_ready, neg_ready, exp_done, p_ready, values_done = (
            sem("adacc_ready"), sem("neg_ready"), sem("exp_done"), sem("p_ready"), sem("values_done"))
        cmp_sub, cmp_exp, sq_ready, subrt_ready, od_free, on_free = (
            sem("cmp_sub"), sem("cmp_exp"), sem("sq_ready"), sem("subrt_ready"), sem("od_free"), sem("on_free"))
        mods_ready, mix_full, mixsq, mixms, mixrt, x1_ready = (
            sem("mods_ready"), sem("mix_full"), sem("mixsq"), sem("mixms"), sem("mixrt"), sem("x1_ready"))
        x1sq, x1ms, x1rt, h2_ready, h2T_full, h2T_ready, rout_full, lg_ready = (
            sem("x1sq"), sem("x1ms"), sem("x1rt"), sem("h2_ready"), sem("h2T_full"),
            sem("h2T_ready"), sem("rout_full"), sem("lg_ready"))
        h2_stored = [sem("h2_stored0"), sem("h2_stored1")]
        eg_in, eg_out, e2_in, e2_out, m_ready, rank_full = (
            sem("eg_in"), sem("eg_out"), sem("e2_in"), sem("e2_out"), sem("m_ready"), sem("rank_full"))
        lists_empty, lists_zeroed, lists_stored, lists_loaded, addr_ready, idx_ready, over_ready = (
            sem("lists_empty"), sem("lists_zeroed"), sem("lists_stored"), sem("lists_loaded"),
            sem("addr_ready"), sem("idx_ready"), sem("over_ready"))
        xg_zero = sem("xg_zero")
        x_in = [sem("x_in0"), sem("x_in1")]
        y_out = [sem("y_out0"), sem("y_out1")]
        idx_cp, xT_full, xT_ready, gu_done, sg_ready, hid_ready, hT_full, hidT_ready, d_done, y_ready = (
            sem("idx_cp"), sem("xT_full"), sem("xT_ready"), sem("gu_done"), sem("sg_ready"), sem("hid_ready"),
            sem("hT_full"), sem("hidT_ready"), sem("d_done"), sem("y_ready"))
        o_gu, o_wd, o_x, o_idx, o_xT, o_xTr, o_gus, o_sg, o_hid, o_hT, o_hTr, o_y, o_yr, o_out = (
            sem("o_gu"), sem("o_wd"), sem("o_x"), sem("o_idx"), sem("o_xT"), sem("o_xTr"), sem("o_gus"), sem("o_sg"),
            sem("o_hid"), sem("o_hT"), sem("o_hTr"), sem("o_y"), sem("o_yr"), sem("o_out"))
        scores_seen, copy_seen, rows_seen = sem("scores_seen"), sem("copy_seen"), sem("rows_seen")
        o_stored = sem("o_stored")
        y_back = [sem("y_back0"), sem("y_back1")]
        f_ready, fsq, fms, frt, o_ready, stored = (
            sem("f_ready"), sem("fsq"), sem("fms"), sem("frt"), sem("o_ready"), sem("stored"))

        wg_v = w_exp_gate.rearrange("l e (p c) n -> (l e) p (c n)", p=P)
        wu_v = w_exp_up.rearrange("l e (p c) n -> (l e) p (c n)", p=P)
        wd_v = w_exp_down.rearrange("l e (h p j) n -> (l e h) p (j n)", h=2, p=P)
        gu_w = [exp_w[:, b, 0:8192].rearrange("p (g c n) -> p g c n", g=2, c=DC) for b in range(2)]
        dn_w = [exp_w[:, b, 8192:12288].rearrange("p (h j n) -> p h j n", h=2, j=2) for b in range(2)]
        w_in_v = w_in[0].rearrange("(p c) n -> p c n", p=P)
        w_ada_v = w_ada[0].rearrange("(p c) n -> p c n", p=P)

        def xn(t):
            return ovf[:, t * D:(t + 1) * D]

        def one(ap):
            return ap.rearrange("a p n -> (a p) n")

        def load_gu(eng, e, b, signal):
            eng.dma_start(exp_w[:, b, 0:4096], one(wg_v[bass.ds(e, 1)])).then_inc(signal, 16)
            eng.dma_start(exp_w[:, b, 4096:8192], one(wu_v[bass.ds(e, 1)])).then_inc(signal, 16)

        def load_wd(eng, e, b, signal):
            for half in range(2):
                eng.dma_start(exp_w[:, b, 8192 + half * 2048:10240 + half * 2048],
                              one(wd_v[bass.ds(e * 2 + half, 1)])).then_inc(signal, 16)

        def load_win(eng, j):
            for i, o in enumerate((C_DQ, C_DK, C_DV)):
                eng.dma_start(w_slot[:, :, i * P:(i + 1) * P], w_in_v[:, :, bass.ds(j * P + o, P)]).then_inc(d_win, 16)
            for hd in range(2):
                eng.dma_start(w_slot[:, :, 384 + hd * HD:448 + hd * HD],
                              w_in_v[:, :, bass.ds(j * HD + (C_NQ + hd * 256), HD)]).then_inc(d_win, 16)

        def bank_wait(eng, j, u):
            eng.wait_ge(bank_free, j * USES + (PRE_USES + u - NBANK + 1))

        MAPS = [(0, "A0", 0), (0, "A1", 1), (1, "S0", 2), (2, "S1", 0), (1, "W0", 1), (2, "W1", 2)]
        M_A0, M_A1, M_S0, M_S1, M_W0, M_W1 = range(6)
        T_A, T_S0, T_S1, T_W0, T_C, T_W1 = range(6)
        T_FIRST = [0, 4, 8, 12, 16, 18]
        PRE_V = 2

        block = ctx.enter_context(nc.Block())

        @block.sync
        def _(sp):
            sp.dma_start(xs[:, :, :], x[0].rearrange("(t p) n -> p t n", p=P)).then_inc(d_x, 16)
            for i, s in enumerate((d_ada0, d_win, d_ada, d_ada3)):
                sp.dma_start(ada_early[i].rearrange("p (c n) -> p c n", c=DC),
                             w_ada_v[:, :, i * 512:(i + 1) * 512]).then_inc(s, 16)
            sp.dma_start(w_kv, w_in_v[:, :, C_KV:C_KV + N_KV]).then_inc(d_kv, 16)
            for i, w in enumerate((cmp_w1_k, cmp_w1_v)):
                sp.dma_start(cmp_w1[:, i], w[0].rearrange("(b p) n -> p b n", p=P)).then_inc(d_w1, 16)
            sp.wait_ge(acc_ready, 2)
            load_win(sp, 0)
            sp.wait_ge(row_ready, 4)
            for dst, o in ((shc, 0), (scc, D)):
                sp.dma_start(dst, mod_row[0:1, o:o + D]).then_inc(d_cols, 16)
            sp.wait_ge(acc_ready, 3)

            def load_ada(j, half):
                sp.wait_ge(adacc_ready, j * 2 + (half + AHEAD))
                sp.dma_start(ada_slot, w_ada_v[:, :, bass.ds(j * D + (2 * D + half * 512), 512)]).then_inc(d_ada, 16)

            load_ada(0, 0)
            sp.wait_ge(bank_full, PRE_PROJ + 4)
            load_win(sp, 1)
            with sp.Fori(0, NJ - 2) as j:
                load_ada(j, 1)
                load_ada(j + 1, 0)
                sp.wait_ge(bank_full, j * USES + (PRE_USES + USE["NQ"] + 1))
                load_win(sp, j + 2)
            load_ada(NJ - 2, 1)
            load_ada(NJ - 1, 0)
            sp.wait_ge(bank_full, (NJ - 2) * USES + PRE_USES + USE["NQ"] + 1)
            sp.dma_start(wo[:, 0:4, :], w_out[0, 0:512, :].rearrange("(c p) n -> p c n", p=P)).then_inc(d_wo, 16)
            load_ada(NJ - 1, 1)
            sp.wait_ge(adacc_ready, 2 * NJ + AHEAD)
            for hd in range(2):
                sp.dma_start(wo[hd * HD:(hd + 1) * HD, 4:8, :],
                             w_out[0, 512 + hd * 256:768 + hd * 256, :].rearrange("(c p) n -> p c n", p=HD)).then_inc(d_wo, 16)
            sp.wait_ge(on_free, NJ + AHEAD)
            sp.wait_ge(od_free, NJ + AHEAD)
            for i, v in enumerate((b_ada[0:1, 2 * D:3 * D], b_ada[0:1, 3 * D:4 * D], b_ada[0:1, 4 * D:5 * D],
                                   b_ada[0:1, 5 * D:6 * D], g_post_mix, g_pre_ffn, g_post_ffn)):
                sp.dma_start(bc_rows[:, i, :], v.to_broadcast([P, D])).then_inc(d_bc, 16)
            sp.wait_ge(mods_ready, 4)
            load_gu(sp, 1, 1, d_gu[1])
            load_wd(sp, 1, 1, d_wd[1])

            for t in range(NT):
                sp.wait_ge(h2_ready, t + 1)
                sp.dma_start(h2_d[t * P:(t + 1) * P, :], h2[t % 2]).then_inc(h2_stored[t % 2], 16)
            sp.wait_ge(lists_stored, 2 * NT * 16)
            lv = list_d.rearrange("(s n) a -> s (n a)", n=NCOL)
            sp.dma_start(gidx[:, :], lv).then_inc(lists_loaded, 16)
            sp.dma_start(sidx[0:CAP, :], lv).then_inc(lists_loaded, 16)
            sp.dma_start(sidx[CAP:P, :], lv).then_inc(lists_loaded, 16)

            with sp.Fori(1, NE // 2) as g:
                for b in range(2):
                    sp.wait_ge(gu_done, g * 2 + (b - 1))
                    load_gu(sp, g * 2 + b, b, d_gu[b])
                    sp.wait_ge(d_done, g * 2 + (b - 1))
                    load_wd(sp, g * 2 + b, b, d_wd[b])
            sp.wait_ge(over_ready, 2)
            sp.wait_ge(d_done, NE)
            n_blocks = sp.value_load(n_over[0:1, 0:1], min_val=0, max_val=MAX_EXTRA)
            with sp.Fori(0, MAX_EXTRA) as k:
                with sp.If(k < n_blocks):
                    sp.wait_ge(o_y, k + AHEAD)
                    sp.wait_ge(over_ready, 2)
                    e = sp.value_load(over_e[0:1, bass.ds(k, 1)], min_val=0, max_val=NE - 1)
                    load_gu(sp, e, 0, o_gu)
                    load_wd(sp, e, 0, o_wd)

            for b in range(2):
                sp.wait_ge(y_out[b], 16 * (NE // 2))
            sp.wait_ge(o_stored, n_blocks + AHEAD)
            for t in range(NT):
                if t >= 2:
                    sp.wait_ge(o_ready, t - 1)
                for kk in range(2):
                    r0 = 2 * (kk * SEQ + t * P)
                    sp.dma_start(ytok[t % 2][:, kk * D:(kk + 1) * D],
                                 y_d[r0:r0 + 2 * P, :].rearrange("(p h) n -> p (h n)", h=2)).then_inc(y_back[t % 2], 16)
            for t in range(NT):
                sp.wait_ge(o_ready, t + 1)
                sp.dma_start(out[0, t * P:(t + 1) * P, :], xs[:, t, :]).then_inc(stored, 16)
            sp.wait_ge(stored, 16 * NT)

        @block.gpsimd
        def _(pool):
            pool.sem_inc(o_stored, AHEAD)
            steps = [0]

            def step(ins):
                steps[0] += 1
                ins.then_inc(p_step, 1)
                pool.wait_ge(p_step, steps[0])

            step(pool.memset(ident[:, :], 0.0))
            pool.affine_select(out=ident[:, :], in_=ident[:, :], compare_op=ALU.not_equal, fill=1.0, base=0,
                               pattern=[[-1, P]], channel_multiplier=1).then_inc(k_ident, 1)
            pool.memset(ones[:, :], 1.0).then_inc(k_ident, 1)
            pool.memset(qdn[:, :, :], 0.0).then_inc(k_zero, 1)
            pool.memset(kcp[:, :], 0.0).then_inc(k_zero, 1)
            pool.memset(vcp[:, :, :], 0.0).then_inc(k_zero, 1)
            for tile_, vals in ((slope, (1.0, 1.0, 2.0 ** -4)), (sl_r, (0.25, 0.5, 0.5)),
                                (qsc, (SCALE, SCALE, SCALE * 16)), (qs_r, (4.0, 2.0, 2.0))):
                for i, v in enumerate(vals):
                    pool.memset(tile_[:, i:i + 1], v).then_inc(k_const, 1)
            step(pool.iota(dist[:, :], pattern=[[1, SEQ]], base=-(SEQ - P), channel_multiplier=-1,
                           allow_small_or_imprecise_dtypes=True))
            pool.affine_select(out=dist[:, :], in_=dist[:, :], compare_op=ALU.is_ge, fill=NEG, base=SEQ - P,
                               pattern=[[-1, SEQ]], channel_multiplier=1).then_inc(k_const, 1)
            step(pool.iota(dist_c[:, :, :], pattern=[[-P, NT], [CMP_STRIDE, NCP]], base=CMP_BLOCK - 1,
                           channel_multiplier=-1, allow_small_or_imprecise_dtypes=True))
            pool.affine_select(out=dist_c[:, :, :], in_=dist_c[:, :, :], compare_op=ALU.is_ge, fill=NEG,
                               base=-(CMP_BLOCK - 1), pattern=[[P, NT], [-CMP_STRIDE, NCP]],
                               channel_multiplier=1).then_inc(k_const, 1)
            pool.iota(val_i[:, :], pattern=[[SEQ, 2], [P, NT]], base=0, channel_multiplier=1).then_inc(p_step, 1)
            steps[0] += 1
            pool.memset(gidx[:, :], NO_ROW).then_inc(lists_empty, 1)
            pool.wait_ge(lists_empty, 1)
            pool.dma_start(list_d.rearrange("(s n) a -> s (n a)", n=NCOL), gidx[:, :]).then_inc(lists_zeroed, 16)

            pool.wait_ge(on_free, NJ + AHEAD)
            pool.wait_ge(od_free, NJ + AHEAD)
            step(pool.memset(tri, 1.0))
            pool.affine_select(out=tri, in_=tri, compare_op=ALU.is_gt, fill=0.0, base=0,
                               pattern=[[1, P]], channel_multiplier=-1).then_inc(k_router, 1)
            pool.iota(iota_e, pattern=[[1, NE]], base=0, channel_multiplier=0,
                      allow_small_or_imprecise_dtypes=True).then_inc(k_router, 1)
            pool.iota(key64, pattern=[[-1, NE]], base=NE, channel_multiplier=0,
                      allow_small_or_imprecise_dtypes=True).then_inc(k_router, 1)
            pool.iota(key8, pattern=[[-1, NG]], base=NG, channel_multiplier=0,
                      allow_small_or_imprecise_dtypes=True).then_inc(k_router, 1)
            pool.wait_ge(mix_full, NT)
            pool.iota(thr[:, 0:NCMPR * NE], pattern=[[CAP, NCMPR], [0, NE]], base=CAP, channel_multiplier=0,
                      allow_small_or_imprecise_dtypes=True).then_inc(k_router, 1)
            pool.iota(thr[:, 512:512 + MAX_EXTRA + 1], pattern=[[1, MAX_EXTRA + 1]], base=0, channel_multiplier=0,
                      allow_small_or_imprecise_dtypes=True).then_inc(k_router, 1)
            for b in range(2):
                pool.memset(xg[b], 0.0).then_inc(xg_zero, 1)

            pool.wait_ge(addr_ready, 1)
            pool.wait_ge(lists_zeroed, 16)
            for i in range(2 * NT):
                pool.indirect_dma_start(list_d, bass.IndirectOffsetOnAxis(addr_i[:, i:i + 1], 0), val_i[:, i:i + 1], None,
                                        bounds_check=CAP * NCOL - 1, oob_is_err=False).then_inc(lists_stored, 16)

            gather_max = pool.to_reg(SEQ - 1)
            scatter_max = pool.to_reg(4 * SEQ - 1)

            def gather_rows(column, b, copied, copies, full):
                pool.tensor_copy(gcol[:, b:b + 1], gidx[:, column]).then_inc(copied, 1)
                pool.wait_ge(copied, copies)
                pool.sem_inc(copy_seen, 1)
                pool.indirect_dma_start(xg[b], None, h2_d, bass.IndirectOffsetOnAxis(gcol[:, b:b + 1], 0),
                                        bounds_check=gather_max, oob_is_err=False).then_inc(full, 16)

            def scatter_rows(column, b, copied, copies, full):
                pool.tensor_copy(scol[:, b:b + 1], sidx[:, column]).then_inc(copied, 1)
                pool.wait_ge(copied, copies)
                pool.sem_inc(copy_seen, 1)
                pool.indirect_dma_start(y_d, bass.IndirectOffsetOnAxis(scol[:, b:b + 1], 0), yb[b], None,
                                        bounds_check=scatter_max, oob_is_err=False).then_inc(full, 16)

            pool.wait_ge(idx_ready, 3)
            for b in range(2):
                pool.wait_ge(h2_stored[b], 16 * NT // 2)
            pool.wait_ge(xg_zero, 2)
            gather_rows(slice(0, 1), 0, idx_cp, 1, x_in[0])
            gather_rows(slice(1, 2), 1, idx_cp, 2, x_in[1])
            pool.wait_ge(y_ready, 1)
            scatter_rows(slice(0, 1), 0, idx_cp, 3, y_out[0])
            pool.wait_ge(xT_full, 1)
            gather_rows(slice(2, 3), 0, idx_cp, 4, x_in[0])
            pool.wait_ge(y_ready, 2)
            scatter_rows(slice(1, 2), 1, idx_cp, 5, y_out[1])
            with pool.Fori(1, NE // 2 - 1) as g:
                for b in (1, 0):
                    e = g * 2 + (2 - b)
                    pool.wait_ge(xT_full, g * 2 + (1 - b))
                    pool.wait_ge(x_in[b], g * 16 + 16 * (1 - b))
                    gather_rows(bass.ds(e, 1), b, idx_cp, g * 4 + (4 - 2 * b), x_in[b])
                    pool.wait_ge(y_ready, e)
                    pool.wait_ge(y_out[1 - b], g * 16)
                    scatter_rows(bass.ds(g * 2 + (1 - b), 1), 1 - b, idx_cp, g * 4 + (5 - 2 * b), y_out[1 - b])
            pool.wait_ge(xT_full, NE - 2)
            pool.wait_ge(x_in[1], 16 * (NE // 2 - 1))
            gather_rows(slice(NE - 1, NE), 1, idx_cp, 2 * NE - 2, x_in[1])
            for b in range(2):
                pool.wait_ge(y_ready, NE - 1 + b)
                pool.wait_ge(y_out[b], 16 * (NE // 2 - 1))
                scatter_rows(slice(NE - 2 + b, NE - 1 + b), b, idx_cp, 2 * NE - 1 + b, y_out[b])

            for b in range(2):
                pool.wait_ge(y_out[b], 16 * (NE // 2))
            pool.wait_ge(over_ready, 2)
            n_blocks = pool.value_load(n_over[0:1, 0:1], min_val=0, max_val=MAX_EXTRA)
            with pool.Fori(0, MAX_EXTRA) as k:
                with pool.If(k < n_blocks):
                    pool.wait_ge(o_xT, k + AHEAD)
                    gather_rows(bass.ds(k + NE, 1), 0, o_idx, k * 2 + 1, o_x)
                    pool.wait_ge(o_yr, k + 1)
                    scatter_rows(bass.ds(k + NE, 1), 0, o_idx, k * 2 + 2, o_out)
                    pool.wait_ge(o_out, k * 16 + 16)
                    pool.sem_inc(o_stored, 1)
                    pool.wait_ge(over_ready, 2)

        @block.tensor
        def _(pe):
            pe.sem_inc(o_y, AHEAD)
            pe.sem_inc(o_xT, AHEAD)

            def mm(out_, lhsT, rhs, start=True, stop=True):
                return pe.matmul(out_, lhsT, rhs, start=start, stop=stop, skip_group_check=True)

            lo, hi = slice(0, HD), slice(HD, P)
            pe.wait_ge(k_ident, 2)
            for i in range(4):
                pe.wait_ge(acc_ready, i + 1)
                mm(ps[:, SB + i, :], ones[:, :], ada_acc[:, i % 2, :]).then_inc(bank_full, 1)
            for c_ in range(DC):
                if c_ >= 2:
                    pe.wait_ge(tbank_free, c_ - 1)
                for t in range(NT):
                    pe.wait_ge(xn_ready, t + 1)
                    ins = pe.transpose(ps[:, TB + c_ % 2, t * P:(t + 1) * P], xn(t)[:, c_::DC], ident[:, :])
                ins.then_inc(tbank_full, 1)
            pe.wait_ge(d_small, 16 * N_SMALL)
            for w in range(2):
                pe.wait_ge(tbank_free, DC - 1 + w)
                pe.transpose(ps[:, TB + w, 0:16], pos_in[:, w, :], ident[0:16, 0:16]).then_inc(tbank_full, 1)
            pe.wait_ge(tbank_free, PRE_T)
            pe.wait_ge(d_kv, 16)
            for i, o in enumerate((0, 128, 256, 512)):
                pe.wait_ge(bank_free, i + 1)
                for c_ in range(DC):
                    ins = mm(ps[:, SB + i, :], w_kv[:, c_, o:o + P], hT[:, c_, :], c_ == 0, c_ == DC - 1)
                ins.then_inc(bank_full, 1)
            for t in range(NT):
                pe.wait_ge(bank_free, 4 + t + 1)
                for o, n, at in ((384, 128, 0), (640, 152, 128)):
                    for c_ in range(DC):
                        ins = mm(ps[:, SB + t, at:at + n], hT[:, c_, t * P:(t + 1) * P], w_kv[:, c_, o:o + n],
                                 c_ == 0, c_ == DC - 1)
                ins.then_inc(bank_full, 1)
            pe.wait_ge(d_w1, 32)
            for w in range(2):
                pe.wait_ge(bank_free, 8 + w + 1)
                for b in range(16):
                    mm(ps[:, SB + w, 0:62].rearrange("p (h n) -> p h n", h=2), cmp_w1[:, w, b, :],
                       ckp[:, w, :, b:b + 8 * (NCMP - 1) + 1:8], b == 0, b == 15)
                for b in range(16):
                    ins = mm(ps[:, SB + w, 62:63], cmp_w1[:, w, b, :], posT[:, w, b:b + 1], b == 0, b == 15)
                ins.then_inc(bank_full, 1)

            def project(name, u):
                if name == "DV":
                    for t in range(NT):
                        for c_ in range(DC):
                            ins = mm(ps[:, SB + u % NBANK, t * P:(t + 1) * P], hT[:, c_, t * P:(t + 1) * P],
                                     w_slot[:, c_, 256:384], c_ == 0, c_ == DC - 1)
                else:
                    o = {"DQ": 0, "DK": 128, "NQ": 384}[name]
                    for c_ in range(DC):
                        ins = mm(ps[:, SB + u % NBANK, :], w_slot[:, c_, o:o + P], hT[:, c_, :], c_ == 0, c_ == DC - 1)
                ins.then_inc(bank_full, 1)

            pe.wait_ge(d_win, 96)
            for i, name in enumerate(("DQ", "DK", "DV", "NQ")):
                pe.wait_ge(bank_free, PRE_PROJ + i - NBANK + 1)
                project(name, PRE_PROJ + i)
            pe.wait_ge(gelu_ready, 2)
            pe.wait_ge(bank_free, 15)
            for h, rows in enumerate((lo, hi)):
                ins = mm(ps[rows, SB + 2, 0:NCMP], cmp_w2[:, 0, :], cmp_g[:, 0, h * NCMP:(h + 1) * NCMP])
            ins.then_inc(bank_full, 1)
            pe.wait_ge(bank_free, 16)
            for h in range(2):
                ins = mm(ps[0:NCMP, SB + 3, h * HD:(h + 1) * HD], cmp_g[:, 1, h * NCMP:(h + 1) * NCMP], cmp_w2[:, 1, :])
            ins.then_inc(bank_full, 1)
            pe.wait_ge(bank_full, PRE_USES)
            pe.sem_inc(values_done, PRE_V)

            def head_step(j, last):
                at = LAST_USE if last else USE

                def bank(u):
                    return SB + u % NBANK

                def scores(m, q, k):
                    u = at[MAPS[m][1]]
                    for i in range(NT):
                        bank_wait(pe, j, u + i)
                        mm(ps[:, bank(u + i), 0:LEN[i]], q[:, i * P:(i + 1) * P], k[:, 0:LEN[i]]).then_inc(bank_full, 1)

                def next_heads(name):
                    if not last:
                        bank_wait(pe, j, at[name])
                        project(name, at[name])

                def turn(unit, buf):
                    pe.wait_ge(p_ready, j * 6 + (unit + 1))
                    for k in range(NT):
                        pe.wait_ge(tbank_free, j * T_USES + (PRE_T + T_FIRST[unit] + k - 1))
                        for i in range(k, NT):
                            ins = pe.transpose(ps[:, TB + k % 2, (i - k) * P:(i - k + 1) * P],
                                               prob[:, buf, QOFF[i] + k * P:QOFF[i] + (k + 1) * P], ident[:, :])
                        ins.then_inc(tbank_full, 1)

                def values(unit, bank_, rows, v, first):
                    for k in range(NT):
                        pe.wait_ge(tbank_free, j * T_USES + (PRE_T + T_FIRST[unit] + k + 1))
                        ins = mm(ps[rows, bank_, k * P:SEQ], v(k), probT[:, unit % 2, TOFF[k]:TOFF[k] + TLEN[k]],
                                 first and k == 0, k == NT - 1)
                    ins.then_inc(values_done, 1)

                pe.wait_ge(bank_free, j * USES + PRE_USES)
                scores(M_A0, qd[:, 0, :], kd)
                scores(M_A1, qd[:, 1, :], kd)
                bank_wait(pe, j, at["CMP"])
                for hd in range(2):
                    for i in range(NT):
                        ins = mm(ps[:, bank(at["CMP"]), (hd * NT + i) * NCP:(hd * NT + i + 1) * NCP],
                                 qn[:, hd, i * P:(i + 1) * P], kcp[:, :])
                ins.then_inc(bank_full, 1)
                scores(M_S0, qn[:, 0, :], kslc)
                if not last:
                    pe.wait_ge(d_win, j * 80 + 176)
                next_heads("DQ")
                turn(T_A, 0)
                pe.wait_ge(od_free, j + AHEAD)
                values(T_A, OD, slice(0, P), lambda k: vd[:, k, :], True)
                scores(M_S1, qn[:, 1, :], kslc)
                next_heads("DK")
                turn(T_S0, 2)
                pe.wait_ge(on_free, j + AHEAD)
                values(T_S0, ON, lo, lambda k: vsw[:, 0, k, lo], True)
                scores(M_W0, qn[:, 0, :], kwin)
                pe.wait_ge(sq_ready, j + 1)
                bank_wait(pe, j, at["SUB"])
                mm(ps[:, bank(at["SUB"]), :], ones[:, :], sqv).then_inc(bank_full, 1)
                next_heads("DV")
                turn(T_S1, 0)
                values(T_S1, ON, hi, lambda k: vsw[:, 0, k, hi], True)
                scores(M_W1, qn[:, 1, :], kwin)
                next_heads("NQ")
                turn(T_W0, 1)
                values(T_W0, ON, lo, lambda k: vsw[:, 1, k, lo], False)
                for half, name in enumerate(("ADA0", "ADA1")):
                    pe.wait_ge(adacc_ready, j * 2 + (half + 1 + AHEAD))
                    bank_wait(pe, j, at[name])
                    mm(ps[:, bank(at[name]), :], ones[:, :], ada_acc[:, half, :]).then_inc(bank_full, 1)
                pe.wait_ge(p_ready, j * 6 + (T_C + 1))
                for hd in range(2):
                    pe.wait_ge(tbank_free, j * T_USES + (PRE_T + T_FIRST[T_C] + hd - 1))
                    for i in range(NT):
                        ins = pe.transpose(ps[0:NCP, TB + hd, i * P:(i + 1) * P], pc[:, hd, i, :], ident[:, :])
                    ins.then_inc(tbank_full, 1)
                for hd, rows in enumerate((lo, hi)):
                    pe.wait_ge(tbank_free, j * T_USES + (PRE_T + T_FIRST[T_C] + hd + 1))
                    ins = mm(ps[rows, ON, :], vcp[:, hd, :], probT[:, T_C % 2, hd * SEQ:(hd + 1) * SEQ], False, True)
                ins.then_inc(values_done, 1)
                turn(T_W1, 2)
                values(T_W1, ON, hi, lambda k: vsw[:, 1, k, hi], False)

            with pe.Fori(0, NJ - 1) as j:
                head_step(j, False)
            head_step(NJ - 1, True)

            pe.wait_ge(bank_free, ALL_USES)
            pe.wait_ge(od_free, NJ + AHEAD)
            pe.wait_ge(on_free, NJ + AHEAD)
            pe.wait_ge(d_wo, 48)

            def mixer(t):
                for n in range(2):
                    for c_ in range(DC):
                        ins = mm(ps[:, 2 * t + n, :], ov[:, c_, t * P:(t + 1) * P], wo[:, c_, n * 512:(n + 1) * 512],
                                 c_ == 0, c_ == DC - 1)
                ins.then_inc(mix_full, 1)

            def turn_h2(t):
                pe.wait_ge(h2_ready, t + 1)
                for c_ in range(DC):
                    ins = pe.transpose(ps[:, 2 * t + c_ // 4, (c_ % 4) * P:(c_ % 4 + 1) * P], h2[t % 2][:, c_::DC],
                                       ident[:, :])
                ins.then_inc(h2T_full, 1)

            def logits(t):
                pe.wait_ge(h2T_ready, t + 1)
                for c_ in range(DC):
                    ins = mm(ps[:, 2 * t, 0:NR], h2T[t % 2][:, c_, :], w_r[:, c_, :], c_ == 0, c_ == DC - 1)
                ins.then_inc(rout_full, 1)

            for t in range(NT):
                mixer(t)
            for t in range(NT):
                turn_h2(t)
                logits(t)
            pe.wait_ge(m_ready, 1)
            pe.wait_ge(k_router, 6)
            for t in range(NT):
                for t2 in range(t):
                    mm(ps[:, 0, t * NE:(t + 1) * NE], ones[:, :], msum[:, t2, :], t2 == 0, False)
                mm(ps[:, 0, t * NE:(t + 1) * NE], tri, msum[:, t, :], t == 0, True)
            for t in range(NT):
                ins = mm(ps[:, 1, 0:NE], ones[:, :], msum[:, t, :], t == 0, t == NT - 1)
            ins.then_inc(rank_full, 1)

            def turn_rows(b, done):
                for c_ in range(DC):
                    ins = pe.transpose(ps[:, b, c_ * CAP:(c_ + 1) * CAP], xg[b][:, c_::DC], ident[0:CAP, 0:CAP])
                ins.then_inc(done, 1)

            def gate_up(b, done):
                for c_ in range(DC):
                    for h, rows in enumerate((lo, hi)):
                        ins = mm(ps[rows, 2 + b, :].rearrange("p (g n) -> p g n", g=2), xT[b][:, c_ * CAP:(c_ + 1) * CAP],
                                 gu_w[b][:, :, c_, h * 256:(h + 1) * 256], c_ == 0, c_ == DC - 1)
                ins.then_inc(done, 1)

            def turn_hidden(b, done):
                for jj in range(2):
                    ins = pe.transpose(ps[:, 4 + b, jj * P:(jj + 1) * P], hid[b][:, jj::2], ident[:, :])
                ins.then_inc(done, 1)

            def down(b, done):
                for i in range(4):
                    hf, jj = i // 2, i % 2
                    for n, rows in enumerate((lo, hi)):
                        ins = mm(ps[rows, 6 + b, :], hidT[b][:, jj * P + hf * CAP:jj * P + (hf + 1) * CAP],
                                 dn_w[b][:, hf, jj, n * 512:(n + 1) * 512], i == 0, i == 3)
                ins.then_inc(done, 1)

            pe.wait_ge(addr_ready, 1)
            with pe.Fori(0, NE // 2) as g:
                for b in range(2):
                    pe.wait_ge(x_in[b], g * 16 + 16)
                    pe.sem_inc(rows_seen, 1)
                    turn_rows(b, xT_full)
                    pe.wait_ge(xT_ready, g * 2 + (b + 1))
                    pe.wait_ge(d_gu[b], g * 32 + 32)
                    gate_up(b, gu_done)
                    pe.wait_ge(hid_ready, g * 2 + (b + 1))
                    turn_hidden(b, hT_full)
                    pe.wait_ge(hidT_ready, g * 2 + (b + 1))
                    pe.wait_ge(d_wd[b], g * 32 + 32)
                    down(b, d_done)
            pe.wait_ge(over_ready, 2)
            n_blocks = pe.value_load(n_over[0:1, 0:1], min_val=0, max_val=MAX_EXTRA)
            pe.wait_ge(y_ready, NE)
            with pe.Fori(0, MAX_EXTRA) as k:
                with pe.If(k < n_blocks):
                    pe.wait_ge(o_x, k * 16 + 16)
                    pe.sem_inc(rows_seen, 1)
                    turn_rows(0, o_xT)
                    pe.wait_ge(o_xTr, k + 1)
                    pe.wait_ge(o_gu, k * 32 + 32)
                    gate_up(0, o_gus)
                    pe.wait_ge(o_hid, k + 1)
                    turn_hidden(0, o_hT)
                    pe.wait_ge(o_hTr, k + 1)
                    pe.wait_ge(o_wd, k * 32 + 32)
                    down(0, o_y)
                    pe.wait_ge(o_yr, k + 1)
                    pe.wait_ge(over_ready, 2)

        @block.scalar
        def _(act):
            act.sem_inc(on_free, AHEAD)
            act.dma_start(craw, c.rearrange("a (p n) -> (a p) n", p=P)).then_inc(d_c, 16)

            def cols(v):
                return v.rearrange("a (p n) -> (a p) n", p=P)

            small_loads = [(gpc, cols(g_pre_mix)), (bsh, cols(b_ada[0:1, 0:D])), (bsc, cols(b_ada[0:1, D:2 * D])),
                           (gsub, g_subln.rearrange("a p -> p a")),
                           (pos_in[:, 0, :], cmp_pos_k[0].rearrange("(b r) d -> b (r d)", r=2)),
                           (pos_in[:, 1, :], cmp_pos_v[0].rearrange("(b r) d -> b (r d)", r=2)),
                           (cmp_w2[:, 0, :], cmp_w2_k[0]), (cmp_w2[:, 1, :], cmp_w2_v[0])]
            small_loads += [(lam_in[:, i, :], v.to_broadcast([P, HD])) for i, v in enumerate((lam_q1, lam_k1, lam_q2, lam_k2))]
            small_loads += [(w_r[:, :, 0:NG], w_router_grp[0].rearrange("(p n) g -> p n g", p=P)),
                            (w_r[:, :, NG:NR], w_router_exp[0].rearrange("(p n) g -> p n g", p=P)),
                            (bias_r[:, 0:NG], b_router_grp.to_broadcast([P, NG])),
                            (bias_r[:, NG:NR], b_router_exp.to_broadcast([P, NE]))]
            assert len(small_loads) == N_SMALL
            for dst, src in small_loads:
                act.dma_start(dst, src).then_inc(d_small, 16)

            act.wait_ge(d_c, 16)
            act.activation(cexp, craw, ACT.Exp, scale=-1.0).then_inc(cexp_ready, 1)
            act.wait_ge(d_x, 16)
            for t in range(NT):
                act.activation(xn(t), xs[:, t, :], ACT.Square, accum_out=ssq[:, t:t + 1]).then_inc(ssq_ready, 1)
            act.wait_ge(ms_ready, 1)
            act.activation(rstd, ssq, ACT.Sqrt).then_inc(rt_ready, 1)
            act.wait_ge(rstd_ready, 1)
            for t in range(NT):
                act.wait_ge(ssq_ready, t + 1)
                act.activation(xn(t), xs[:, t, :], ACT.Copy, scale=rstd[:, t:t + 1]).then_inc(xn_ready, 1)
            act.wait_ge(cols_ready, 2)
            for c_ in range(DC):
                act.wait_ge(tbank_full, c_ + 1)
                act.activation(hT[:, c_, :], ps[:, TB + c_ % 2, :], ACT.Identity, scale=scc[:, c_:c_ + 1],
                               bias=shc[:, c_:c_ + 1]).then_inc(tbank_free, 1)
            for w in range(2):
                act.wait_ge(tbank_full, DC + w + 1)
                act.activation(posT[:, w, :], ps[:, TB + w, 0:16], ACT.Copy).then_inc(tbank_free, 1)
            act.wait_ge(lam_ready, 2)
            act.activation(lame, lam2, ACT.Exp).then_inc(lame_ready, 1)
            act.wait_ge(bank_free, 12)
            act.activation(gates[:, :, :], gates[:, :, :], ACT.Exp, scale=-1.0).then_inc(gexp_ready, 1)
            for w in range(2):
                act.wait_ge(bank_free, 12 + w + 1)
                act.activation(cmp_g[:, w, 0:62], cmp_h[:, w, 0:62], ACT.Gelu_apprx_tanh,
                               bias=cmp_h[:, w, 62:63]).then_inc(gelu_ready, 1)
            act.wait_ge(bank_full, 12)
            load_gu(act, 0, 0, d_gu[0])
            load_wd(act, 0, 0, d_wd[0])
            act.wait_ge(bank_full, PRE_USES)

            def head_step(j, last):
                at = LAST_USE if last else USE

                def exps(m):
                    act.wait_ge(neg_ready, j * 6 + (m + 1))
                    for i in range(NT):
                        p_ = prob[:, MAPS[m][2], QOFF[i]:QOFF[i] + LEN[i]]
                        ins = act.activation(p_, p_, ACT.Exp, bias=nmx[:, m, i:i + 1], accum_out=lsum[:, m, i:i + 1])
                    ins.then_inc(exp_done, 1)

                def take(unit):
                    act.wait_ge(values_done, j * 6 + (PRE_V + unit - 1))
                    for k in range(NT):
                        act.wait_ge(tbank_full, j * T_USES + (PRE_T + T_FIRST[unit] + k + 1))
                        act.activation(probT[:, unit % 2, TOFF[k]:TOFF[k] + TLEN[k]], ps[:, TB + k % 2, 0:TLEN[k]],
                                       ACT.Copy).then_inc(tbank_free, 1)

                exps(M_A0)
                exps(M_A1)
                act.wait_ge(cmp_sub, j + 1)
                for hd in range(2):
                    p_ = pc[:, hd, :, :]
                    ins = act.activation(p_, p_, ACT.Exp, scale=slope[:, 1 + hd:2 + hd])
                ins.then_inc(cmp_exp, 1)
                exps(M_S0)
                take(T_A)
                act.wait_ge(values_done, j * 6 + (PRE_V + T_A + 1))
                act.wait_ge(od_free, j + AHEAD)
                act.activation(sqv, ps[:, OD, :], ACT.Square).then_inc(sq_ready, 1)
                exps(M_S1)
                take(T_S0)
                exps(M_W0)
                act.wait_ge(bank_free, j * USES + (PRE_USES + at["SUB"] + 1))
                act.activation(sqv, sqv, ACT.Sqrt).then_inc(subrt_ready, 1)
                take(T_S1)
                exps(M_W1)
                take(T_W0)
                act.wait_ge(values_done, j * 6 + (PRE_V + T_C - 1))
                for hd in range(2):
                    act.wait_ge(tbank_full, j * T_USES + (PRE_T + T_FIRST[T_C] + hd + 1))
                    act.activation(probT[0:NCP, T_C % 2, hd * SEQ:(hd + 1) * SEQ], ps[0:NCP, TB + hd, :],
                                   ACT.Copy).then_inc(tbank_free, 1)
                take(T_W1)
                act.wait_ge(values_done, j * 6 + (PRE_V + T_W1 + 1))
                act.activation(ovf[:, bass.ds(j * SEQ + 4 * SEQ, SEQ)], ps[:, ON, :], ACT.Copy).then_inc(on_free, 1)

            with act.Fori(0, NJ - 1) as j:
                head_step(j, False)
            head_step(NJ - 1, True)

            for t in range(NT):
                act.wait_ge(mix_full, t + 1)
                act.activation(sqj, ps[:, 2 * t:2 * t + 2, :], ACT.Square, accum_out=ssq2[:, t:t + 1]).then_inc(mixsq, 1)
                act.wait_ge(mixms, t + 1)
                act.activation(rstd2[:, t:t + 1], ssq2[:, t:t + 1], ACT.Sqrt).then_inc(mixrt, 1)
                act.wait_ge(x1_ready, t + 1)
                act.activation(sqj, xs[:, t, :].rearrange("p (a b) -> p a b", a=2), ACT.Square,
                               accum_out=ssq2[:, 4 + t:5 + t]).then_inc(x1sq, 1)
                act.wait_ge(x1ms, t + 1)
                act.activation(rstd2[:, 4 + t:5 + t], ssq2[:, 4 + t:5 + t], ACT.Sqrt).then_inc(x1rt, 1)
                act.wait_ge(h2T_full, t + 1)
                if t >= 2:
                    act.wait_ge(rout_full, t - 1)
                act.activation(h2T[t % 2], ps[:, 2 * t:2 * t + 2, :].rearrange("p a (c n) -> p (a c) n", c=4),
                               ACT.Copy).then_inc(h2T_ready, 1)
            act.wait_ge(eg_in, 1)
            act.activation(eg, eg, ACT.Exp).then_inc(eg_out, 1)
            act.wait_ge(e2_in, 1)
            act.activation(rt[:, 4, :], rt[:, 4, :], ACT.Exp).then_inc(e2_out, 1)

            def expert(e, b, buffer_free):
                act.wait_ge(xT_full, e + 1)
                act.activation(xT[b], ps[:, b, :], ACT.Copy).then_inc(xT_ready, 1)
                act.wait_ge(gu_done, e + 1)
                act.activation(sg[b], ps[:, 2 + b, 0:256], ACT.Silu).then_inc(sg_ready, 1)
                act.wait_ge(d_done, e + 1)
                if buffer_free is not None:
                    act.wait_ge(y_out[b], buffer_free)
                act.activation(yb[b], ps[:, 6 + b, :], ACT.Copy).then_inc(y_ready, 1)

            for b in range(2):
                expert(b, b, None)
            with act.Fori(1, NE // 2) as g:
                for b in range(2):
                    expert(g * 2 + b, b, g * 16)
            act.wait_ge(over_ready, 2)
            n_blocks = act.value_load(n_over[0:1, 0:1], min_val=0, max_val=MAX_EXTRA)
            act.wait_ge(y_out[0], 16 * (NE // 2))
            with act.Fori(0, MAX_EXTRA) as k:
                with act.If(k < n_blocks):
                    act.wait_ge(o_xT, k + (1 + AHEAD))
                    act.activation(xT[0], ps[:, 0, :], ACT.Copy).then_inc(o_xTr, 1)
                    act.wait_ge(o_gus, k + 1)
                    act.activation(sg[0], ps[:, 2, 0:256], ACT.Silu).then_inc(o_sg, 1)
                    act.wait_ge(o_y, k + (1 + AHEAD))
                    act.wait_ge(o_stored, k + AHEAD)
                    act.activation(yb[0], ps[:, 6, :], ACT.Copy).then_inc(o_yr, 1)

            for t in range(NT):
                act.wait_ge(f_ready, t + 1)
                act.activation(fsqj, ytok[t % 2][:, 0:D], ACT.Square, accum_out=ssq3[:, t:t + 1]).then_inc(fsq, 1)
                act.wait_ge(fms, t + 1)
                act.activation(rstd3[:, t:t + 1], ssq3[:, t:t + 1], ACT.Sqrt).then_inc(frt, 1)

        @block.vector
        def _(dve):
            dve.sem_inc(adacc_ready, AHEAD)
            dve.sem_inc(od_free, AHEAD)
            steps = [0]

            def step(ins):
                steps[0] += 1
                ins.then_inc(v_step, 1)
                dve.wait_ge(v_step, steps[0])

            def mean_square(ap, n):
                return dve.tensor_scalar(ap, ap, 1.0 / n, EPS, ALU.mult, ALU.add)

            dve.wait_ge(cexp_ready, 1)
            step(dve.tensor_scalar(cexp, cexp, 1.0, None, ALU.add))
            step(dve.reciprocal(cexp, cexp))
            step(dve.tensor_tensor(cs, craw, cexp, ALU.mult))
            dve.wait_ge(ssq_ready, NT)
            mean_square(ssq, D).then_inc(ms_ready, 1)
            dve.wait_ge(rt_ready, 1)
            dve.reciprocal(rstd, rstd).then_inc(rstd_ready, 1)

            def weigh(buf, w, advance, last):
                advance(dve.tensor_scalar(ada_acc[:, buf, :], w[:, 0, :], cs[:, 0:1], None, ALU.mult))
                for c_ in range(1, DC):
                    ins = dve.scalar_tensor_tensor(ada_acc[:, buf, :], w[:, c_, :], cs[:, c_:c_ + 1],
                                                   ada_acc[:, buf, :], ALU.mult, ALU.add)
                    if c_ < DC - 1:
                        advance(ins)
                ins.then_inc(last, 1)

            def copy_row(i):
                dve.wait_ge(bank_full, i + 1)
                dve.tensor_copy(mod_row[0:1, i * 512:(i + 1) * 512], ps[0:1, SB + i, :]).then_inc(row_ready, 1)

            for i, s in enumerate((d_ada0, d_win, d_ada, d_ada3)):
                dve.wait_ge(s, 16)
                if i >= 2:
                    dve.wait_ge(bank_full, i - 1)
                weigh(i % 2, ada_early[i].rearrange("p (c n) -> p c n", c=DC), step, acc_ready)
            for i in range(4):
                copy_row(i)
            dve.wait_ge(row_ready, 4)
            for i in range(4):
                dve.sem_inc(bank_free, 1)
            dve.wait_ge(d_small, 16 * N_SMALL)
            dve.wait_ge(d_cols, 32)
            step(dve.tensor_tensor(bsc, bsc, scc, ALU.add))
            dve.scalar_tensor_tensor(scc, bsc, 1.0, gpc, ALU.add, ALU.mult).then_inc(cols_ready, 1)
            dve.tensor_tensor(shc, shc, bsh, ALU.add).then_inc(cols_ready, 1)
            for i in range(2):
                dve.tensor_tensor_reduce(lam_junk[:, i, :], lam_in[:, 2 * i, :], lam_in[:, 2 * i + 1, :], 1.0, 0.0,
                                         ALU.mult, ALU.add, lam2[:, i:i + 1]).then_inc(lam_ready, 1)
            step(dve.tensor_scalar(gsub, gsub, 1.0 - LAMBDA_INIT, None, ALU.mult))
            dve.wait_ge(lame_ready, 1)
            step(dve.tensor_tensor(lamd, lame[:, 0:1], lame[:, 1:2], ALU.subtract))
            step(dve.tensor_scalar(nlam, lamd, -1.0, -LAMBDA_INIT, ALU.mult, ALU.add))

            dve.wait_ge(k_zero, 3)
            for w in range(2):
                dve.wait_ge(bank_full, 4 + w + 1)
                for h, rows in enumerate((slice(0, HD), slice(HD, P))):
                    for par, to in enumerate((slice(0, HD), slice(HD, P))):
                        ins = dve.tensor_copy(ckp[to, w, h, :], ps[rows, SB + w, par::2])
                ins.then_inc(bank_free, 1)
            for i, k_ in ((2, kslc), (3, kwin)):
                dve.wait_ge(bank_full, 4 + i + 1)
                dve.tensor_copy(k_[:, :], ps[:, SB + i, :]).then_inc(bank_free, 1)
            gv = gates[:, :, :].rearrange("p h (n t) -> p h n t", t=NT)
            for t in range(NT):
                dve.wait_ge(bank_full, 8 + t + 1)
                dve.tensor_copy(vsw[:, :, t, :], ps[:, SB + t, 0:256].rearrange("p (w n) -> p w n", w=2))
                dve.tensor_copy(gv[:, :, :, t], ps[:, SB + t, 256:280].rearrange("p (h n) -> p h n", h=2)).then_inc(bank_free, 1)
            for w in range(2):
                dve.wait_ge(bank_full, 12 + w + 1)
                dve.tensor_copy(cmp_h[:, w, 0:63], ps[:, SB + w, 0:63]).then_inc(bank_free, 1)
            dve.wait_ge(gexp_ready, 1)
            step(dve.tensor_scalar(gates[:, :, :], gates[:, :, :], 1.0, None, ALU.add))
            step(dve.reciprocal(gates[:, :, :], gates[:, :, :]))

            def drain(name, u):
                src = ps[:, SB + u % NBANK, :]
                if name in ("DQ", "NQ"):
                    q, (c0, c1) = (qd, (0, 0)) if name == "DQ" else (qn, (1, 2))
                    dve.tensor_scalar(q[0:HD, 0, :], src[0:HD], qsc[0:HD, c0:c0 + 1], None, ALU.mult)
                    ins = dve.tensor_scalar(q[HD:P, 1, :], src[HD:P], qsc[HD:P, c1:c1 + 1], None, ALU.mult)
                elif name == "DK":
                    ins = dve.tensor_copy(kd[:, :], src)
                else:
                    ins = dve.tensor_copy(vd[:, :, :].rearrange("p t n -> p (t n)"), src)
                ins.then_inc(bank_free, 1)

            dve.wait_ge(k_const, N_CONST)
            step(dve.tensor_tensor(qsc, qsc, qs_r, ALU.mult))
            for i, name in enumerate(("DQ", "DK", "DV", "NQ")):
                dve.wait_ge(bank_full, PRE_PROJ + i + 1)
                drain(name, PRE_PROJ + i)
            dve.wait_ge(bank_full, 19)
            dve.tensor_copy(kcp[:, 0:NCMP], ps[:, SB + 2, 0:NCMP]).then_inc(bank_free, 1)
            dve.wait_ge(bank_full, 20)
            dve.tensor_copy(vcp[0:NCMP, :, :], ps[0:NCMP, SB + 3, 0:P].rearrange("p (h n) -> p h n", h=2)).then_inc(bank_free, 1)

            def head_step(j, last):
                at = LAST_USE if last else USE
                n = [0]

                def lstep(ins):
                    n[0] += 1
                    ins.then_inc(v_loop, 1)
                    dve.wait_ge(v_loop, j * V_LOOP + n[0])

                def full(u):
                    dve.wait_ge(bank_full, j * USES + (PRE_USES + u + 1))

                def self_read(u):
                    dve.wait_ge(bank_free, j * USES + (PRE_USES + u + 1))

                def bank(u):
                    return SB + u % NBANK

                def next_heads(name):
                    if not last:
                        full(at[name])
                        drain(name, at[name])

                def biased(m, buf_free):
                    col_, name, buf = MAPS[m]
                    u = at[name]
                    dve.wait_ge(tbank_full, j * T_USES + (PRE_T + buf_free))
                    for i in range(NT):
                        full(u + i)
                        dve.sem_inc(scores_seen, 1)
                        dve.tensor_tensor_reduce(prob[:, buf, QOFF[i]:QOFF[i] + LEN[i]], ps[:, bank(u + i), 0:LEN[i]],
                                                 dist[:, SEQ - LEN[i]:SEQ], slope[:, col_:col_ + 1], -3.0e38, ALU.add,
                                                 ALU.max, mx[:, m, i:i + 1]).then_inc(bank_free, 1)
                    self_read(u + NT - 1)
                    dve.tensor_scalar(nmx[:, m, :], mx[:, m, :], -1.0, None, ALU.mult).then_inc(neg_ready, 1)

                def weighted(m, g_):
                    buf = MAPS[m][2]
                    dve.wait_ge(exp_done, j * 6 + (m + 1))
                    lstep(dve.tensor_scalar(rl[:, m, :], lsum[:, m, :], SUM_FLOOR, None, ALU.max))
                    lstep(dve.reciprocal(rl[:, m, :], rl[:, m, :]))
                    lstep(dve.tensor_tensor(rl[:, m, :], rl[:, m, :], g_, ALU.mult))
                    for i in range(NT):
                        p_ = prob[:, buf, QOFF[i]:QOFF[i] + LEN[i]]
                        ins = dve.tensor_scalar(p_, p_, rl[:, m, i:i + 1], None, ALU.mult)
                    ins.then_inc(p_ready, 1)

                dve.tensor_tensor(slope, slope, sl_r, ALU.mult).then_inc(v_loop, 1)
                n[0] += 1
                lstep(dve.tensor_copy(gcur.rearrange("p h b t -> p h (b t)"), gates[:, :, bass.ds(j * 12, 12)]))
                biased(M_A0, T_FIRST[T_W0] + NT - T_USES)
                biased(M_A1, T_FIRST[T_W0] + NT - T_USES)
                full(at["CMP"])
                for hd in range(2):
                    ins = dve.tensor_tensor(pc[:, hd, :, :], ps[:, bank(at["CMP"]), hd * P:(hd + 1) * P].rearrange(
                        "p (t n) -> p t n", t=NT), dist_c[:, :, :], ALU.add)
                ins.then_inc(bank_free, 1)
                self_read(at["CMP"])
                pc8 = pc[:, :, :, :].rearrange("p h t n -> p (h t) n")
                lstep(dve.tensor_reduce(cmx, pc8, AX, ALU.max))
                lstep(dve.tensor_scalar(cmx, cmx, MAX_FLOOR, None, ALU.max))
                dve.tensor_tensor(pc8, pc8, cmx.unsqueeze(2).to_broadcast([P, 8, NCP]), ALU.subtract).then_inc(cmp_sub, 1)
                biased(M_S0, 0)
                dve.wait_ge(exp_done, j * 6 + 2)
                lstep(dve.tensor_scalar(rl[:, 0:2, :], lsum[:, 0:2, :], SUM_FLOOR, None, ALU.max))
                lstep(dve.reciprocal(rl[:, 0:2, :], rl[:, 0:2, :]))
                lstep(dve.tensor_scalar(rl[:, 1, :], rl[:, 1, :], nlam, None, ALU.mult))
                for i in range(NT):
                    p1 = prob[:, 1, QOFF[i]:QOFF[i] + LEN[i]]
                    ins = dve.tensor_scalar(p1, p1, rl[:, 1, i:i + 1], None, ALU.mult)
                lstep(ins)
                for i in range(NT):
                    p0, p1 = (prob[:, b, QOFF[i]:QOFF[i] + LEN[i]] for b in range(2))
                    ins = dve.scalar_tensor_tensor(p0, p0, rl[:, 0, i:i + 1], p1, ALU.mult, ALU.add)
                ins.then_inc(p_ready, 1)
                if not last:
                    lstep(dve.tensor_tensor(qsc, qsc, qs_r, ALU.mult))
                next_heads("DQ")
                weighted(M_S0, gcur[:, 0, 1, :])
                biased(M_S1, T_FIRST[T_A] + NT)
                dve.wait_ge(d_ada, j * 32 + 32)
                weigh(0, ada_slot, lstep, adacc_ready)
                next_heads("DK")
                biased(M_W0, T_FIRST[T_A] + NT)
                weighted(M_S1, gcur[:, 1, 1, :])
                full(at["SUB"])
                dve.tensor_scalar(sqv, ps[:, bank(at["SUB"]), :], 1.0 / P, EPS, ALU.mult, ALU.add).then_inc(bank_free, 1)
                dve.wait_ge(d_ada, j * 32 + 48)
                weigh(1, ada_slot, lstep, adacc_ready)
                next_heads("DV")
                biased(M_W1, T_FIRST[T_S0] + NT)
                weighted(M_W0, gcur[:, 0, 2, :])
                next_heads("NQ")
                dve.wait_ge(cmp_exp, j + 1)
                lstep(dve.tensor_reduce(cl, pc8, AX, ALU.add))
                lstep(dve.tensor_scalar(cl, cl, SUM_FLOOR, None, ALU.max))
                lstep(dve.reciprocal(cl, cl))
                clv = cl.rearrange("p (h t) -> p h t", h=2)
                lstep(dve.tensor_tensor(clv, clv, gcur[:, :, 0, :], ALU.mult))
                dve.tensor_tensor(pc8, pc8, cl.unsqueeze(2).to_broadcast([P, 8, NCP]), ALU.mult).then_inc(p_ready, 1)
                weighted(M_W1, gcur[:, 1, 2, :])
                dve.wait_ge(subrt_ready, j + 1)
                lstep(dve.reciprocal(sqv, sqv))
                dve.scalar_tensor_tensor(ovf[:, bass.ds(j * SEQ, SEQ)], ps[:, OD, :], gsub, sqv, ALU.mult,
                                         ALU.mult).then_inc(od_free, 1)
                for half, name in enumerate(("ADA0", "ADA1")):
                    full(at[name])
                    dve.tensor_copy(modsf[:, bass.ds(j * D + half * 512, 512)], ps[:, bank(at[name]), :]).then_inc(bank_free, 1)
                assert last or n[0] == V_LOOP, n[0]

            with dve.Fori(0, NJ - 1) as j:
                head_step(j, False)
            head_step(NJ - 1, True)

            dve.wait_ge(d_bc, 16 * 7)
            dve.wait_ge(bank_free, ALL_USES)
            step(dve.tensor_tensor(modsf, modsf, e1[:, 0:4 * D], ALU.add))
            dve.tensor_tensor(mods[:, 0, :], mods[:, 0, :], bc_rows[:, 4, :], ALU.mult).then_inc(mods_ready, 1)
            dve.scalar_tensor_tensor(mods[:, 2, :], mods[:, 2, :], 1.0, bc_rows[:, 5, :], ALU.add, ALU.mult).then_inc(mods_ready, 1)
            dve.tensor_tensor(mods[:, 3, :], mods[:, 3, :], bc_rows[:, 6, :], ALU.mult).then_inc(mods_ready, 2)
            dve.wait_ge(mods_ready, 4)

            mixv = [ps[:, 2 * t:2 * t + 2, :] for t in range(NT)]
            for t in range(NT):
                dve.wait_ge(mixsq, t + 1)
                mean_square(ssq2[:, t:t + 1], D).then_inc(mixms, 1)
                dve.wait_ge(mixrt, t + 1)
                step(dve.reciprocal(rstd2[:, t:t + 1], rstd2[:, t:t + 1]))
                step(dve.scalar_tensor_tensor(tmpx.rearrange("p (a b) -> p a b", a=2), mixv[t], rstd2[:, t:t + 1],
                                              mods[:, 0, :].rearrange("p (a b) -> p a b", a=2), ALU.mult, ALU.mult))
                dve.tensor_tensor(xs[:, t, :], xs[:, t, :], tmpx, ALU.add).then_inc(x1_ready, 1)
                dve.wait_ge(x1sq, t + 1)
                mean_square(ssq2[:, 4 + t:5 + t], D).then_inc(x1ms, 1)
                dve.wait_ge(x1rt, t + 1)
                step(dve.reciprocal(rstd2[:, 4 + t:5 + t], rstd2[:, 4 + t:5 + t]))
                if t >= 2:
                    dve.wait_ge(h2T_full, t - 1)
                    dve.wait_ge(h2_stored[t % 2], 16 * (t // 2))
                if t == 0:
                    dve.wait_ge(mix_full, NT)
                step(dve.scalar_tensor_tensor(h2[t % 2], xs[:, t, :], rstd2[:, 4 + t:5 + t], mods[:, 2, :],
                                              ALU.mult, ALU.mult))
                dve.tensor_tensor(h2[t % 2], h2[t % 2], mods[:, 1, :], ALU.add).then_inc(h2_ready, 1)

            for t in range(NT):
                dve.wait_ge(rout_full, t + 1)
                dve.tensor_tensor(lg[:, t, :], ps[:, 2 * t, 0:NR], bias_r[:, :], ALU.add).then_inc(lg_ready, 1)
            dve.wait_ge(lg_ready, NT)
            dve.wait_ge(k_router, 6)
            b8, b64 = [P, NT, NG], [P, NT, NE]
            mg, kg, v1, v2, kk_ = rt[:, 0, :], rt[:, 1, :], rt[:, 2, :], rt[:, 3, :], rt[:, 5, :]
            e2 = rt[:, 4, :]

            def wide(ap, shape):
                return ap.unsqueeze(2).to_broadcast(shape)

            def first_max(onehot, vals, mval, keyrow, shape):
                step(dve.tensor_tensor(onehot, vals, wide(mval, shape), ALU.is_equal))
                step(dve.tensor_tensor(onehot, onehot, keyrow.unsqueeze(1).to_broadcast(shape), ALU.mult))
                step(dve.tensor_reduce(kk_, onehot, AX, ALU.max))
                step(dve.tensor_tensor(onehot, onehot, wide(kk_, shape), ALU.is_equal))

            step(dve.tensor_reduce(mg, lg[:, :, 0:NG], AX, ALU.max))
            dve.tensor_tensor(eg, lg[:, :, 0:NG], wide(mg, b8), ALU.subtract).then_inc(eg_in, 1)
            first_max(ohg, lg[:, :, 0:NG], mg, key8, b8)
            for t in range(NT):
                le_t = lg[:, t, NG:NR].rearrange("p (g e) -> p g e", g=NG)
                lem_t = lem[:, t, :].rearrange("p (g e) -> p g e", g=NG)
                sel_t = sel[:, t, :].rearrange("p (g e) -> p g e", g=NG)
                oh_t = ohg[:, t, :].unsqueeze(2).to_broadcast([P, NG, NG])
                step(dve.tensor_tensor(lem_t, le_t, oh_t, ALU.mult))
                step(dve.tensor_scalar(sel_t, oh_t, 1.0, -NEG, ALU.subtract, ALU.mult))
                step(dve.tensor_tensor(lem_t, lem_t, sel_t, ALU.add))
            step(dve.tensor_reduce(v1, lem, AX, ALU.max))
            first_max(oh[0], lem, v1, key64, b64)
            step(dve.scalar_tensor_tensor(lem, oh[0], 4.0 * NEG, lem, ALU.mult, ALU.add))
            step(dve.tensor_reduce(v2, lem, AX, ALU.max))
            first_max(oh[1], lem, v2, key64, b64)
            dve.tensor_tensor(msum, oh[0], oh[1], ALU.add).then_inc(m_ready, 1)
            dve.tensor_tensor(e2, v2, v1, ALU.subtract).then_inc(e2_in, 1)
            dve.wait_ge(eg_out, 1)
            step(dve.tensor_reduce(pgrp, eg, AX, ALU.add))
            dve.wait_ge(e2_out, 1)
            step(dve.tensor_scalar(mg, e2, 1.0, None, ALU.add))
            step(dve.tensor_tensor(mg, mg, pgrp, ALU.mult))
            step(dve.reciprocal(wts[:, :, 0], mg))
            step(dve.tensor_tensor(wts[:, :, 1], wts[:, :, 0], e2, ALU.mult))

            dve.wait_ge(rank_full, 1)
            dve.tensor_copy(rank, ps[:, 0, 0:NT * NE].rearrange("p (t e) -> p t e", t=NT)).then_inc(v_step, 1)
            steps[0] += 1
            step(dve.tensor_copy(cnt, ps[:, 1, 0:NE]))
            thr3 = thr[:, 0:NCMPR * NE].rearrange("p (m e) -> p m e", m=NCMPR)
            cmp3 = cmpx[:, 0:NCMPR * NE].rearrange("p (m e) -> p m e", m=NCMPR)
            step(dve.tensor_tensor(cmp3, cnt.unsqueeze(1).to_broadcast([P, NCMPR, NE]), thr3, ALU.is_gt))
            step(dve.tensor_reduce(extra_row, cmp3.rearrange("p m e -> p e m"), AX, ALU.add))
            step(dve.tensor_tensor_scan(cum, ones[:, 0:NE], extra_row, 0.0, ALU.mult, ALU.add))
            oe = cmpx[0:1, 0:(MAX_EXTRA + 1) * NE].rearrange("p (k e) -> p k e", e=NE)
            kr = thr[0:1, 512:512 + MAX_EXTRA + 1]
            step(dve.tensor_tensor(oe, cum[0:1, :].unsqueeze(1).to_broadcast([1, MAX_EXTRA + 1, NE]),
                                   kr.unsqueeze(2).to_broadcast([1, MAX_EXTRA + 1, NE]), ALU.is_le))
            step(dve.tensor_reduce(small[0:1, OVF:OVF + MAX_EXTRA + 1], oe, AX, ALU.add))
            dve.tensor_scalar(over_e[0:1, :], small[0:1, OVF:OVF + MAX_EXTRA + 1], float(NE - 1), None, ALU.min).then_inc(over_ready, 1)
            dve.tensor_copy(n_over[0:1, 0:1], cum[0:1, NE - 1:NE]).then_inc(over_ready, 1)
            step(dve.tensor_tensor(base_e, cum, extra_row, ALU.subtract))
            step(dve.tensor_tensor(base_e, base_e, iota_e, ALU.subtract))
            step(dve.tensor_scalar(base_e, base_e, float(NE - 1), None, ALU.add))
            step(dve.tensor_scalar(rblk, rank, float(CAP), None, ALU.is_ge))
            step(dve.tensor_copy(sel, rblk))
            for m in range(2, NCMPR + 1):
                step(dve.scalar_tensor_tensor(rblk, rank, float(CAP * m), rblk, ALU.is_ge, ALU.add))
            step(dve.scalar_tensor_tensor(rank, rblk, -float(CAP), rank, ALU.mult, ALU.add))
            step(dve.tensor_tensor(rblk, rblk, base_e.unsqueeze(1).to_broadcast(b64), ALU.add))
            step(dve.tensor_tensor(rblk, rblk, sel, ALU.mult))
            step(dve.tensor_tensor(rblk, rblk, iota_e.unsqueeze(1).to_broadcast(b64), ALU.add))
            step(dve.scalar_tensor_tensor(rank, rank, float(NCOL), rblk, ALU.mult, ALU.add))
            for kk in range(2):
                step(dve.tensor_tensor(oh[kk], oh[kk], rank, ALU.mult))
                step(dve.tensor_reduce(addr_f[:, kk * NT:(kk + 1) * NT], oh[kk], AX, ALU.add))
            dve.tensor_copy(addr_i[:, :], addr_f).then_inc(addr_ready, 1)
            dve.wait_ge(lists_loaded, 48)
            step(dve.tensor_scalar(list_tmp, gidx[:, :], float(SEQ), float(SEQ), ALU.is_ge, ALU.mult))
            dve.tensor_tensor(gidx[:, :], gidx[:, :], list_tmp, ALU.subtract).then_inc(idx_ready, 1)
            dve.tensor_scalar(sidx[0:CAP, :], sidx[0:CAP, :], 2.0, None, ALU.mult).then_inc(idx_ready, 1)
            dve.tensor_scalar(sidx[CAP:P, :], sidx[CAP:P, :], 2.0, 1.0, ALU.mult, ALU.add).then_inc(idx_ready, 1)

            with dve.Fori(0, NE // 2) as g:
                for b in range(2):
                    dve.wait_ge(sg_ready, g * 2 + (b + 1))
                    dve.tensor_tensor(hid[b], sg[b], ps[:, 2 + b, 256:512], ALU.mult).then_inc(hid_ready, 1)
                    dve.wait_ge(hT_full, g * 2 + (b + 1))
                    dve.tensor_copy(hidT[b], ps[:, 4 + b, 0:256]).then_inc(hidT_ready, 1)
            dve.wait_ge(over_ready, 2)
            n_blocks = dve.value_load(n_over[0:1, 0:1], min_val=0, max_val=MAX_EXTRA)
            with dve.Fori(0, MAX_EXTRA) as k:
                with dve.If(k < n_blocks):
                    dve.wait_ge(o_sg, k + 1)
                    dve.tensor_tensor(hid[0], sg[0], ps[:, 2, 256:512], ALU.mult).then_inc(o_hid, 1)
                    dve.wait_ge(o_hT, k + 1)
                    dve.tensor_copy(hidT[0], ps[:, 4, 0:256]).then_inc(o_hTr, 1)

            for t in range(NT):
                y0, y1 = ytok[t % 2][:, 0:D], ytok[t % 2][:, D:2 * D]
                dve.wait_ge(y_back[t % 2], 32 * (t // 2 + 1))
                step(dve.tensor_scalar(y0, y0, wts[:, t, 0:1], None, ALU.mult))
                dve.scalar_tensor_tensor(y0, y1, wts[:, t, 1:2], y0, ALU.mult, ALU.add).then_inc(f_ready, 1)
                dve.wait_ge(fsq, t + 1)
                mean_square(ssq3[:, t:t + 1], D).then_inc(fms, 1)
                dve.wait_ge(frt, t + 1)
                step(dve.reciprocal(rstd3[:, t:t + 1], rstd3[:, t:t + 1]))
                step(dve.scalar_tensor_tensor(y1, y0, rstd3[:, t:t + 1], mods[:, 3, :], ALU.mult, ALU.mult))
                dve.tensor_tensor(xs[:, t, :], xs[:, t, :], y1, ALU.add).then_inc(o_ready, 1)


_INS = ['x', 'c', 'w_ada', 'b_ada', 'g_pre_mix', 'g_post_mix', 'g_pre_ffn', 'g_post_ffn', 'w_in',
        'lam_q1', 'lam_k1', 'lam_q2', 'lam_k2', 'g_subln', 'cmp_pos_k', 'cmp_pos_v', 'cmp_w1_k', 'cmp_w1_v',
        'cmp_w2_k', 'cmp_w2_v', 'w_out', 'w_router_grp', 'b_router_grp', 'w_router_exp', 'b_router_exp',
        'w_exp_gate', 'w_exp_up', 'w_exp_down']


def kernel(**inputs):
    import numpy as _np
    import concourse.bacc as _bacc
    from concourse import mybir as _mybir
    from concourse.bass_utils import run_bass_kernel_spmd as _run

    nc = _bacc.Bacc("TRN2", target_bir_lowering=False, num_devices=1)
    arrays, args = {}, []
    for name in _INS:
        a = _np.ascontiguousarray(inputs[name])
        arrays[f"in_{name}_dram"] = a
        args.append(nc.dram_tensor(f"in_{name}_dram", a.shape, _mybir.dt.from_np(a.dtype), kind="ExternalInput").ap())
    args.append(nc.dram_tensor("out_dram", (1, SEQ, D), F32, kind="ExternalOutput").ap())
    build(nc, *args)
    r = _run(nc, [arrays], core_ids=[0])
    return r.results[0]["out_dram"]
```

```python
from contextlib import ExitStack

import concourse.bass as bass
from concourse import mybir

F32 = mybir.dt.float32
I32 = mybir.dt.int32
ALU = mybir.AluOpType
ACT = mybir.ActivationFunctionType
AX = mybir.AxisListType.X

P = 128
D = 1024
SEQ = 512
DC = D // P
NT = SEQ // P
HD = 64
NJ = 4
NSA_HEADS = 8
NCMP = 31
NCP = 32
CMP_BLOCK = 32
CMP_STRIDE = 16
NEG = -1e30
MAX_FLOOR = -1e20
SUM_FLOOR = 1e-30
EPS = 1e-6
LAMBDA_INIT = 0.8 - 0.6
SCALE = HD ** -0.5
NG = 8
NE = 64
NR = NG + NE
F = 512
CAP = 64
MAX_EXTRA = 2 * SEQ // (CAP + 1)
NCOL = NE + MAX_EXTRA + 1
NCMPR = SEQ // CAP - 1
NO_ROW = 1 << 14

C_DQ, C_DK, C_DV, C_NQ, C_KV = 0, 512, 1024, 1536, 2048
N_KV = 792
LEN = [P * (i + 1) for i in range(NT)]
QOFF = [P * i * (i + 1) // 2 for i in range(NT)]
TLEN = [SEQ - P * k for k in range(NT)]
TOFF = [sum(TLEN[:k]) for k in range(NT)]
NS = sum(LEN)

STEP_USES = (("A0", NT), ("A1", NT), ("CMP", 1), ("S0", NT), ("DQ", 1), ("S1", NT), ("DK", 1), ("W0", NT),
             ("SUB", 1), ("DV", 1), ("W1", NT), ("NQ", 1), ("ADA0", 1), ("ADA1", 1))


def first_uses(last):
    at, u = {}, 0
    for name, uses in STEP_USES:
        if not (last and name in ("DQ", "DK", "DV", "NQ")):
            at[name] = u
            u += uses
    return at, u


USE, USES = first_uses(False)
LAST_USE, LAST_USES = first_uses(True)
PRE_USES = 20
ALL_USES = PRE_USES + (NJ - 1) * USES + LAST_USES
PRE_PROJ = 14
NBANK = 4
PRE_T = 10
T_USES = 22
N_SMALL = 13
N_CONST = 14
V_LOOP = 40
AHEAD = 1
OVF = 400


def build(nc, x, c, w_ada, b_ada, g_pre_mix, g_post_mix, g_pre_ffn, g_post_ffn, w_in,
          lam_q1, lam_k1, lam_q2, lam_k2, g_subln, cmp_pos_k, cmp_pos_v, cmp_w1_k, cmp_w1_v,
          cmp_w2_k, cmp_w2_v, w_out, w_router_grp, b_router_grp, w_router_exp, b_router_exp,
          w_exp_gate, w_exp_up, w_exp_down, out):
    with ExitStack() as ctx:
        def sb(name, shape, dt=F32):
            return ctx.enter_context(nc.sbuf_tensor(name, shape, dt))

        def sem(name):
            return ctx.enter_context(nc.semaphore(name))

        exp_w = sb("exp_w", [P, 2, 3 * 4096])
        stream = sb("stream", [P, 2, 4096])
        ov = sb("ov", [P, 8, SEQ])
        mods = sb("mods", [P, NJ, D])
        modsf = mods[:, :, :].rearrange("p a b -> p (a b)")
        xs = sb("xs", [P, NT, D])
        qdn = sb("qdn", [P, 4, SEQ])
        qd = qdn[:, 0:2, :]
        qn = qdn[:, 2:4, :]
        kd = sb("kd", [P, SEQ])
        vd = sb("vd", [P, NT, P])
        ident = sb("ident", [P, P])
        ones = sb("ones", [P, P])
        dist = sb("dist", [P, SEQ])
        dist_c = sb("dist_c", [P, NT, NCP])
        kcp = sb("kcp", [P, NCP])
        vcp = sb("vcp", [P, 2, HD])
        pc = sb("pc", [P, 2, NT, NCP])
        gates = sb("gates", [P, 2, NJ * 3 * NT])
        ada_acc = sb("ada_acc", [P, 2, 512])
        small = sb("small", [P, 512])
        bias_r = sb("bias_r", [P, NR])
        w_r = sb("w_r", [P, DC, NR])

        e1 = exp_w[:, 1, :]
        hT = e1[:, 0:4096].rearrange("p (c t) -> p c t", c=DC)
        prob = e1[:, 4096:4096 + 3 * NS].rearrange("p (b n) -> p b n", b=3)
        probT = e1[:, 7936:7936 + 2 * NS].rearrange("p (b n) -> p b n", b=2)
        vsw = e1[:, 10496:10496 + 2 * SEQ].rearrange("p (w t n) -> p w t n", w=2, t=NT)
        cmp_w1 = e1[:, 4096:8192].rearrange("p (w b n) -> p w b n", w=2, b=16)
        ckp = e1[:, 8192:9728].rearrange("p (w h n) -> p w h n", w=2, h=3)
        cmp_h = e1[:, 9728:9856].rearrange("p (w n) -> p w n", w=2)
        cmp_g = e1[:, 9856:9984].rearrange("p (w n) -> p w n", w=2)
        cmp_w2 = e1[:, 9984:10112].rearrange("p (w n) -> p w n", w=2)
        pos_in = e1[0:16, 10112:10368].rearrange("p (w n) -> p w n", w=2)
        lam_in = e1[:, 10368:10624].rearrange("p (w n) -> p w n", w=4)
        lam_junk = e1[:, 10624:10752].rearrange("p (w n) -> p w n", w=2)
        sqv = e1[:, 11520:11520 + SEQ]
        bc_rows = e1[:, 0:7 * D].rearrange("p (r n) -> p r n", r=7)
        w_kv = exp_w[:, 0, 4096:4096 + DC * N_KV].rearrange("p (c n) -> p c n", c=DC)
        ada_early = [exp_w[:, 0, 0:4096], stream[:, 0, :], stream[:, 1, :],
                     mods[:, :, :].rearrange("p a b -> p (a b)")]
        kslc = sb("kslc", [P, SEQ])
        kwin = sb("kwin", [P, SEQ])

        w_slot = stream[:, 0, :].rearrange("p (c n) -> p c n", c=DC)
        ada_slot = stream[:, 1, :].rearrange("p (c n) -> p c n", c=DC)
        wo = stream[:, :, :].rearrange("p a (c n) -> p (a c) n", c=4)

        cs = small[:, 0:8]
        craw = small[:, 8:16]
        cexp = small[:, 16:24]
        shc = small[:, 24:32]
        scc = small[:, 32:40]
        gpc = small[:, 40:48]
        bsh = small[:, 48:56]
        bsc = small[:, 56:64]
        ssq = small[:, 64:68]
        rstd = small[:, 68:72]
        slope = small[:, 72:75]
        qsc = small[:, 75:78]
        sl_r = small[:, 78:81]
        qs_r = small[:, 81:84]
        mx = small[:, 84:108].rearrange("p (m t) -> p m t", m=6)
        nmx = small[:, 108:132].rearrange("p (m t) -> p m t", m=6)
        lsum = small[:, 132:156].rearrange("p (m t) -> p m t", m=6)
        rl = small[:, 156:180].rearrange("p (m t) -> p m t", m=6)
        gcur = small[:, 180:204].rearrange("p (h b t) -> p h b t", h=2, b=3)
        cmx = small[:, 204:212]
        cl = small[:, 212:220]
        lam2 = small[:, 220:222]
        lame = small[:, 222:224]
        nlam = small[:, 224:225]
        gsub = small[:, 225:226]
        gsub2 = small[:, 227:228]
        lamd = small[:, 228:229]
        ssq2 = small[:, 232:240]
        rstd2 = small[:, 240:248]
        wts = small[:, 248:256].rearrange("p (t k) -> p t k", k=2)
        pgrp = small[:, 256:260]
        rt = small[:, 260:292].rearrange("p (a t) -> p a t", t=NT)
        extra_row = small[:, 296:360]
        ssq3 = small[:, 360:364]
        rstd3 = small[:, 364:368]
        key8 = small[:, 368:376]
        addr_f = small[:, 376:384]
        addr_i = sb("addr_i", [P, 8], I32)
        val_i = sb("val_i", [P, 8], I32)
        n_over = sb("n_over", [1, 1], I32)
        over_e = sb("over_e", [1, MAX_EXTRA + 1], I32)
        sidx = sb("sidx", [P, NCOL], I32)
        scol = sb("scol", [P, 2], I32)

        ovf = ov[:, :, :].rearrange("p a b -> p (a b)")
        hbuf = qdn[:, :, :].rearrange("p a b -> p (a b)")[:, 0:1536].rearrange("p (b n) -> p b n", b=2)
        sg = [hbuf[:, b, 0:256] for b in range(2)]
        hid = [hbuf[:, b, 256:512] for b in range(2)]
        hidT = [hbuf[:, b, 512:768] for b in range(2)]
        h2 = [ov[:, :, t * P:(t + 1) * P].rearrange("p c q -> p q c") for t in range(NT)]

        def h2_chunk(t, c_):
            return ov[:, c_, t * P:(t + 1) * P]

        streamf = stream[:, :, :].rearrange("p a b -> p (a b)")
        h2T = [e1[:, (8 + b) * D:(9 + b) * D].rearrange("p (c t) -> p c t", c=DC) for b in range(2)]
        xT = [streamf[:, b * 512:(b + 1) * 512] for b in range(2)]
        yb = [streamf[:, 1024 + b * 512:1536 + b * 512] for b in range(2)]
        sel2 = streamf[:, 2048:2560].rearrange("p (k t n) -> p k t n", k=2, t=NT)
        xg = streamf[:, 3072:3584]
        sel1 = [streamf[:, 2560 + b * 256:2816 + b * 256].rearrange("p (t n) -> p t n", t=NT) for b in range(2)]
        tmpx = ada_acc[:, :, :].rearrange("p a b -> p (a b)")
        sqj = qdn[:, 0:2, :]
        fsqj = tmpx
        ytok = [streamf[:, t * 2 * D:(t + 1) * 2 * D] for t in range(NT)]
        lg = qd[:, 0, 0:NT * NR].rearrange("p (t n) -> p t n", t=NT)
        le = qd[:, 1, 0:256].rearrange("p (t e) -> p t e", t=NT)
        eqg = qn[:, 0, 0:32].rearrange("p (t e) -> p t e", t=NT)
        ohg = qn[:, 0, 32:64].rearrange("p (t e) -> p t e", t=NT)
        eg = qn[:, 0, 64:96].rearrange("p (t e) -> p t e", t=NT)
        oh = [qn[:, 1, 0:256].rearrange("p (t e) -> p t e", t=NT),
              qn[:, 1, 256:512].rearrange("p (t e) -> p t e", t=NT)]
        lem = kd[:, 0:256].rearrange("p (t e) -> p t e", t=NT)
        key = kd[:, 256:512].rearrange("p (t e) -> p t e", t=NT)
        sel = vd[:, :, :].rearrange("p t n -> p (t n)")[:, 0:256].rearrange("p (t e) -> p t e", t=NT)
        msum = vd[:, :, :].rearrange("p t n -> p (t n)")[:, 256:512].rearrange("p (t e) -> p t e", t=NT)
        rank = kslc[:, 0:256].rearrange("p (t e) -> p t e", t=NT)
        csum = kslc[:, 256:512].rearrange("p (t e) -> p t e", t=NT)
        cum = kwin[:, 64:128]
        iota_e = kwin[:, 128:192]
        key64 = kwin[:, 192:256]
        base_e = kwin[:, 256:320]
        slot_addr = kwin[:, 320:320 + CAP]
        rank8, base8, blk8 = kwin[:, 384:392], kwin[:, 392:400], kwin[:, 400:408]
        e8 = kwin[:, 408:416].rearrange("p (k t) -> p k t", k=2)
        over8 = kwin[:, 416:416 + 8 * NCMPR].rearrange("p (c m) -> p c m", m=NCMPR)
        oh2 = qn[:, 1, 0:512].rearrange("p (k t e) -> p k t e", k=2, t=NT)
        pick = streamf[:, 5 * D:5 * D + 512].rearrange("p (k t e) -> p k t e", k=2, t=NT)
        cmpx = streamf[:, 6 * D:7 * D]
        thr = streamf[:, 7 * D:8 * D]
        tri = dist[:, 0:P]

        ps = ctx.enter_context(nc.psum_tensor("ps", [P, 8, 512], F32))
        SB, TB, OD, ON = 0, 4, 6, 7

        y_d = nc.dram_tensor("y_d", (2 * 2 * SEQ, D // 2), F32, kind="Internal").ap()
        list_d = nc.dram_tensor("list_d", (CAP * NCOL, 1), I32, kind="Internal").ap()

        d_x, d_c, d_small, d_kv, d_w1 = sem("d_x"), sem("d_c"), sem("d_small"), sem("d_kv"), sem("d_w1")
        d_ada0, d_ada3, d_win, d_ada = sem("d_ada0"), sem("d_ada3"), sem("d_win"), sem("d_ada")
        d_cols, d_wo, d_bc = sem("d_cols"), sem("d_wo"), sem("d_bc")
        d_gu = [sem("d_gu0"), sem("d_gu1")]
        d_wd = [sem("d_wd0"), sem("d_wd1")]
        k_ident, k_zero, k_const, k_router = sem("k_ident"), sem("k_zero"), sem("k_const"), sem("k_router")
        v_step, v_loop, p_step = sem("v_step"), sem("v_loop"), sem("p_step")
        cexp_ready, acc_ready = sem("cexp_ready"), sem("acc_ready")
        ssq_ready, ms_ready, rt_ready, rstd_ready, xn_ready = (
            sem("ssq_ready"), sem("ms_ready"), sem("rt_ready"), sem("rstd_ready"), sem("xn_ready"))
        cols_ready, gelu_ready, lam_ready, lame_ready, gexp_ready, loop_vars = (
            sem("cols_ready"), sem("gelu_ready"), sem("lam_ready"), sem("lame_ready"), sem("gexp_ready"),
            sem("loop_vars"))
        bank_full, bank_free = sem("bank_full"), sem("bank_free")
        tbank_full, tbank_free = sem("tbank_full"), sem("tbank_free")
        adacc_ready, neg_ready, exp_done, p_ready, values_done = (
            sem("adacc_ready"), sem("neg_ready"), sem("exp_done"), sem("p_ready"), sem("values_done"))
        cmp_sub, cmp_exp, sq_ready, subrt_ready, od_free, on_free = (
            sem("cmp_sub"), sem("cmp_exp"), sem("sq_ready"), sem("subrt_ready"), sem("od_free"), sem("on_free"))
        mods_ready, mix_full, mixsq, mixms, mixrt, x1_ready = (
            sem("mods_ready"), sem("mix_full"), sem("mixsq"), sem("mixms"), sem("mixrt"), sem("x1_ready"))
        x1sq, x1ms, x1rt, h2_ready, h2T_full, h2T_ready, rout_full, lg_ready = (
            sem("x1sq"), sem("x1ms"), sem("x1rt"), sem("h2_ready"), sem("h2T_full"),
            sem("h2T_ready"), sem("rout_full"), sem("lg_ready"))
        eg_in, eg_out, e2_in, e2_out, m_ready, rank_full = (
            sem("eg_in"), sem("eg_out"), sem("e2_in"), sem("e2_out"), sem("m_ready"), sem("rank_full"))
        lists_empty, lists_zeroed, lists_stored, lists_loaded, addr_ready, idx_ready, over_ready = (
            sem("lists_empty"), sem("lists_zeroed"), sem("lists_stored"), sem("lists_loaded"),
            sem("addr_ready"), sem("idx_ready"), sem("over_ready"))
        sel_ready, v_moe = sem("sel_ready"), sem("v_moe")
        y_out = [sem("y_out0"), sem("y_out1")]
        idx_cp, xg_full, xg_ready, xT_full, xT_ready, gu_done, sg_ready, hid_ready, hT_full, hidT_ready, d_done, y_ready = (
            sem("idx_cp"), sem("xg_full"), sem("xg_ready"), sem("xT_full"), sem("xT_ready"), sem("gu_done"),
            sem("sg_ready"), sem("hid_ready"), sem("hT_full"), sem("hidT_ready"), sem("d_done"), sem("y_ready"))
        scores_seen, copy_seen = sem("scores_seen"), sem("copy_seen")
        y_back = [sem(f"y_back{t}") for t in range(NT)]
        f_scaled = sem("f_scaled")
        y0_ready, f_ready, fsq, fms, frt, o_ready, stored = (
            sem("y0_ready"), sem("f_ready"), sem("fsq"), sem("fms"), sem("frt"), sem("o_ready"), sem("stored"))

        wg_v = w_exp_gate.rearrange("l e (p c) n -> (l e) p (c n)", p=P)
        wu_v = w_exp_up.rearrange("l e (p c) n -> (l e) p (c n)", p=P)
        wd_v = w_exp_down.rearrange("l e (h p j) n -> (l e h) p (j n)", h=2, p=P)
        gu_w = [exp_w[:, b, 0:8192].rearrange("p (g c n) -> p g c n", g=2, c=DC) for b in range(2)]
        dn_w = [exp_w[:, b, 8192:12288].rearrange("p (h j n) -> p h j n", h=2, j=2) for b in range(2)]
        w_in_v = w_in[0].rearrange("(p c) n -> p c n", p=P)
        w_ada_v = w_ada[0].rearrange("(p c) n -> p c n", p=P)

        def xn(t):
            return ovf[:, t * D:(t + 1) * D]

        def one(ap):
            return ap.rearrange("a p n -> (a p) n")

        def load_gu(eng, e, b, signal):
            eng.dma_start(exp_w[:, b, 0:4096], one(wg_v[bass.ds(e, 1)])).then_inc(signal, 16)
            eng.dma_start(exp_w[:, b, 4096:8192], one(wu_v[bass.ds(e, 1)])).then_inc(signal, 16)

        def load_wd(eng, e, b, signal):
            for half in range(2):
                eng.dma_start(exp_w[:, b, 8192 + half * 2048:10240 + half * 2048],
                              one(wd_v[bass.ds(e * 2 + half, 1)])).then_inc(signal, 16)

        def load_win(eng, j):
            for i, o in enumerate((C_DQ, C_DK, C_DV)):
                eng.dma_start(w_slot[:, :, i * P:(i + 1) * P], w_in_v[:, :, bass.ds(j * P + o, P)]).then_inc(d_win, 16)
            for hd in range(2):
                eng.dma_start(w_slot[:, :, 384 + hd * HD:448 + hd * HD],
                              w_in_v[:, :, bass.ds(j * HD + (C_NQ + hd * 256), HD)]).then_inc(d_win, 16)

        def bank_wait(eng, j, u):
            eng.wait_ge(bank_free, j * USES + (PRE_USES + u - NBANK + 1))

        MAPS = [(0, "A0", 0), (0, "A1", 1), (1, "S0", 2), (2, "S1", 0), (1, "W0", 1), (2, "W1", 2)]
        M_A0, M_A1, M_S0, M_S1, M_W0, M_W1 = range(6)
        T_A, T_S0, T_S1, T_W0, T_C, T_W1 = range(6)
        T_FIRST = [0, 4, 8, 12, 16, 18]
        PRE_V = 2

        block = ctx.enter_context(nc.Block())

        @block.sync
        def _(sp):
            sp.dma_start(craw, c.rearrange("a (p n) -> (a p) n", p=P)).then_inc(d_c, 16)
            for i, s in enumerate((d_ada0, d_win, d_ada, d_ada3)):
                if i == 1:
                    sp.dma_start(xs[:, :, :], x[0].rearrange("(t p) n -> p t n", p=P)).then_inc(d_x, 16)
                sp.dma_start(ada_early[i].rearrange("p (c n) -> p c n", c=DC),
                             w_ada_v[:, :, i * 512:(i + 1) * 512]).then_inc(s, 16)
            sp.dma_start(w_kv, w_in_v[:, :, C_KV:C_KV + N_KV]).then_inc(d_kv, 16)
            for i, w in enumerate((cmp_w1_k, cmp_w1_v)):
                sp.dma_start(cmp_w1[:, i], w[0].rearrange("(b p) n -> p b n", p=P)).then_inc(d_w1, 16)
            sp.wait_ge(acc_ready, 2)
            load_win(sp, 0)
            sp.wait_ge(acc_ready, 3)

            def load_ada(j, half):
                sp.wait_ge(adacc_ready, j * 2 + (half + AHEAD))
                sp.dma_start(ada_slot, w_ada_v[:, :, bass.ds(j * D + (2 * D + half * 512), 512)]).then_inc(d_ada, 16)

            load_ada(0, 0)
            sp.wait_ge(bank_full, PRE_PROJ + 4)
            load_win(sp, 1)
            with sp.Fori(0, NJ - 2) as j:
                load_ada(j, 1)
                load_ada(j + 1, 0)
                sp.wait_ge(bank_full, j * USES + (PRE_USES + USE["NQ"] + 1))
                load_win(sp, j + 2)
            load_ada(NJ - 2, 1)
            load_ada(NJ - 1, 0)
            sp.wait_ge(bank_full, (NJ - 2) * USES + PRE_USES + USE["NQ"] + 1)
            sp.dma_start(wo[:, 0:4, :], w_out[0, 0:512, :].rearrange("(c p) n -> p c n", p=P)).then_inc(d_wo, 16)
            load_ada(NJ - 1, 1)
            sp.wait_ge(adacc_ready, 2 * NJ + AHEAD)
            for hd in range(2):
                sp.dma_start(wo[hd * HD:(hd + 1) * HD, 4:8, :],
                             w_out[0, 512 + hd * 256:768 + hd * 256, :].rearrange("(c p) n -> p c n", p=HD)).then_inc(d_wo, 16)
            sp.wait_ge(on_free, NJ + AHEAD)
            sp.wait_ge(od_free, NJ + AHEAD)
            for i, v in enumerate((b_ada[0:1, 2 * D:3 * D], b_ada[0:1, 3 * D:4 * D], b_ada[0:1, 4 * D:5 * D],
                                   b_ada[0:1, 5 * D:6 * D], g_post_mix, g_pre_ffn, g_post_ffn)):
                sp.dma_start(bc_rows[:, i, :], v.to_broadcast([P, D])).then_inc(d_bc, 16)
            sp.wait_ge(mods_ready, 4)
            load_gu(sp, 1, 1, d_gu[1])
            sp.wait_ge(rout_full, NT)
            load_wd(sp, 1, 1, d_wd[1])

            sp.wait_ge(lists_stored, 2 * NT * 16)
            lv = list_d.rearrange("(s n) a -> s (n a)", n=NCOL)
            sp.dma_start(sidx[0:CAP, :], lv).then_inc(lists_loaded, 16)
            sp.dma_start(sidx[CAP:P, :], lv).then_inc(lists_loaded, 16)

            with sp.Fori(1, NE // 2) as g:
                for b in range(2):
                    sp.wait_ge(gu_done, g * 2 + (b - 1))
                    load_gu(sp, g * 2 + b, b, d_gu[b])
                    sp.wait_ge(d_done, g * 2 + (b - 1))
                    load_wd(sp, g * 2 + b, b, d_wd[b])
            sp.wait_ge(over_ready, 2)
            n_blocks = sp.value_load(n_over[0:1, 0:1], min_val=0, max_val=MAX_EXTRA)

            def load_again(k, used):
                sp.wait_ge(over_ready, 2)
                e = sp.value_load(over_e[0:1, bass.ds(k, 1)], min_val=0, max_val=NE - 1)
                sp.wait_ge(gu_done, used)
                load_gu(sp, e, 0, d_gu[0])
                sp.wait_ge(d_done, used)
                load_wd(sp, e, 0, d_wd[0])

            with sp.If(n_blocks > 0):
                load_again(0, NE - 1)
            with sp.Fori(1, MAX_EXTRA) as k:
                with sp.If(k < n_blocks):
                    load_again(k, k + NE)
            sp.wait_ge(y_out[1], 16 * (NE // 2))
            sp.wait_ge(y_out[0], n_blocks * 16 + 16 * (NE // 2))
            for t in range(NT):
                for kk in range(2):
                    r0 = 2 * (kk * SEQ + t * P)
                    sp.dma_start(ytok[t][:, kk * D:(kk + 1) * D],
                                 y_d[r0:r0 + 2 * P, :].rearrange("(p h) n -> p (h n)", h=2)).then_inc(y_back[t], 16)
            for t in range(NT):
                sp.wait_ge(o_ready, t + 1)
                sp.dma_start(out[0, t * P:(t + 1) * P, :], xs[:, t, :]).then_inc(stored, 16)
            sp.wait_ge(stored, 16 * NT)

        @block.gpsimd
        def _(pool):
            steps = [0]

            def step(ins):
                steps[0] += 1
                ins.then_inc(p_step, 1)
                pool.wait_ge(p_step, steps[0])

            small_loads = [(gsub, g_subln.rearrange("a p -> p a")),
                           (pos_in[:, 0, :], cmp_pos_k[0].rearrange("(b r) d -> b (r d)", r=2)),
                           (pos_in[:, 1, :], cmp_pos_v[0].rearrange("(b r) d -> b (r d)", r=2)),
                           (cmp_w2[:, 0, :], cmp_w2_k[0]), (cmp_w2[:, 1, :], cmp_w2_v[0])]
            small_loads += [(lam_in[:, i, :], v.to_broadcast([P, HD])) for i, v in enumerate((lam_q1, lam_k1, lam_q2, lam_k2))]
            small_loads += [(w_r[:, :, 0:NG], w_router_grp[0].rearrange("(p n) g -> p n g", p=P)),
                            (w_r[:, :, NG:NR], w_router_exp[0].rearrange("(p n) g -> p n g", p=P)),
                            (bias_r[:, 0:NG], b_router_grp.to_broadcast([P, NG])),
                            (bias_r[:, NG:NR], b_router_exp.to_broadcast([P, NE]))]
            assert len(small_loads) == N_SMALL
            step(pool.memset(ident[:, :], 0.0))
            pool.affine_select(out=ident[:, :], in_=ident[:, :], compare_op=ALU.not_equal, fill=1.0, base=0,
                               pattern=[[-1, P]], channel_multiplier=1).then_inc(k_ident, 1)
            pool.memset(ones[:, :], 1.0).then_inc(k_ident, 1)
            pool.memset(qdn[:, :, :], 0.0).then_inc(k_zero, 1)
            pool.memset(kcp[:, :], 0.0).then_inc(k_zero, 1)
            pool.memset(vcp[:, :, :], 0.0).then_inc(k_zero, 1)
            pool.memset(ckp[:, :, 2, :], 0.0).then_inc(k_zero, 1)
            for tile_, vals in ((slope, (1.0, 1.0, 2.0 ** -4)), (sl_r, (0.25, 0.5, 0.5)),
                                (qsc, (SCALE, SCALE, SCALE * 16)), (qs_r, (4.0, 2.0, 2.0))):
                for i, v in enumerate(vals):
                    pool.memset(tile_[:, i:i + 1], v).then_inc(k_const, 1)
            step(pool.iota(dist[:, :], pattern=[[1, SEQ]], base=-(SEQ - P), channel_multiplier=-1,
                           allow_small_or_imprecise_dtypes=True))
            pool.affine_select(out=dist[:, :], in_=dist[:, :], compare_op=ALU.is_ge, fill=NEG, base=SEQ - P,
                               pattern=[[-1, SEQ]], channel_multiplier=1).then_inc(k_const, 1)
            step(pool.iota(dist_c[:, :, :], pattern=[[-P, NT], [CMP_STRIDE, NCP]], base=CMP_BLOCK - 1,
                           channel_multiplier=-1, allow_small_or_imprecise_dtypes=True))
            pool.affine_select(out=dist_c[:, :, :], in_=dist_c[:, :, :], compare_op=ALU.is_ge, fill=NEG,
                               base=-(CMP_BLOCK - 1), pattern=[[P, NT], [-CMP_STRIDE, NCP]],
                               channel_multiplier=1).then_inc(k_const, 1)
            for dst, src in small_loads:
                pool.dma_start(dst, src).then_inc(d_small, 16)
            pool.iota(val_i[:, :], pattern=[[SEQ, 2], [P, NT]], base=0, channel_multiplier=1).then_inc(p_step, 1)
            steps[0] += 1
            pool.memset(sidx[0:CAP, :], NO_ROW).then_inc(lists_empty, 1)
            pool.wait_ge(lists_empty, 1)
            pool.dma_start(list_d.rearrange("(s n) a -> s (n a)", n=NCOL), sidx[0:CAP, :]).then_inc(lists_zeroed, 16)

            pool.wait_ge(on_free, NJ + AHEAD)
            pool.wait_ge(od_free, NJ + AHEAD)
            step(pool.memset(tri, 1.0))
            pool.affine_select(out=tri, in_=tri, compare_op=ALU.is_gt, fill=0.0, base=0,
                               pattern=[[1, P]], channel_multiplier=-1).then_inc(k_router, 1)
            pool.iota(iota_e, pattern=[[1, NE]], base=0, channel_multiplier=0,
                      allow_small_or_imprecise_dtypes=True).then_inc(k_router, 1)
            pool.iota(key64, pattern=[[-1, NE]], base=NE, channel_multiplier=0,
                      allow_small_or_imprecise_dtypes=True).then_inc(k_router, 1)
            pool.iota(key8, pattern=[[-1, NG]], base=NG, channel_multiplier=0,
                      allow_small_or_imprecise_dtypes=True).then_inc(k_router, 1)
            pool.wait_ge(mix_full, NT)
            pool.iota(thr[:, 0:NCMPR * NE], pattern=[[CAP, NCMPR], [0, NE]], base=CAP, channel_multiplier=0,
                      allow_small_or_imprecise_dtypes=True).then_inc(k_router, 1)
            pool.iota(thr[:, 512:512 + MAX_EXTRA + 1], pattern=[[1, MAX_EXTRA + 1]], base=0, channel_multiplier=0,
                      allow_small_or_imprecise_dtypes=True).then_inc(k_router, 1)
            pool.iota(slot_addr, pattern=[[NCOL, CAP]], base=0, channel_multiplier=0,
                      allow_small_or_imprecise_dtypes=True).then_inc(k_router, 1)

            pool.wait_ge(addr_ready, 1)
            pool.wait_ge(lists_zeroed, 16)
            for i in range(2 * NT):
                pool.indirect_dma_start(list_d, bass.IndirectOffsetOnAxis(addr_i[:, i:i + 1], 0), val_i[:, i:i + 1], None,
                                        bounds_check=CAP * NCOL - 1, oob_is_err=False).then_inc(lists_stored, 16)

            scatter_max = pool.to_reg(4 * SEQ - 1)

            def scatter_rows(column, b, copied, copies, full):
                pool.tensor_copy(scol[:, b:b + 1], sidx[:, column]).then_inc(copied, 1)
                pool.wait_ge(copied, copies)
                pool.sem_inc(copy_seen, 1)
                pool.indirect_dma_start(y_d, bass.IndirectOffsetOnAxis(scol[:, b:b + 1], 0), yb[b], None,
                                        bounds_check=scatter_max, oob_is_err=False).then_inc(full, 16)

            pool.wait_ge(idx_ready, 2)
            for b in range(2):
                pool.wait_ge(y_ready, b + 1)
                scatter_rows(slice(b, b + 1), b, idx_cp, b + 1, y_out[b])
            with pool.Fori(1, NE // 2) as g:
                for b in range(2):
                    pool.wait_ge(y_ready, g * 2 + (b + 1))
                    pool.wait_ge(y_out[b], g * 16)
                    scatter_rows(bass.ds(g * 2 + b, 1), b, idx_cp, g * 2 + (b + 1), y_out[b])

            for b in range(2):
                pool.wait_ge(y_out[b], 16 * (NE // 2))
            pool.wait_ge(over_ready, 2)
            n_blocks = pool.value_load(n_over[0:1, 0:1], min_val=0, max_val=MAX_EXTRA)
            with pool.Fori(0, MAX_EXTRA) as k:
                with pool.If(k < n_blocks):
                    pool.wait_ge(y_ready, k + (NE + 1))
                    pool.wait_ge(y_out[0], k * 16 + 16 * (NE // 2))
                    scatter_rows(bass.ds(k + NE, 1), 0, idx_cp, k + (NE + 1), y_out[0])
                    pool.wait_ge(over_ready, 2)

            for t in range(NT):
                pool.wait_ge(f_scaled, t + 1)
                pool.tensor_tensor(xs[:, t, :], xs[:, t, :], ytok[t][:, D:2 * D], ALU.add).then_inc(o_ready, 1)

        @block.tensor
        def _(pe):

            def mm(out_, lhsT, rhs, start=True, stop=True):
                return pe.matmul(out_, lhsT, rhs, start=start, stop=stop, skip_group_check=True)

            lo, hi = slice(0, HD), slice(HD, P)
            pe.wait_ge(k_ident, 2)
            for i in range(4):
                pe.wait_ge(acc_ready, i + 1)
                for c_ in range(DC):
                    ins = mm(ps[i % 2 * HD:(i % 2 + 1) * HD, SB + i // 2, c_:c_ + 1], ada_acc[:, i % 2, c_::DC], ones[:, 0:1])
                ins.then_inc(bank_full, 1)
            for c_ in range(DC):
                if c_ >= 2:
                    pe.wait_ge(tbank_free, c_ - 1)
                for t in range(NT):
                    pe.wait_ge(xn_ready, t + 1)
                    ins = pe.transpose(ps[:, TB + c_ % 2, t * P:(t + 1) * P], xn(t)[:, c_::DC], ident[:, :])
                ins.then_inc(tbank_full, 1)
            pe.wait_ge(tbank_free, DC)
            pe.wait_ge(d_kv, 16)
            for i, o in enumerate((0, 128, 256, 512)):
                pe.wait_ge(bank_free, i + 1)
                for c_ in range(DC):
                    ins = mm(ps[:, SB + i, :], w_kv[:, c_, o:o + P], hT[:, c_, :], c_ == 0, c_ == DC - 1)
                ins.then_inc(bank_full, 1)
            pe.wait_ge(d_small, 16 * N_SMALL)
            for w in range(2):
                pe.transpose(ps[:, TB + w, 0:16], pos_in[:, w, :], ident[0:16, 0:16]).then_inc(tbank_full, 1)
            for t in range(NT):
                pe.wait_ge(bank_free, 4 + t + 1)
                for o, n, at in ((384, 128, 0), (640, 152, 128)):
                    for c_ in range(DC):
                        ins = mm(ps[:, SB + t, at:at + n], hT[:, c_, t * P:(t + 1) * P], w_kv[:, c_, o:o + n],
                                 c_ == 0, c_ == DC - 1)
                ins.then_inc(bank_full, 1)
            pe.wait_ge(d_w1, 32)
            pe.wait_ge(tbank_free, PRE_T)
            for w in range(2):
                pe.wait_ge(bank_free, 8 + w + 1)
                for b in range(16):
                    ins = mm(ps[:, SB + w, 0:3 * NCMP].rearrange("p (h n) -> p h n", h=3), cmp_w1[:, w, b, :],
                             ckp[:, w, :, b:b + 8 * (NCMP - 1) + 1:8], b == 0, b == 15)
                ins.then_inc(bank_full, 1)

            def project(name, u):
                if name == "DV":
                    for t in range(NT):
                        for c_ in range(DC):
                            ins = mm(ps[:, SB + u % NBANK, t * P:(t + 1) * P], hT[:, c_, t * P:(t + 1) * P],
                                     w_slot[:, c_, 256:384], c_ == 0, c_ == DC - 1)
                else:
                    o = {"DQ": 0, "DK": 128, "NQ": 384}[name]
                    for c_ in range(DC):
                        ins = mm(ps[:, SB + u % NBANK, :], w_slot[:, c_, o:o + P], hT[:, c_, :], c_ == 0, c_ == DC - 1)
                ins.then_inc(bank_full, 1)

            pe.wait_ge(d_win, 96)
            for i, name in enumerate(("DQ", "DK", "DV", "NQ")):
                pe.wait_ge(bank_free, PRE_PROJ + i - NBANK + 1)
                project(name, PRE_PROJ + i)
            pe.wait_ge(gelu_ready, 2)
            pe.wait_ge(bank_free, 15)
            for h, rows in enumerate((lo, hi)):
                ins = mm(ps[rows, SB + 2, 0:NCMP], cmp_w2[:, 0, :], cmp_g[:, 0, h * NCMP:(h + 1) * NCMP])
            ins.then_inc(bank_full, 1)
            pe.wait_ge(bank_free, 16)
            for h in range(2):
                ins = mm(ps[0:NCMP, SB + 3, h * HD:(h + 1) * HD], cmp_g[:, 1, h * NCMP:(h + 1) * NCMP], cmp_w2[:, 1, :])
            ins.then_inc(bank_full, 1)
            pe.wait_ge(bank_full, PRE_USES)
            pe.sem_inc(values_done, PRE_V)

            def head_step(j, last):
                at = LAST_USE if last else USE

                def bank(u):
                    return SB + u % NBANK

                def scores(m, q, k):
                    u = at[MAPS[m][1]]
                    for i in range(NT):
                        bank_wait(pe, j, u + i)
                        mm(ps[:, bank(u + i), 0:LEN[i]], q[:, i * P:(i + 1) * P], k[:, 0:LEN[i]]).then_inc(bank_full, 1)

                def next_heads(name):
                    if not last:
                        bank_wait(pe, j, at[name])
                        project(name, at[name])

                def turn(unit, buf):
                    pe.wait_ge(p_ready, j * 6 + (unit + 1))
                    for k in range(NT):
                        pe.wait_ge(tbank_free, j * T_USES + (PRE_T + T_FIRST[unit] + k - 1))
                        for i in range(k, NT):
                            ins = pe.transpose(ps[:, TB + k % 2, (i - k) * P:(i - k + 1) * P],
                                               prob[:, buf, QOFF[i] + k * P:QOFF[i] + (k + 1) * P], ident[:, :])
                        ins.then_inc(tbank_full, 1)

                def values(unit, bank_, rows, v, first):
                    for k in range(NT):
                        pe.wait_ge(tbank_free, j * T_USES + (PRE_T + T_FIRST[unit] + k + 1))
                        ins = mm(ps[rows, bank_, k * P:SEQ], v(k), probT[:, unit % 2, TOFF[k]:TOFF[k] + TLEN[k]],
                                 first and k == 0, k == NT - 1)
                    ins.then_inc(values_done, 1)

                pe.wait_ge(bank_free, j * USES + PRE_USES)
                scores(M_A0, qd[:, 0, :], kd)
                scores(M_A1, qd[:, 1, :], kd)
                bank_wait(pe, j, at["CMP"])
                for hd in range(2):
                    for i in range(NT):
                        ins = mm(ps[:, bank(at["CMP"]), (hd * NT + i) * NCP:(hd * NT + i + 1) * NCP],
                                 qn[:, hd, i * P:(i + 1) * P], kcp[:, :])
                ins.then_inc(bank_full, 1)
                scores(M_S0, qn[:, 0, :], kslc)
                if not last:
                    pe.wait_ge(d_win, j * 80 + 176)
                next_heads("DQ")
                turn(T_A, 0)
                pe.wait_ge(od_free, j + AHEAD)
                values(T_A, OD, slice(0, P), lambda k: vd[:, k, :], True)
                scores(M_S1, qn[:, 1, :], kslc)
                next_heads("DK")
                turn(T_S0, 2)
                pe.wait_ge(on_free, j + AHEAD)
                values(T_S0, ON, lo, lambda k: vsw[:, 0, k, lo], True)
                scores(M_W0, qn[:, 0, :], kwin)
                pe.wait_ge(sq_ready, j + 1)
                bank_wait(pe, j, at["SUB"])
                mm(ps[:, bank(at["SUB"]), :], ones[:, :], sqv).then_inc(bank_full, 1)
                next_heads("DV")
                turn(T_S1, 0)
                values(T_S1, ON, hi, lambda k: vsw[:, 0, k, hi], True)
                scores(M_W1, qn[:, 1, :], kwin)
                next_heads("NQ")
                turn(T_W0, 1)
                values(T_W0, ON, lo, lambda k: vsw[:, 1, k, lo], False)
                for half, name in enumerate(("ADA0", "ADA1")):
                    pe.wait_ge(adacc_ready, j * 2 + (half + 1 + AHEAD))
                    bank_wait(pe, j, at[name])
                    mm(ps[:, bank(at[name]), :], ones[:, :], ada_acc[:, half, :]).then_inc(bank_full, 1)
                pe.wait_ge(p_ready, j * 6 + (T_C + 1))
                for hd in range(2):
                    pe.wait_ge(tbank_free, j * T_USES + (PRE_T + T_FIRST[T_C] + hd - 1))
                    for i in range(NT):
                        ins = pe.transpose(ps[0:NCP, TB + hd, i * P:(i + 1) * P], pc[:, hd, i, :], ident[:, :])
                    ins.then_inc(tbank_full, 1)
                for hd, rows in enumerate((lo, hi)):
                    pe.wait_ge(tbank_free, j * T_USES + (PRE_T + T_FIRST[T_C] + hd + 1))
                    ins = mm(ps[rows, ON, :], vcp[:, hd, :], probT[:, T_C % 2, hd * SEQ:(hd + 1) * SEQ], False, True)
                ins.then_inc(values_done, 1)
                turn(T_W1, 2)
                values(T_W1, ON, hi, lambda k: vsw[:, 1, k, hi], False)

            with pe.Fori(0, NJ - 1) as j:
                head_step(j, False)
            head_step(NJ - 1, True)

            pe.wait_ge(bank_free, ALL_USES)
            pe.wait_ge(od_free, NJ + AHEAD)
            pe.wait_ge(on_free, NJ + AHEAD)
            pe.wait_ge(d_wo, 48)

            def mixer(t):
                for n in range(2):
                    for c_ in range(DC):
                        ins = mm(ps[:, 2 * t + n, :], ov[:, c_, t * P:(t + 1) * P], wo[:, c_, n * 512:(n + 1) * 512],
                                 c_ == 0, c_ == DC - 1)
                ins.then_inc(mix_full, 1)

            def turn_h2(t):
                pe.wait_ge(h2_ready, t + 1)
                for c_ in range(DC):
                    ins = pe.transpose(ps[:, 2 * t + c_ // 4, (c_ % 4) * P:(c_ % 4 + 1) * P], h2_chunk(t, c_), ident[:, :])
                ins.then_inc(h2T_full, 1)

            def logits(t):
                pe.wait_ge(h2T_ready, t + 1)
                for c_ in range(DC):
                    ins = mm(ps[:, 2 * t, 0:NR], h2T[t % 2][:, c_, :], w_r[:, c_, :], c_ == 0, c_ == DC - 1)
                ins.then_inc(rout_full, 1)

            mixer(0)
            for t in range(1, NT):
                mixer(t)
                turn_h2(t - 1)
                logits(t - 1)
            turn_h2(NT - 1)
            logits(NT - 1)
            pe.wait_ge(m_ready, 1)
            pe.wait_ge(k_router, 7)
            msumf = msum.rearrange("p t e -> p (t e)")
            mm(ps[:, 1, 0:NT * NE], ones[:, :], msumf).then_inc(rank_full, 1)
            mm(ps[:, 0, 0:NT * NE], tri, msumf).then_inc(rank_full, 1)

            def gather(b):
                for t in range(NT):
                    for h, rows in enumerate((lo, hi)):
                        ins = mm(ps[rows, 0, :].rearrange("p (c q) -> p c q", c=4), sel1[b][:, t, :],
                                 ov[:, 4 * h:4 * h + 4, t * P:(t + 1) * P], t == 0, t == NT - 1)
                ins.then_inc(xg_full, 1)

            def turn_rows():
                for i in range(4):
                    ins = pe.transpose(ps[:, 1, i * P:(i + 1) * P], xg[:, i * P:(i + 1) * P], ident[:, :])
                ins.then_inc(xT_full, 1)

            def gate_up(b, done):
                for c_ in range(DC):
                    for h, rows in enumerate((lo, hi)):
                        ins = mm(ps[rows, 2 + b, :].rearrange("p (g n) -> p g n", g=2), xT[b][:, c_ % 4 * P + c_ // 4 * CAP:c_ % 4 * P + (c_ // 4 + 1) * CAP],
                                 gu_w[b][:, :, c_, h * 256:(h + 1) * 256], c_ == 0, c_ == DC - 1)
                ins.then_inc(done, 1)

            def turn_hidden(b, done):
                for jj in range(2):
                    ins = pe.transpose(ps[:, 4 + b, jj * P:(jj + 1) * P], hid[b][:, jj::2], ident[:, :])
                ins.then_inc(done, 1)

            def down(b, done):
                for i in range(4):
                    hf, jj = i // 2, i % 2
                    for n, rows in enumerate((lo, hi)):
                        ins = mm(ps[rows, 6 + b, :], hidT[b][:, jj * P + hf * CAP:jj * P + (hf + 1) * CAP],
                                 dn_w[b][:, hf, jj, n * 512:(n + 1) * 512], i == 0, i == 3)
                ins.then_inc(done, 1)

            def expert(e, b, use, following):
                pe.wait_ge(xT_ready, e + 1)
                pe.wait_ge(d_gu[b], use * 32 + 32)
                gate_up(b, gu_done)
                pe.wait_ge(sel_ready, e + 2)
                gather(following)
                pe.wait_ge(hid_ready, e + 1)
                turn_hidden(b, hT_full)
                pe.wait_ge(xg_ready, e + 2)
                turn_rows()
                pe.wait_ge(hidT_ready, e + 1)
                pe.wait_ge(d_wd[b], use * 32 + 32)
                down(b, d_done)

            pe.wait_ge(sel_ready, 1)
            gather(0)
            pe.wait_ge(xg_ready, 1)
            turn_rows()
            with pe.Fori(0, NE // 2) as g:
                for b in range(2):
                    expert(g * 2 + b, b, g, 1 - b)
            pe.wait_ge(over_ready, 2)
            n_blocks = pe.value_load(n_over[0:1, 0:1], min_val=0, max_val=MAX_EXTRA)
            with pe.Fori(0, MAX_EXTRA) as k:
                with pe.If(k < n_blocks):
                    pe.wait_ge(y_ready, k + NE)
                    expert(k + NE, 0, k + NE // 2, 0)
                    pe.wait_ge(over_ready, 2)

        @block.scalar
        def _(act):
            act.sem_inc(on_free, AHEAD)

            def cols(v):
                return v.rearrange("a (p n) -> (a p) n", p=P)

            for dst, src in ((gpc, g_pre_mix), (bsh, b_ada[0:1, 0:D]), (bsc, b_ada[0:1, D:2 * D])):
                act.dma_start(dst, cols(src)).then_inc(d_cols, 16)
            act.wait_ge(d_c, 16)
            act.activation(cexp, craw, ACT.Exp, scale=-1.0).then_inc(cexp_ready, 1)
            act.wait_ge(d_x, 16)
            for t in range(NT):
                act.activation(xn(t), xs[:, t, :], ACT.Square, accum_out=ssq[:, t:t + 1]).then_inc(ssq_ready, 1)
            act.wait_ge(ms_ready, 1)
            act.activation(rstd, ssq, ACT.Sqrt).then_inc(rt_ready, 1)
            act.wait_ge(rstd_ready, 1)
            for t in range(NT):
                act.wait_ge(ssq_ready, t + 1)
                act.activation(xn(t), xs[:, t, :], ACT.Copy, scale=rstd[:, t:t + 1]).then_inc(xn_ready, 1)
            act.wait_ge(cols_ready, 2)
            for c_ in range(DC):
                act.wait_ge(tbank_full, c_ + 1)
                act.activation(hT[:, c_, :], ps[:, TB + c_ % 2, :], ACT.Identity, scale=scc[:, c_:c_ + 1],
                               bias=shc[:, c_:c_ + 1]).then_inc(tbank_free, 1)
            act.wait_ge(k_zero, 4)
            for w in range(2):
                act.wait_ge(tbank_full, DC + w + 1)
                act.activation(ckp[:, w, 2, 0:16], ps[:, TB + w, 0:16], ACT.Copy).then_inc(tbank_free, 1)
            act.wait_ge(lam_ready, 2)
            act.activation(lame, lam2, ACT.Exp).then_inc(lame_ready, 1)
            act.wait_ge(bank_free, 12)
            act.activation(gates[:, :, :], gates[:, :, :], ACT.Exp, scale=-1.0).then_inc(gexp_ready, 1)
            for w in range(2):
                act.wait_ge(bank_free, 12 + w + 1)
                act.activation(cmp_g[:, w, 0:62], cmp_h[:, w, 0:62], ACT.Gelu_apprx_tanh,
                               bias=cmp_h[:, w, 62:63]).then_inc(gelu_ready, 1)
            act.wait_ge(bank_full, 12)
            load_gu(act, 0, 0, d_gu[0])
            load_wd(act, 0, 0, d_wd[0])
            act.wait_ge(bank_full, PRE_USES)

            def head_step(j, last):
                at = LAST_USE if last else USE

                def exps(m):
                    act.wait_ge(neg_ready, j * 6 + (m + 1))
                    for i in range(NT):
                        p_ = prob[:, MAPS[m][2], QOFF[i]:QOFF[i] + LEN[i]]
                        ins = act.activation(p_, p_, ACT.Exp, bias=nmx[:, m, i:i + 1], accum_out=lsum[:, m, i:i + 1])
                    ins.then_inc(exp_done, 1)

                def take(unit):
                    act.wait_ge(values_done, j * 6 + (PRE_V + unit - 1))
                    for k in range(NT):
                        act.wait_ge(tbank_full, j * T_USES + (PRE_T + T_FIRST[unit] + k + 1))
                        act.activation(probT[:, unit % 2, TOFF[k]:TOFF[k] + TLEN[k]], ps[:, TB + k % 2, 0:TLEN[k]],
                                       ACT.Copy).then_inc(tbank_free, 1)

                exps(M_A0)
                exps(M_A1)
                act.wait_ge(cmp_sub, j + 1)
                for hd in range(2):
                    p_ = pc[:, hd, :, :]
                    ins = act.activation(p_, p_, ACT.Exp, scale=slope[:, 1 + hd:2 + hd])
                ins.then_inc(cmp_exp, 1)
                exps(M_S0)
                take(T_A)
                act.wait_ge(values_done, j * 6 + (PRE_V + T_A + 1))
                act.wait_ge(od_free, j + AHEAD)
                act.activation(sqv, ps[:, OD, :], ACT.Square).then_inc(sq_ready, 1)
                exps(M_S1)
                take(T_S0)
                exps(M_W0)
                act.wait_ge(bank_free, j * USES + (PRE_USES + at["SUB"] + 1))
                act.activation(sqv, sqv, ACT.Sqrt).then_inc(subrt_ready, 1)
                take(T_S1)
                exps(M_W1)
                take(T_W0)
                act.wait_ge(values_done, j * 6 + (PRE_V + T_C - 1))
                for hd in range(2):
                    act.wait_ge(tbank_full, j * T_USES + (PRE_T + T_FIRST[T_C] + hd + 1))
                    act.activation(probT[0:NCP, T_C % 2, hd * SEQ:(hd + 1) * SEQ], ps[0:NCP, TB + hd, :],
                                   ACT.Copy).then_inc(tbank_free, 1)
                take(T_W1)
                act.wait_ge(values_done, j * 6 + (PRE_V + T_W1 + 1))
                act.activation(ovf[:, bass.ds(j * SEQ + 4 * SEQ, SEQ)], ps[:, ON, :], ACT.Copy).then_inc(on_free, 1)

            with act.Fori(0, NJ - 1) as j:
                head_step(j, False)
            head_step(NJ - 1, True)

            def take_h2T(t):
                act.wait_ge(h2T_full, t + 1)
                if t >= 2:
                    act.wait_ge(rout_full, t - 1)
                act.activation(h2T[t % 2], ps[:, 2 * t:2 * t + 2, :].rearrange("p a (c n) -> p (a c) n", c=4),
                               ACT.Copy).then_inc(h2T_ready, 1)

            act.wait_ge(mods_ready, 4)
            for t in range(NT):
                act.wait_ge(mix_full, t + 1)
                act.activation(sqj, ps[:, 2 * t:2 * t + 2, :], ACT.Square, accum_out=ssq2[:, t:t + 1]).then_inc(mixsq, 1)
                if t:
                    take_h2T(t - 1)
                act.wait_ge(mixms, t + 1)
                act.activation(rstd2[:, t:t + 1], ssq2[:, t:t + 1], ACT.Sqrt).then_inc(mixrt, 1)
                act.wait_ge(x1_ready, t + 1)
                act.activation(sqj, xs[:, t, :].rearrange("p (a b) -> p a b", a=2), ACT.Square,
                               accum_out=ssq2[:, 4 + t:5 + t]).then_inc(x1sq, 1)
                act.wait_ge(x1ms, t + 1)
                act.activation(rstd2[:, 4 + t:5 + t], ssq2[:, 4 + t:5 + t], ACT.Sqrt).then_inc(x1rt, 1)
            take_h2T(NT - 1)
            act.wait_ge(eg_in, 1)
            act.activation(eg, eg, ACT.Exp).then_inc(eg_out, 1)
            act.wait_ge(e2_in, 1)
            act.activation(rt[:, 4, :], rt[:, 4, :], ACT.Exp).then_inc(e2_out, 1)

            def expert(e, b, following, buffer_free):
                act.wait_ge(gu_done, e + 1)
                act.activation(sg[b], ps[:, 2 + b, 0:256], ACT.Silu).then_inc(sg_ready, 1)
                act.wait_ge(xg_full, e + 2)
                act.activation(xg, ps[:, 0, :], ACT.Copy).then_inc(xg_ready, 1)
                act.wait_ge(xT_full, e + 2)
                act.activation(xT[following], ps[:, 1, :], ACT.Copy).then_inc(xT_ready, 1)
                act.wait_ge(d_done, e + 1)
                if buffer_free is not None:
                    act.wait_ge(y_out[b], buffer_free)
                act.activation(yb[b], ps[:, 6 + b, :], ACT.Copy).then_inc(y_ready, 1)

            act.wait_ge(xg_full, 1)
            act.activation(xg, ps[:, 0, :], ACT.Copy).then_inc(xg_ready, 1)
            act.wait_ge(xT_full, 1)
            act.activation(xT[0], ps[:, 1, :], ACT.Copy).then_inc(xT_ready, 1)
            for b in range(2):
                expert(b, b, 1 - b, None)
            with act.Fori(1, NE // 2) as g:
                for b in range(2):
                    expert(g * 2 + b, b, 1 - b, g * 16)
            act.wait_ge(over_ready, 2)
            n_blocks = act.value_load(n_over[0:1, 0:1], min_val=0, max_val=MAX_EXTRA)
            with act.Fori(0, MAX_EXTRA) as k:
                with act.If(k < n_blocks):
                    expert(k + NE, 0, 0, k * 16 + 16 * (NE // 2))

            def root(t):
                act.wait_ge(f_ready, t + 1)
                act.activation(fsqj, ytok[t][:, 0:D], ACT.Square, accum_out=ssq3[:, t:t + 1]).then_inc(fsq, 1)
                act.wait_ge(fms, t + 1)
                act.activation(rstd3[:, t:t + 1], ssq3[:, t:t + 1], ACT.Sqrt).then_inc(frt, 1)

            for t in range(NT):
                act.wait_ge(y_back[t], 32)
                y0 = ytok[t][:, 0:D]
                act.activation(y0, y0, ACT.Copy, scale=wts[:, t, 0:1]).then_inc(y0_ready, 1)
                if t:
                    root(t - 1)
            root(NT - 1)

        @block.vector
        def _(dve):
            dve.sem_inc(adacc_ready, AHEAD)
            dve.sem_inc(od_free, AHEAD)
            steps = [0]

            def step(ins):
                steps[0] += 1
                ins.then_inc(v_step, 1)
                dve.wait_ge(v_step, steps[0])

            def mean_square(ap, n):
                return dve.tensor_scalar(ap, ap, 1.0 / n, EPS, ALU.mult, ALU.add)

            dve.wait_ge(cexp_ready, 1)
            step(dve.tensor_scalar(cexp, cexp, 1.0, None, ALU.add))
            step(dve.reciprocal(cexp, cexp))
            step(dve.tensor_tensor(cs, craw, cexp, ALU.mult))

            def weigh(buf, w, advance, last):
                advance(dve.tensor_scalar(ada_acc[:, buf, :], w[:, 0, :], cs[:, 0:1], None, ALU.mult))
                for c_ in range(1, DC):
                    ins = dve.scalar_tensor_tensor(ada_acc[:, buf, :], w[:, c_, :], cs[:, c_:c_ + 1],
                                                   ada_acc[:, buf, :], ALU.mult, ALU.add)
                    if c_ < DC - 1:
                        advance(ins)
                ins.then_inc(last, 1)

            for i, s in enumerate((d_ada0, d_win, d_ada, d_ada3)):
                dve.wait_ge(s, 16)
                if i >= 2:
                    dve.wait_ge(bank_full, i - 1)
                weigh(i % 2, ada_early[i].rearrange("p (c n) -> p c n", c=DC), step, acc_ready)
                if i == 1:
                    dve.wait_ge(ssq_ready, NT)
                    mean_square(ssq, D).then_inc(ms_ready, 1)
                if i == 2:
                    dve.wait_ge(rt_ready, 1)
                    dve.reciprocal(rstd, rstd).then_inc(rstd_ready, 1)
            dve.wait_ge(d_cols, 48)
            dve.wait_ge(bank_full, 4)
            step(dve.tensor_tensor(bsc, bsc, ps[:, SB + 1, 0:DC], ALU.add))
            dve.scalar_tensor_tensor(scc, bsc, 1.0, gpc, ALU.add, ALU.mult).then_inc(cols_ready, 1)
            dve.tensor_tensor(shc, ps[:, SB, 0:DC], bsh, ALU.add).then_inc(cols_ready, 1)
            dve.wait_ge(cols_ready, 2)
            for i in range(4):
                dve.sem_inc(bank_free, 1)
            dve.wait_ge(d_small, 16 * N_SMALL)
            for i in range(2):
                dve.tensor_tensor_reduce(lam_junk[:, i, :], lam_in[:, 2 * i, :], lam_in[:, 2 * i + 1, :], 1.0, 0.0,
                                         ALU.mult, ALU.add, lam2[:, i:i + 1]).then_inc(lam_ready, 1)
            step(dve.tensor_scalar(gsub, gsub, 1.0 - LAMBDA_INIT, None, ALU.mult))
            dve.wait_ge(lame_ready, 1)
            step(dve.tensor_tensor(lamd, lame[:, 0:1], lame[:, 1:2], ALU.subtract))
            step(dve.tensor_scalar(nlam, lamd, -1.0, -LAMBDA_INIT, ALU.mult, ALU.add))

            dve.wait_ge(k_zero, 4)
            for w in range(2):
                dve.wait_ge(bank_full, 4 + w + 1)
                for h, rows in enumerate((slice(0, HD), slice(HD, P))):
                    for par, to in enumerate((slice(0, HD), slice(HD, P))):
                        ins = dve.tensor_copy(ckp[to, w, h, :], ps[rows, SB + w, par::2])
                ins.then_inc(bank_free, 1)
            for i, k_ in ((2, kslc), (3, kwin)):
                dve.wait_ge(bank_full, 4 + i + 1)
                dve.tensor_copy(k_[:, :], ps[:, SB + i, :]).then_inc(bank_free, 1)
            gv = gates[:, :, :].rearrange("p h (n t) -> p h n t", t=NT)
            for t in range(NT):
                dve.wait_ge(bank_full, 8 + t + 1)
                dve.tensor_copy(vsw[:, :, t, :], ps[:, SB + t, 0:256].rearrange("p (w n) -> p w n", w=2))
                dve.tensor_copy(gv[:, :, :, t], ps[:, SB + t, 256:280].rearrange("p (h n) -> p h n", h=2)).then_inc(bank_free, 1)
            for w in range(2):
                dve.wait_ge(bank_full, 12 + w + 1)
                dve.tensor_copy(cmp_h[:, w, 0:63], ps[:, SB + w, 0:63]).then_inc(bank_free, 1)
            dve.wait_ge(gexp_ready, 1)
            step(dve.tensor_scalar(gates[:, :, :], gates[:, :, :], 1.0, None, ALU.add))
            step(dve.reciprocal(gates[:, :, :], gates[:, :, :]))

            def drain(name, u):
                src = ps[:, SB + u % NBANK, :]
                if name in ("DQ", "NQ"):
                    q, (c0, c1) = (qd, (0, 0)) if name == "DQ" else (qn, (1, 2))
                    dve.tensor_scalar(q[0:HD, 0, :], src[0:HD], qsc[0:HD, c0:c0 + 1], None, ALU.mult)
                    ins = dve.tensor_scalar(q[HD:P, 1, :], src[HD:P], qsc[HD:P, c1:c1 + 1], None, ALU.mult)
                elif name == "DK":
                    ins = dve.tensor_copy(kd[:, :], src)
                else:
                    ins = dve.tensor_copy(vd[:, :, :].rearrange("p t n -> p (t n)"), src)
                ins.then_inc(bank_free, 1)

            dve.wait_ge(k_const, N_CONST)
            step(dve.tensor_tensor(qsc, qsc, qs_r, ALU.mult))
            for i, name in enumerate(("DQ", "DK", "DV", "NQ")):
                dve.wait_ge(bank_full, PRE_PROJ + i + 1)
                drain(name, PRE_PROJ + i)
            dve.wait_ge(bank_full, 19)
            dve.tensor_copy(kcp[:, 0:NCMP], ps[:, SB + 2, 0:NCMP]).then_inc(bank_free, 1)
            dve.wait_ge(bank_full, 20)
            dve.tensor_copy(vcp[0:NCMP, :, :], ps[0:NCMP, SB + 3, 0:P].rearrange("p (h n) -> p h n", h=2)).then_inc(bank_free, 1)

            def head_step(j, last):
                at = LAST_USE if last else USE
                n = [0]

                def lstep(ins):
                    n[0] += 1
                    ins.then_inc(v_loop, 1)
                    dve.wait_ge(v_loop, j * V_LOOP + n[0])

                def full(u):
                    dve.wait_ge(bank_full, j * USES + (PRE_USES + u + 1))

                def self_read(u):
                    dve.wait_ge(bank_free, j * USES + (PRE_USES + u + 1))

                def bank(u):
                    return SB + u % NBANK

                def next_heads(name):
                    if not last:
                        full(at[name])
                        drain(name, at[name])

                def biased(m, buf_free):
                    col_, name, buf = MAPS[m]
                    u = at[name]
                    dve.wait_ge(tbank_full, j * T_USES + (PRE_T + buf_free))
                    for i in range(NT):
                        full(u + i)
                        dve.sem_inc(scores_seen, 1)
                        dve.tensor_tensor_reduce(prob[:, buf, QOFF[i]:QOFF[i] + LEN[i]], ps[:, bank(u + i), 0:LEN[i]],
                                                 dist[:, SEQ - LEN[i]:SEQ], slope[:, col_:col_ + 1], -3.0e38, ALU.add,
                                                 ALU.max, mx[:, m, i:i + 1]).then_inc(bank_free, 1)
                    self_read(u + NT - 1)
                    dve.tensor_scalar(nmx[:, m, :], mx[:, m, :], -1.0, None, ALU.mult).then_inc(neg_ready, 1)

                def weighted(m, g_):
                    buf = MAPS[m][2]
                    dve.wait_ge(exp_done, j * 6 + (m + 1))
                    lstep(dve.tensor_scalar(rl[:, m, :], lsum[:, m, :], SUM_FLOOR, None, ALU.max))
                    lstep(dve.reciprocal(rl[:, m, :], rl[:, m, :]))
                    lstep(dve.tensor_tensor(rl[:, m, :], rl[:, m, :], g_, ALU.mult))
                    for i in range(NT):
                        p_ = prob[:, buf, QOFF[i]:QOFF[i] + LEN[i]]
                        ins = dve.tensor_scalar(p_, p_, rl[:, m, i:i + 1], None, ALU.mult)
                    ins.then_inc(p_ready, 1)

                dve.tensor_tensor(slope, slope, sl_r, ALU.mult).then_inc(v_loop, 1)
                n[0] += 1
                lstep(dve.tensor_copy(gcur.rearrange("p h b t -> p h (b t)"), gates[:, :, bass.ds(j * 12, 12)]))
                biased(M_A0, T_FIRST[T_W0] + NT - T_USES)
                biased(M_A1, T_FIRST[T_W0] + NT - T_USES)
                full(at["CMP"])
                for hd in range(2):
                    ins = dve.tensor_tensor(pc[:, hd, :, :], ps[:, bank(at["CMP"]), hd * P:(hd + 1) * P].rearrange(
                        "p (t n) -> p t n", t=NT), dist_c[:, :, :], ALU.add)
                ins.then_inc(bank_free, 1)
                self_read(at["CMP"])
                pc8 = pc[:, :, :, :].rearrange("p h t n -> p (h t) n")
                lstep(dve.tensor_reduce(cmx, pc8, AX, ALU.max))
                lstep(dve.tensor_scalar(cmx, cmx, MAX_FLOOR, None, ALU.max))
                dve.tensor_tensor(pc8, pc8, cmx.unsqueeze(2).to_broadcast([P, 8, NCP]), ALU.subtract).then_inc(cmp_sub, 1)
                biased(M_S0, 0)
                dve.wait_ge(exp_done, j * 6 + 2)
                lstep(dve.tensor_scalar(rl[:, 0:2, :], lsum[:, 0:2, :], SUM_FLOOR, None, ALU.max))
                lstep(dve.reciprocal(rl[:, 0:2, :], rl[:, 0:2, :]))
                lstep(dve.tensor_scalar(rl[:, 1, :], rl[:, 1, :], nlam, None, ALU.mult))
                for i in range(NT):
                    p1 = prob[:, 1, QOFF[i]:QOFF[i] + LEN[i]]
                    ins = dve.tensor_scalar(p1, p1, rl[:, 1, i:i + 1], None, ALU.mult)
                lstep(ins)
                for i in range(NT):
                    p0, p1 = (prob[:, b, QOFF[i]:QOFF[i] + LEN[i]] for b in range(2))
                    ins = dve.scalar_tensor_tensor(p0, p0, rl[:, 0, i:i + 1], p1, ALU.mult, ALU.add)
                ins.then_inc(p_ready, 1)
                if not last:
                    lstep(dve.tensor_tensor(qsc, qsc, qs_r, ALU.mult))
                next_heads("DQ")
                weighted(M_S0, gcur[:, 0, 1, :])
                biased(M_S1, T_FIRST[T_A] + NT)
                dve.wait_ge(d_ada, j * 32 + 32)
                weigh(0, ada_slot, lstep, adacc_ready)
                next_heads("DK")
                biased(M_W0, T_FIRST[T_A] + NT)
                weighted(M_S1, gcur[:, 1, 1, :])
                full(at["SUB"])
                dve.tensor_scalar(sqv, ps[:, bank(at["SUB"]), :], 1.0 / P, EPS, ALU.mult, ALU.add).then_inc(bank_free, 1)
                dve.wait_ge(d_ada, j * 32 + 48)
                weigh(1, ada_slot, lstep, adacc_ready)
                next_heads("DV")
                biased(M_W1, T_FIRST[T_S0] + NT)
                weighted(M_W0, gcur[:, 0, 2, :])
                next_heads("NQ")
                dve.wait_ge(cmp_exp, j + 1)
                lstep(dve.tensor_reduce(cl, pc8, AX, ALU.add))
                lstep(dve.tensor_scalar(cl, cl, SUM_FLOOR, None, ALU.max))
                lstep(dve.reciprocal(cl, cl))
                clv = cl.rearrange("p (h t) -> p h t", h=2)
                lstep(dve.tensor_tensor(clv, clv, gcur[:, :, 0, :], ALU.mult))
                dve.tensor_tensor(pc8, pc8, cl.unsqueeze(2).to_broadcast([P, 8, NCP]), ALU.mult).then_inc(p_ready, 1)
                weighted(M_W1, gcur[:, 1, 2, :])
                dve.wait_ge(subrt_ready, j + 1)
                lstep(dve.reciprocal(sqv, sqv))
                dve.scalar_tensor_tensor(ovf[:, bass.ds(j * SEQ, SEQ)], ps[:, OD, :], gsub, sqv, ALU.mult,
                                         ALU.mult).then_inc(od_free, 1)
                for half, name in enumerate(("ADA0", "ADA1")):
                    full(at[name])
                    dve.tensor_copy(modsf[:, bass.ds(j * D + half * 512, 512)], ps[:, bank(at[name]), :]).then_inc(bank_free, 1)
                assert last or n[0] == V_LOOP, n[0]

            with dve.Fori(0, NJ - 1) as j:
                head_step(j, False)
            head_step(NJ - 1, True)

            dve.wait_ge(d_bc, 16 * 7)
            dve.wait_ge(bank_free, ALL_USES)
            step(dve.tensor_tensor(modsf, modsf, e1[:, 0:4 * D], ALU.add))
            dve.tensor_tensor(mods[:, 0, :], mods[:, 0, :], bc_rows[:, 4, :], ALU.mult).then_inc(mods_ready, 1)
            dve.scalar_tensor_tensor(mods[:, 2, :], mods[:, 2, :], 1.0, bc_rows[:, 5, :], ALU.add, ALU.mult).then_inc(mods_ready, 1)
            dve.tensor_tensor(mods[:, 3, :], mods[:, 3, :], bc_rows[:, 6, :], ALU.mult).then_inc(mods_ready, 2)
            dve.wait_ge(mods_ready, 4)

            mixv = [ps[:, 2 * t:2 * t + 2, :] for t in range(NT)]
            for t in range(NT):
                dve.wait_ge(mixsq, t + 1)
                mean_square(ssq2[:, t:t + 1], D).then_inc(mixms, 1)
                dve.wait_ge(mixrt, t + 1)
                step(dve.reciprocal(rstd2[:, t:t + 1], rstd2[:, t:t + 1]))
                step(dve.scalar_tensor_tensor(tmpx.rearrange("p (a b) -> p a b", a=2), mixv[t], rstd2[:, t:t + 1],
                                              mods[:, 0, :].rearrange("p (a b) -> p a b", a=2), ALU.mult, ALU.mult))
                dve.tensor_tensor(xs[:, t, :], xs[:, t, :], tmpx, ALU.add).then_inc(x1_ready, 1)
                dve.wait_ge(x1sq, t + 1)
                mean_square(ssq2[:, 4 + t:5 + t], D).then_inc(x1ms, 1)
                dve.wait_ge(x1rt, t + 1)
                step(dve.reciprocal(rstd2[:, 4 + t:5 + t], rstd2[:, 4 + t:5 + t]))
                step(dve.scalar_tensor_tensor(h2[t], xs[:, t, :].rearrange("p (q c) -> p q c", c=DC), rstd2[:, 4 + t:5 + t],
                                              mods[:, 2, :].rearrange("p (q c) -> p q c", c=DC), ALU.mult, ALU.mult))
                dve.tensor_tensor(h2[t], h2[t], mods[:, 1, :].rearrange("p (q c) -> p q c", c=DC), ALU.add).then_inc(h2_ready, 1)

            for t in range(NT):
                dve.wait_ge(rout_full, t + 1)
                dve.tensor_tensor(lg[:, t, :], ps[:, 2 * t, 0:NR], bias_r[:, :], ALU.add).then_inc(lg_ready, 1)
            dve.wait_ge(lg_ready, NT)
            dve.wait_ge(k_router, 7)
            b8, b64 = [P, NT, NG], [P, NT, NE]
            mg, v1, v2 = rt[:, 0, :], rt[:, 2, :], rt[:, 3, :]
            e2 = rt[:, 4, :]

            def wide(ap, shape):
                return ap.unsqueeze(2).to_broadcast(shape)

            def first_max(onehot, vals, mval, keyrow, shape, kk_):
                step(dve.tensor_tensor(onehot, vals, wide(mval, shape), ALU.is_equal))
                step(dve.tensor_tensor(onehot, onehot, keyrow.unsqueeze(1).to_broadcast(shape), ALU.mult))
                step(dve.tensor_reduce(kk_, onehot, AX, ALU.max))
                step(dve.tensor_tensor(onehot, onehot, wide(kk_, shape), ALU.is_equal))

            step(dve.tensor_reduce(mg, lg[:, :, 0:NG], AX, ALU.max))
            dve.tensor_tensor(eg, lg[:, :, 0:NG], wide(mg, b8), ALU.subtract).then_inc(eg_in, 1)
            first_max(ohg, lg[:, :, 0:NG], mg, key8, b8, rt[:, 1, :])
            b88 = [P, NT, NG, NE // NG]
            le4, lem4, sel4 = (a.rearrange("p t (g e) -> p t g e", g=NG) for a in (lg[:, :, NG:NR], lem, sel))
            oh4 = ohg.unsqueeze(3).to_broadcast(b88)
            step(dve.tensor_tensor(lem4, le4, oh4, ALU.mult))
            step(dve.tensor_scalar(sel4, oh4, 1.0, -NEG, ALU.subtract, ALU.mult))
            step(dve.tensor_tensor(lem4, lem4, sel4, ALU.add))
            step(dve.tensor_reduce(v1, lem, AX, ALU.max))
            first_max(oh[0], lem, v1, key64, b64, rt[:, 5, :])
            step(dve.scalar_tensor_tensor(lem, oh[0], 4.0 * NEG, lem, ALU.mult, ALU.add))
            step(dve.tensor_reduce(v2, lem, AX, ALU.max))
            first_max(oh[1], lem, v2, key64, b64, rt[:, 6, :])
            dve.tensor_tensor(msum, oh[0], oh[1], ALU.add).then_inc(m_ready, 1)
            dve.tensor_tensor(e2, v2, v1, ALU.subtract).then_inc(e2_in, 1)
            dve.wait_ge(eg_out, 1)
            step(dve.tensor_reduce(pgrp, eg, AX, ALU.add))
            dve.wait_ge(e2_out, 1)
            step(dve.tensor_scalar(mg, e2, 1.0, None, ALU.add))
            step(dve.tensor_tensor(mg, mg, pgrp, ALU.mult))
            step(dve.reciprocal(wts[:, :, 0], mg))
            step(dve.tensor_tensor(wts[:, :, 1], wts[:, :, 0], e2, ALU.mult))

            step(dve.tensor_scalar(e8, rt[:, 5:7, :], -1.0, float(NE), ALU.mult, ALU.add))
            dve.wait_ge(rank_full, 1)
            step(dve.tensor_copy(csum, ps[:, 1, 0:NT * NE].rearrange("p (t e) -> p t e", t=NT)))
            for t in range(1, NT):
                step(dve.tensor_tensor(csum[:, t, :], csum[:, t, :], csum[:, t - 1, :], ALU.add))
            dve.wait_ge(rank_full, 2)
            ranks = ps[:, 0, 0:NT * NE].rearrange("p (t e) -> p t e", t=NT)
            dve.tensor_copy(rank[:, 0, :], ranks[:, 0, :]).then_inc(v_step, 1)
            steps[0] += 1
            step(dve.tensor_tensor(rank[:, 1:NT, :], ranks[:, 1:NT, :], csum[:, 0:NT - 1, :], ALU.add))
            cnt = csum[:, NT - 1, :]
            thr3 = thr[:, 0:NCMPR * NE].rearrange("p (m e) -> p m e", m=NCMPR)
            cmp3 = cmpx[:, 0:NCMPR * NE].rearrange("p (m e) -> p m e", m=NCMPR)
            step(dve.tensor_tensor(cmp3, cnt.unsqueeze(1).to_broadcast([P, NCMPR, NE]), thr3, ALU.is_gt))
            step(dve.tensor_reduce(extra_row, cmp3.rearrange("p m e -> p e m"), AX, ALU.add))
            step(dve.tensor_tensor_scan(cum, ones[:, 0:NE], extra_row, 0.0, ALU.mult, ALU.add))
            step(dve.tensor_tensor(base_e, cum, extra_row, ALU.subtract))
            b2 = [P, 2, NT, NE]

            def of_chosen(out_, table):
                step(dve.tensor_tensor(pick, oh2, table, ALU.mult))
                step(dve.tensor_reduce(out_.rearrange("p (k t) -> p k t", k=2), pick, AX, ALU.add))

            of_chosen(rank8, rank.unsqueeze(1).to_broadcast(b2))
            of_chosen(base8, base_e.unsqueeze(1).unsqueeze(1).to_broadcast(b2))
            step(dve.tensor_tensor(over8, rank8.unsqueeze(2).to_broadcast([P, 8, NCMPR]),
                                   thr[:, 0:NCMPR * NE:NE].unsqueeze(1).to_broadcast([P, 8, NCMPR]), ALU.is_ge))
            step(dve.tensor_reduce(blk8, over8, AX, ALU.add))
            e8f = e8.rearrange("p k t -> p (k t)")
            dve.scalar_tensor_tensor(rank8, blk8, -float(CAP), rank8, ALU.mult, ALU.add).then_inc(v_step, 1)
            steps[0] += 1
            step(dve.scalar_tensor_tensor(base8, base8, float(NE - 1), blk8, ALU.add, ALU.add))
            dve.tensor_scalar(blk8, blk8, 1.0, None, ALU.min).then_inc(v_step, 1)
            steps[0] += 1
            step(dve.tensor_tensor(base8, base8, e8f, ALU.subtract))
            step(dve.tensor_tensor(base8, base8, blk8, ALU.mult))
            step(dve.tensor_tensor(base8, base8, e8f, ALU.add))
            step(dve.scalar_tensor_tensor(addr_f, rank8, float(NCOL), base8, ALU.mult, ALU.add))
            dve.tensor_copy(addr_i[:, :], addr_f).then_inc(addr_ready, 1)

            def moved_on(ins, count):
                ins.then_inc(v_moe, 1)
                dve.wait_ge(v_moe, count)

            def next_one_hots(b, count, done):
                av = addr_f.rearrange("p (k t) -> p k t", k=2)
                moved_on(dve.tensor_tensor(sel2, av.unsqueeze(3).to_broadcast([P, 2, NT, CAP]),
                                           slot_addr.unsqueeze(1).unsqueeze(1).to_broadcast([P, 2, NT, CAP]),
                                           ALU.is_equal), count)
                dve.tensor_tensor(sel1[b], sel2[:, 0], sel2[:, 1], ALU.add).then_inc(done, 1)
                moved_on(dve.tensor_scalar(addr_f, addr_f, 1.0, None, ALU.subtract), count + 1)

            dve.wait_ge(addr_ready, 1)
            next_one_hots(0, 1, sel_ready)
            oe = cmpx[0:1, 0:(MAX_EXTRA + 1) * NE].rearrange("p (k e) -> p k e", e=NE)
            kr = thr[0:1, 512:512 + MAX_EXTRA + 1]
            step(dve.tensor_tensor(oe, cum[0:1, :].unsqueeze(1).to_broadcast([1, MAX_EXTRA + 1, NE]),
                                   kr.unsqueeze(2).to_broadcast([1, MAX_EXTRA + 1, NE]), ALU.is_le))
            step(dve.tensor_reduce(small[0:1, OVF:OVF + MAX_EXTRA + 1], oe, AX, ALU.add))
            dve.tensor_scalar(over_e[0:1, :], small[0:1, OVF:OVF + MAX_EXTRA + 1], float(NE - 1), None, ALU.min).then_inc(over_ready, 1)
            dve.tensor_copy(n_over[0:1, 0:1], cum[0:1, NE - 1:NE]).then_inc(over_ready, 1)
            dve.wait_ge(lists_loaded, 32)
            dve.tensor_scalar(sidx[0:CAP, :], sidx[0:CAP, :], 2.0, None, ALU.mult).then_inc(idx_ready, 1)
            dve.tensor_scalar(sidx[CAP:P, :], sidx[CAP:P, :], 2.0, 1.0, ALU.mult, ALU.add).then_inc(idx_ready, 1)

            def expert(e, b, following):
                dve.wait_ge(xg_full, e + 1)
                next_one_hots(following, e * 2 + 3, sel_ready)
                dve.wait_ge(sg_ready, e + 1)
                dve.tensor_tensor(hid[b], sg[b], ps[:, 2 + b, 256:512], ALU.mult).then_inc(hid_ready, 1)
                dve.wait_ge(hT_full, e + 1)
                dve.tensor_copy(hidT[b], ps[:, 4 + b, 0:256]).then_inc(hidT_ready, 1)

            with dve.Fori(0, NE // 2) as g:
                for b in range(2):
                    expert(g * 2 + b, b, 1 - b)
            dve.wait_ge(over_ready, 2)
            n_blocks = dve.value_load(n_over[0:1, 0:1], min_val=0, max_val=MAX_EXTRA)
            with dve.Fori(0, MAX_EXTRA) as k:
                with dve.If(k < n_blocks):
                    expert(k + NE, 0, 0)

            def finish(t):
                y0, y1 = ytok[t][:, 0:D], ytok[t][:, D:2 * D]
                dve.wait_ge(fsq, t + 1)
                mean_square(ssq3[:, t:t + 1], D).then_inc(fms, 1)
                dve.wait_ge(frt, t + 1)
                step(dve.reciprocal(rstd3[:, t:t + 1], rstd3[:, t:t + 1]))
                dve.scalar_tensor_tensor(y1, y0, rstd3[:, t:t + 1], mods[:, 3, :], ALU.mult, ALU.mult).then_inc(f_scaled, 1)

            for t in range(NT):
                y0, y1 = ytok[t][:, 0:D], ytok[t][:, D:2 * D]
                dve.wait_ge(y0_ready, t + 1)
                dve.scalar_tensor_tensor(y0, y1, wts[:, t, 1:2], y0, ALU.mult, ALU.add).then_inc(f_ready, 1)
                if t:
                    finish(t - 1)
            finish(NT - 1)


_INS = ['x', 'c', 'w_ada', 'b_ada', 'g_pre_mix', 'g_post_mix', 'g_pre_ffn', 'g_post_ffn', 'w_in',
        'lam_q1', 'lam_k1', 'lam_q2', 'lam_k2', 'g_subln', 'cmp_pos_k', 'cmp_pos_v', 'cmp_w1_k', 'cmp_w1_v',
        'cmp_w2_k', 'cmp_w2_v', 'w_out', 'w_router_grp', 'b_router_grp', 'w_router_exp', 'b_router_exp',
        'w_exp_gate', 'w_exp_up', 'w_exp_down']


def kernel(**inputs):
    import numpy as _np
    import concourse.bacc as _bacc
    from concourse import mybir as _mybir
    from concourse.bass_utils import run_bass_kernel_spmd as _run

    nc = _bacc.Bacc("TRN2", target_bir_lowering=False, num_devices=1)
    arrays, args = {}, []
    for name in _INS:
        a = _np.ascontiguousarray(inputs[name])
        arrays[f"in_{name}_dram"] = a
        args.append(nc.dram_tensor(f"in_{name}_dram", a.shape, _mybir.dt.from_np(a.dtype), kind="ExternalInput").ap())
    args.append(nc.dram_tensor("out_dram", (1, SEQ, D), F32, kind="ExternalOutput").ap())
    build(nc, *args)
    r = _run(nc, [arrays], core_ids=[0])
    return r.results[0]["out_dram"]
```

```python
from contextlib import ExitStack

import concourse.bass as bass
from concourse import mybir

F32 = mybir.dt.float32
I32 = mybir.dt.int32
ALU = mybir.AluOpType
ACT = mybir.ActivationFunctionType
AX = mybir.AxisListType.X

P = 128
D = 1024
SEQ = 512
DC = D // P
NT = SEQ // P
HD = 64
NJ = 4
NCMP = 31
NCP = 32
CMP_BLOCK = 32
CMP_STRIDE = 16
NEG = -1e30
MAX_FLOOR = -1e20
SUM_FLOOR = 1e-30
EPS = 1e-6
LAMBDA_INIT = 0.8 - 0.6
SCALE = HD ** -0.5
NG = 8
NE = 64
NR = NG + NE
F = 512
CAP = 64
MAX_EXTRA = 2 * SEQ // (CAP + 1)
NCOL = NE + MAX_EXTRA + 1
NCMPR = SEQ // CAP - 1
NO_ROW = 1 << 14

C_DQ, C_DK, C_DV, C_NQ, C_KV = 0, 512, 1024, 1536, 2048
N_KV = 792
LEN = [P * (i + 1) for i in range(NT)]
QOFF = [P * i * (i + 1) // 2 for i in range(NT)]
TLEN = [SEQ - P * k for k in range(NT)]
TOFF = [sum(TLEN[:k]) for k in range(NT)]
NS = sum(LEN)

STEP_USES = (("A0", NT), ("A1", NT), ("NQ", 1), ("DV", 1), ("CMP", 1), ("S0", NT), ("S1", NT), ("DQ", 1),
             ("W0", NT), ("SUB", 1), ("W1", NT), ("DK", 1), ("ADA0", 1), ("ADA1", 1))


def first_uses(last):
    at, u = {}, 0
    for name, uses in STEP_USES:
        if not (last and name in ("DQ", "DK", "ADA0", "ADA1")):
            at[name] = u
            u += uses
    return at, u


USE, USES = first_uses(False)
LAST_USE, LAST_USES = first_uses(True)
PRE_USES = 20
ALL_USES = PRE_USES + (NJ - 1) * USES + LAST_USES
PRE_PROJ = 14
NBANK = 4
PRE_T = 10
T_USES = 22
N_SMALL = 13
N_CONST = 15
V_LOOP = 40
AHEAD = 1
OVF = 400


def build(nc, x, c, w_ada, b_ada, g_pre_mix, g_post_mix, g_pre_ffn, g_post_ffn, w_in,
          lam_q1, lam_k1, lam_q2, lam_k2, g_subln, cmp_pos_k, cmp_pos_v, cmp_w1_k, cmp_w1_v,
          cmp_w2_k, cmp_w2_v, w_out, w_router_grp, b_router_grp, w_router_exp, b_router_exp,
          w_exp_gate, w_exp_up, w_exp_down, out):
    with ExitStack() as ctx:
        def sb(name, shape, dt=F32):
            return ctx.enter_context(nc.sbuf_tensor(name, shape, dt))

        def sem(name):
            return ctx.enter_context(nc.semaphore(name))

        exp_w = sb("exp_w", [P, 2, 3 * 4096])
        stream = sb("stream", [P, 2, 4096])
        ov = sb("ov", [P, 8, SEQ])
        mods = sb("mods", [P, NJ, D])
        modsf = mods[:, :, :].rearrange("p a b -> p (a b)")
        xs = sb("xs", [P, NT, D])
        qdn = sb("qdn", [P, 4, SEQ])
        qd = qdn[:, 0:2, :]
        qn = qdn[:, 2:4, :]
        third = sb("third", [P, 4096])
        kd = third[:, 0:512]
        vd = third[:, 512:1024].rearrange("p (t n) -> p t n", t=NT)
        dist = third[:, 1024:1536]
        ada_acc = third[:, 1536:2560].rearrange("p (h n) -> p h n", h=2)
        w_r = third[:, 2560:2560 + DC * NR].rearrange("p (c n) -> p c n", c=DC)
        pc = third[:, 3136:3392].rearrange("p (h t n) -> p h t n", h=2, t=NT)
        dist_c = third[:, 3392:3520].rearrange("p (t n) -> p t n", t=NT)
        vcp = third[:, 3520:3648].rearrange("p (h n) -> p h n", h=2)
        kcp = third[:, 3648:3680]
        gates = third[:, 3680:3776].rearrange("p (h n) -> p h n", h=2)
        ident = sb("ident", [P, P])
        ones = sb("ones", [P, P])
        small = sb("small", [P, 512])
        bias_r = sb("bias_r", [P, NR])

        e1 = exp_w[:, 1, :]
        hT = e1[:, 0:4096].rearrange("p (c t) -> p c t", c=DC)
        prob = e1[:, 4096:4096 + 3 * NS].rearrange("p (b n) -> p b n", b=3)
        probT = [e1[:, 7936:7936 + NS], e1[:, 7936 + NS:7936 + 2 * NS], exp_w[:, 0, 12288 - NS:12288]]
        vsw = e1[:, 10496:10496 + 2 * SEQ].rearrange("p (w t n) -> p w t n", w=2, t=NT)
        cmp_w1 = e1[:, 4096:8192].rearrange("p (w b n) -> p w b n", w=2, b=16)
        ckp = e1[:, 8192:9728].rearrange("p (w h n) -> p w h n", w=2, h=3)
        cmp_h = e1[:, 9728:9856].rearrange("p (w n) -> p w n", w=2)
        cmp_g = e1[:, 9856:9984].rearrange("p (w n) -> p w n", w=2)
        cmp_w2 = e1[:, 9984:10112].rearrange("p (w n) -> p w n", w=2)
        pos_in = e1[0:16, 10112:10368].rearrange("p (w n) -> p w n", w=2)
        lam_in = e1[:, 10368:10624].rearrange("p (w n) -> p w n", w=4)
        lam_junk = e1[:, 10624:10752].rearrange("p (w n) -> p w n", w=2)
        sqv = e1[:, 11520:11520 + SEQ]
        b_rows = e1[:, 0:4 * D]
        g_rows = [exp_w[:, 0, 8192:8192 + D], exp_w[:, 0, 8192 + D:8192 + 2 * D], e1[:, 4 * D:5 * D]]
        w_kv = exp_w[:, 0, 4096:4096 + DC * N_KV].rearrange("p (c n) -> p c n", c=DC)
        ada_early = [exp_w[:, 0, 0:4096], stream[:, 0, :], stream[:, 1, :],
                     mods[:, :, :].rearrange("p a b -> p (a b)")]
        kslc = sb("kslc", [P, SEQ])
        kwin = sb("kwin", [P, SEQ])

        w_slot = stream[:, 0, :].rearrange("p (c n) -> p c n", c=DC)
        ada_slot = stream[:, 1, :].rearrange("p (c n) -> p c n", c=DC)
        wo = stream[:, :, :].rearrange("p a (c n) -> p (a c) n", c=4)

        cs = small[:, 0:8]
        craw = small[:, 8:16]
        cexp = small[:, 16:24]
        shc = small[:, 24:32]
        scc = small[:, 32:40]
        gpc = small[:, 40:48]
        bsh = small[:, 48:56]
        bsc = small[:, 56:64]
        ssq = small[:, 64:68]
        rstd = small[:, 68:72]
        slope = small[:, 72:75]
        qsc = small[:, 75:78]
        sl_r = small[:, 78:81]
        qs_r = small[:, 81:84]
        mx = small[:, 84:108].rearrange("p (m t) -> p m t", m=6)
        nmx = small[:, 108:132].rearrange("p (m t) -> p m t", m=6)
        lsum = small[:, 132:156].rearrange("p (m t) -> p m t", m=6)
        rl = small[:, 156:180].rearrange("p (m t) -> p m t", m=6)
        gcur = small[:, 180:204].rearrange("p (h b t) -> p h b t", h=2, b=3)
        cmx = small[:, 204:212]
        cl = small[:, 212:220]
        lam2 = small[:, 220:222]
        lame = small[:, 222:224]
        nlam = small[:, 224:225]
        gsub = small[:, 225:226]
        lamd = small[:, 228:229]
        ssq2 = small[:, 232:240]
        rstd2 = small[:, 240:248]
        wts = small[:, 248:256].rearrange("p (t k) -> p t k", k=2)
        pgrp = small[:, 256:260]
        rt = small[:, 260:292].rearrange("p (a t) -> p a t", t=NT)
        epsc = small[:, 292:293]
        extra_row = small[:, 296:360]
        ssq3 = small[:, 360:364]
        rstd3 = small[:, 364:368]
        key8 = small[:, 368:376]
        addr_f = small[:, 376:384]
        addr_i = sb("addr_i", [P, 8], I32)
        val_i = sb("val_i", [P, 8], I32)
        n_over = sb("n_over", [1, 1], I32)
        over_e = sb("over_e", [1, MAX_EXTRA + 1], I32)
        sidx = sb("sidx", [P, NCOL], I32)
        scol = sb("scol", [P, 2], I32)

        ovf = ov[:, :, :].rearrange("p a b -> p (a b)")
        hbuf = qdn[:, :, :].rearrange("p a b -> p (a b)")[:, 0:1536].rearrange("p (b n) -> p b n", b=2)
        sg = [hbuf[:, b, 0:256] for b in range(2)]
        hid = [hbuf[:, b, 256:512] for b in range(2)]
        hidT = [hbuf[:, b, 512:768] for b in range(2)]
        h2 = [ov[:, :, t * P:(t + 1) * P].rearrange("p c q -> p q c") for t in range(NT)]

        def h2_chunk(t, c_):
            return ov[:, c_, t * P:(t + 1) * P]

        streamf = stream[:, :, :].rearrange("p a b -> p (a b)")
        h2T = [e1[:, (8 + b) * D:(9 + b) * D].rearrange("p (c t) -> p c t", c=DC) for b in range(2)]
        xT = [modsf[:, b * 512:(b + 1) * 512] for b in range(2)]
        yb = [modsf[:, 1024 + b * 512:1536 + b * 512] for b in range(2)]
        sel2 = modsf[:, 2048:2560].rearrange("p (k t n) -> p k t n", k=2, t=NT)
        sel1 = [modsf[:, 2560 + b * 256:2816 + b * 256].rearrange("p (t n) -> p t n", t=NT) for b in range(2)]
        xg = qdn[:, 3, :]
        tmpx = ada_acc[:, :, :].rearrange("p a b -> p (a b)")
        sqj = qdn[:, 0:2, :]
        fsqj = tmpx
        ytok = [streamf[:, t * 2 * D:(t + 1) * 2 * D] for t in range(NT)]
        lg = qd[:, 0, 0:NT * NR].rearrange("p (t n) -> p t n", t=NT)
        ohg = qn[:, 0, 32:64].rearrange("p (t e) -> p t e", t=NT)
        eg = qn[:, 0, 64:96].rearrange("p (t e) -> p t e", t=NT)
        oh = [qn[:, 1, 0:256].rearrange("p (t e) -> p t e", t=NT),
              qn[:, 1, 256:512].rearrange("p (t e) -> p t e", t=NT)]
        lem = kd[:, 0:256].rearrange("p (t e) -> p t e", t=NT)
        sel = vd[:, :, :].rearrange("p t n -> p (t n)")[:, 0:256].rearrange("p (t e) -> p t e", t=NT)
        msum = vd[:, :, :].rearrange("p t n -> p (t n)")[:, 256:512].rearrange("p (t e) -> p t e", t=NT)
        earlier = kslc[:, NE:5 * NE].rearrange("p (t e) -> p t e", t=NT)
        cnt = kslc[:, 0:NE]
        cum = kwin[:, 64:128]
        key64 = kwin[:, 192:256]
        base_e = kwin[:, 256:320]
        slot_addr = kwin[:, 320:320 + CAP]
        rank8, base8, blk8 = kwin[:, 384:392], kwin[:, 392:400], kwin[:, 400:408]
        e8 = kwin[:, 408:416].rearrange("p (k t) -> p k t", k=2)
        over8 = kwin[:, 416:416 + 8 * NCMPR].rearrange("p (c m) -> p c m", m=NCMPR)
        oh2 = qn[:, 1, 0:512].rearrange("p (k t e) -> p k t e", k=2, t=NT)
        thr7 = kwin[:, 472:472 + NCMPR]
        kr = kwin[0:1, 480:480 + MAX_EXTRA + 1]
        pick = modsf[:, 0:512].rearrange("p (k t e) -> p k t e", k=2, t=NT)
        cmpx = modsf[:, 1024:2048]
        tri = dist[:, 0:P]

        ps = ctx.enter_context(nc.psum_tensor("ps", [P, 8, 512], F32))
        SB, TB, OD, ON = 0, 4, 6, 7

        y_d = nc.dram_tensor("y_d", (2 * 2 * SEQ, D // 2), F32, kind="Internal").ap()
        list_d = nc.dram_tensor("list_d", (CAP * NCOL, 1), I32, kind="Internal").ap()

        d_x, d_c, d_small, d_kv, d_w1 = sem("d_x"), sem("d_c"), sem("d_small"), sem("d_kv"), sem("d_w1")
        d_nv = sem("d_nv")
        d_ada0, d_ada3, d_win, d_ada = sem("d_ada0"), sem("d_ada3"), sem("d_win"), sem("d_ada")
        d_cols, d_wo, d_bc, d_bc_last = sem("d_cols"), sem("d_wo"), sem("d_bc"), sem("d_bc_last")
        d_gu = [sem("d_gu0"), sem("d_gu1"), sem("d_gu2")]
        d_wd = [sem("d_wd0"), sem("d_wd1"), sem("d_wd2")]
        k_ident, k_zero, k_const, k_router = sem("k_ident"), sem("k_zero"), sem("k_const"), sem("k_router")
        v_step, v_loop, p_step = sem("v_step"), sem("v_loop"), sem("p_step")
        cexp_ready, acc_ready, h_ready = sem("cexp_ready"), sem("acc_ready"), sem("h_ready")
        ssq_ready, ms_ready, rt_ready, rstd_ready, xn_ready = (
            sem("ssq_ready"), sem("ms_ready"), sem("rt_ready"), sem("rstd_ready"), sem("xn_ready"))
        cols_ready, gelu_ready, lam_ready, lame_ready, gexp_ready = (
            sem("cols_ready"), sem("gelu_ready"), sem("lam_ready"), sem("lame_ready"), sem("gexp_ready"))
        bank_full, bank_free = sem("bank_full"), sem("bank_free")
        tbank_full, tbank_free = sem("tbank_full"), sem("tbank_free")
        adacc_ready, neg_ready, exp_done, p_ready, values_done = (
            sem("adacc_ready"), sem("neg_ready"), sem("exp_done"), sem("p_ready"), sem("values_done"))
        cmp_sub, cmp_exp, sq_ready, subrt_ready, od_free, on_free = (
            sem("cmp_sub"), sem("cmp_exp"), sem("sq_ready"), sem("subrt_ready"), sem("od_free"), sem("on_free"))
        mods_ready, mix_full, mixsq, mixrt, x1_ready = (
            sem("mods_ready"), sem("mix_full"), sem("mixsq"), sem("mixrt"), sem("x1_ready"))
        x1sq, x1rt, h2_ready, h2T_full, h2T_ready, rout_full, lg_ready = (
            sem("x1sq"), sem("x1rt"), sem("h2_ready"), sem("h2T_full"),
            sem("h2T_ready"), sem("rout_full"), sem("lg_ready"))
        eg_in, eg_out, e2_in, e2_out, m_ready, earlier_ready, rank_full = (
            sem("eg_in"), sem("eg_out"), sem("e2_in"), sem("e2_out"), sem("m_ready"), sem("earlier_ready"),
            sem("rank_full"))
        lists_empty, lists_zeroed, lists_stored, lists_loaded, addr_ready, idx_ready, over_ready = (
            sem("lists_empty"), sem("lists_zeroed"), sem("lists_stored"), sem("lists_loaded"),
            sem("addr_ready"), sem("idx_ready"), sem("over_ready"))
        sel_ready, v_moe = sem("sel_ready"), sem("v_moe")
        y_out = [sem("y_out0"), sem("y_out1")]
        idx_cp, xg_full, xg_ready, xT_full, xT_ready, gu_done, sg_ready, hid_ready, hT_full, hidT_ready, d_done, y_ready = (
            sem("idx_cp"), sem("xg_full"), sem("xg_ready"), sem("xT_full"), sem("xT_ready"), sem("gu_done"),
            sem("sg_ready"), sem("hid_ready"), sem("hT_full"), sem("hidT_ready"), sem("d_done"), sem("y_ready"))
        scores_seen, copy_seen = sem("scores_seen"), sem("copy_seen")
        y_back = [sem(f"y_back{t}") for t in range(NT)]
        f_scaled, root_warm = sem("f_scaled"), sem("root_warm")
        y0_ready, f_ready, fsq, frt, o_ready, stored = (
            sem("y0_ready"), sem("f_ready"), sem("fsq"), sem("frt"), sem("o_ready"), sem("stored"))

        wg_v = w_exp_gate.rearrange("l e (p c) n -> (l e) p (c n)", p=P)
        wu_v = w_exp_up.rearrange("l e (p c) n -> (l e) p (c n)", p=P)
        wd_v = w_exp_down.rearrange("l e (h p j) n -> (l e h) p (j n)", h=2, p=P)
        gu_rooms = [exp_w[:, 0, 0:8192], exp_w[:, 1, 0:8192], streamf]
        gu_w = [a.rearrange("p (g c n) -> p g c n", g=2, c=DC) for a in gu_rooms]
        dn_rooms = [exp_w[:, 0, 8192:12288], exp_w[:, 1, 8192:12288], third]
        dn_w = [a.rearrange("p (h j n) -> p h j n", h=2, j=2) for a in dn_rooms[0:2]]
        dn_w.append(third[:, :].rearrange("p (h j n) -> p h j n", h=2, j=2))
        w_in_v = w_in[0].rearrange("(p c) n -> p c n", p=P)
        w_ada_v = w_ada[0].rearrange("(p c) n -> p c n", p=P)

        def xn(t):
            return ovf[:, t * D:(t + 1) * D]

        def one(ap):
            return ap.rearrange("a p n -> (a p) n")

        def load_gu(eng, e, room):
            eng.dma_start(gu_rooms[room][:, 0:4096], one(wg_v[bass.ds(e, 1)])).then_inc(d_gu[room], 16)
            eng.dma_start(gu_rooms[room][:, 4096:8192], one(wu_v[bass.ds(e, 1)])).then_inc(d_gu[room], 16)

        def load_wd(eng, e, room):
            for half in range(2):
                eng.dma_start(dn_rooms[room][:, half * 2048:(half + 1) * 2048],
                              one(wd_v[bass.ds(e * 2 + half, 1)])).then_inc(d_wd[room], 16)

        def load_dqk(eng, j):
            for i, o in enumerate((C_DQ, C_DK)):
                eng.dma_start(w_slot[:, :, i * P:(i + 1) * P], w_in_v[:, :, bass.ds(j * P + o, P)]).then_inc(d_win, 16)

        def load_nv(eng, j):
            eng.dma_start(w_slot[:, :, 256:384], w_in_v[:, :, bass.ds(j * P + C_DV, P)]).then_inc(d_nv, 16)
            for hd in range(2):
                eng.dma_start(w_slot[:, :, 384 + hd * HD:448 + hd * HD],
                              w_in_v[:, :, bass.ds(j * HD + (C_NQ + hd * 256), HD)]).then_inc(d_nv, 16)

        def bank_wait(eng, j, u):
            eng.wait_ge(bank_free, j * USES + (PRE_USES + u - NBANK + 1))

        MAPS = [(0, "A0", 0), (0, "A1", 1), (1, "S0", 2), (2, "S1", 0), (1, "W0", 1), (2, "W1", 2)]
        M_A0, M_A1, M_S0, M_S1, M_W0, M_W1 = range(6)
        T_A, T_S0, T_S1, T_W0, T_C, T_W1 = range(6)
        T_FIRST = [0, 4, 8, 12, 16, 18]
        V_A, V_S, V_C, V_W, V_STEP = 1, 2, 3, 4, 4

        block = ctx.enter_context(nc.Block())

        @block.sync
        def _(sp):
            sp.dma_start(craw, c.rearrange("a (p n) -> (a p) n", p=P)).then_inc(d_c, 16)
            for i, s in enumerate((d_ada0, d_win, d_ada, d_ada3)):
                if i == 1:
                    sp.dma_start(xs[:, :, :], x[0].rearrange("(t p) n -> p t n", p=P)).then_inc(d_x, 16)
                sp.dma_start(ada_early[i].rearrange("p (c n) -> p c n", c=DC),
                             w_ada_v[:, :, i * 512:(i + 1) * 512]).then_inc(s, 16)
            sp.dma_start(w_kv, w_in_v[:, :, C_KV:C_KV + N_KV]).then_inc(d_kv, 16)
            for i, w in enumerate((cmp_w1_k, cmp_w1_v)):
                sp.dma_start(cmp_w1[:, i], w[0].rearrange("(b p) n -> p b n", p=P)).then_inc(d_w1, 16)
            sp.wait_ge(acc_ready, 2)
            load_dqk(sp, 0)
            load_nv(sp, 0)
            sp.wait_ge(acc_ready, 3)

            def load_ada(h, half, used):
                sp.wait_ge(adacc_ready, used + AHEAD)
                sp.dma_start(ada_slot, w_ada_v[:, :, bass.ds(h * 512 + (2 * D + half * 512), 512)]).then_inc(d_ada, 16)

            for h in range(3):
                load_ada(h, 0, h)
            sp.wait_ge(bank_full, PRE_PROJ + 2)
            load_dqk(sp, 1)
            with sp.Fori(0, NJ - 2) as j:
                sp.wait_ge(bank_full, j * USES + (PRE_USES + USE["DV"] + 1))
                load_nv(sp, j + 1)
                load_ada(j * 2, 3, j * 2 + 3)
                sp.wait_ge(bank_full, j * USES + (PRE_USES + USE["DK"] + 1))
                load_dqk(sp, j + 2)
                load_ada(j * 2, 4, j * 2 + 4)
            sp.wait_ge(bank_full, (NJ - 2) * USES + PRE_USES + USE["DV"] + 1)
            load_nv(sp, NJ - 1)
            load_ada(2 * NJ - 1, 0, 2 * NJ - 1)
            sp.wait_ge(adacc_ready, 2 * NJ + AHEAD)
            for hd in range(2):
                sp.dma_start(wo[hd * HD:(hd + 1) * HD, 4:8, :],
                             w_out[0, 512 + hd * 256:768 + hd * 256, :].rearrange("(c p) n -> p c n", p=HD)).then_inc(d_wo, 16)
            sp.wait_ge(bank_full, (NJ - 1) * USES + PRE_USES + LAST_USE["DV"] + 1)
            sp.dma_start(wo[:, 0:4, :], w_out[0, 0:512, :].rearrange("(c p) n -> p c n", p=P)).then_inc(d_wo, 16)
            sp.dma_start(b_rows, b_ada[0:1, 2 * D:6 * D].to_broadcast([P, 4 * D])).then_inc(d_bc, 16)
            for row, v in zip(g_rows[0:2], (g_post_mix, g_pre_ffn)):
                sp.dma_start(row, v.to_broadcast([P, D])).then_inc(d_bc, 16)
            sp.wait_ge(on_free, NJ + AHEAD)
            sp.wait_ge(od_free, NJ + AHEAD)
            sp.dma_start(g_rows[2], g_post_ffn.to_broadcast([P, D])).then_inc(d_bc_last, 16)
            sp.wait_ge(mods_ready, 4)
            load_wd(sp, 0, 0)
            load_gu(sp, 1, 1)
            sp.wait_ge(mix_full, NT)
            load_gu(sp, 2, 2)
            sp.wait_ge(rout_full, NT)
            load_wd(sp, 1, 1)

            sp.wait_ge(rank_full, 2)
            load_wd(sp, 2, 2)

            sp.wait_ge(lists_stored, 2 * NT * 16)
            lv = list_d.rearrange("(s n) a -> s (n a)", n=NCOL)
            sp.dma_start(sidx[0:CAP, :], lv).then_inc(lists_loaded, 16)
            sp.dma_start(sidx[CAP:P, :], lv).then_inc(lists_loaded, 16)

            def weights_after(e, room, used):
                sp.wait_ge(gu_done, used)
                load_gu(sp, e, room)
                sp.wait_ge(d_done, used)
                load_wd(sp, e, room)

            for e in range(3, 9):
                weights_after(e, e % 3, e - 2)
            for e in (9, 10):
                weights_after(e, (e + 1) % 2, e - 2)
            with sp.Fori(0, (NE - 12) // 2) as g:
                for i in range(2):
                    weights_after(g * 2 + (11 + i), i, g * 2 + (10 + i))
            weights_after(NE - 1, 0, NE - 2)
            sp.wait_ge(over_ready, 2)
            n_blocks = sp.value_load(n_over[0:1, 0:1], min_val=0, max_val=MAX_EXTRA)

            def load_again(k, used):
                sp.wait_ge(over_ready, 2)
                e = sp.value_load(over_e[0:1, bass.ds(k, 1)], min_val=0, max_val=NE - 1)
                sp.wait_ge(gu_done, used)
                load_gu(sp, e, 1)
                sp.wait_ge(d_done, used)
                load_wd(sp, e, 1)

            with sp.If(n_blocks > 0):
                load_again(0, NE - 1)
            with sp.Fori(1, MAX_EXTRA) as k:
                with sp.If(k < n_blocks):
                    load_again(k, k + NE)
            sp.wait_ge(y_out[1], 16 * (NE // 2))
            sp.wait_ge(y_out[0], n_blocks * 16 + 16 * (NE // 2))
            for t in range(NT):
                for kk in range(2):
                    r0 = 2 * (kk * SEQ + t * P)
                    sp.dma_start(ytok[t][:, kk * D:(kk + 1) * D],
                                 y_d[r0:r0 + 2 * P, :].rearrange("(p h) n -> p (h n)", h=2)).then_inc(y_back[t], 16)
            for t in range(NT):
                sp.wait_ge(o_ready, t + 1)
                sp.dma_start(out[0, t * P:(t + 1) * P, :], xs[:, t, :]).then_inc(stored, 16)
            sp.wait_ge(stored, 16 * NT)

        @block.gpsimd
        def _(pool):
            steps = [0]

            def step(ins):
                steps[0] += 1
                ins.then_inc(p_step, 1)
                pool.wait_ge(p_step, steps[0])

            small_loads = [(gsub, g_subln.rearrange("a p -> p a")),
                           (pos_in[:, 0, :], cmp_pos_k[0].rearrange("(b r) d -> b (r d)", r=2)),
                           (pos_in[:, 1, :], cmp_pos_v[0].rearrange("(b r) d -> b (r d)", r=2)),
                           (cmp_w2[:, 0, :], cmp_w2_k[0]), (cmp_w2[:, 1, :], cmp_w2_v[0])]
            small_loads += [(lam_in[:, i, :], v.to_broadcast([P, HD])) for i, v in enumerate((lam_q1, lam_k1, lam_q2, lam_k2))]
            small_loads += [(w_r[:, :, 0:NG], w_router_grp[0].rearrange("(p n) g -> p n g", p=P)),
                            (w_r[:, :, NG:NR], w_router_exp[0].rearrange("(p n) g -> p n g", p=P)),
                            (bias_r[:, 0:NG], b_router_grp.to_broadcast([P, NG])),
                            (bias_r[:, NG:NR], b_router_exp.to_broadcast([P, NE]))]
            assert len(small_loads) == N_SMALL
            step(pool.memset(ident[:, :], 0.0))
            pool.affine_select(out=ident[:, :], in_=ident[:, :], compare_op=ALU.not_equal, fill=1.0, base=0,
                               pattern=[[-1, P]], channel_multiplier=1).then_inc(k_ident, 1)
            pool.memset(ones[:, :], 1.0).then_inc(k_ident, 1)
            pool.memset(qdn[:, :, :], 0.0).then_inc(k_zero, 1)
            pool.memset(kcp[:, :], 0.0).then_inc(k_zero, 1)
            pool.memset(vcp[:, :, :], 0.0).then_inc(k_zero, 1)
            pool.memset(ckp[:, :, 2, :], 0.0).then_inc(k_zero, 1)
            for tile_, vals in ((slope, (1.0, 1.0, 2.0 ** -4)), (sl_r, (0.25, 0.5, 0.5)),
                                (qsc, (SCALE, SCALE, SCALE * 16)), (qs_r, (4.0, 2.0, 2.0))):
                for i, v in enumerate(vals):
                    pool.memset(tile_[:, i:i + 1], v).then_inc(k_const, 1)
            pool.memset(epsc, EPS).then_inc(k_const, 1)
            step(pool.iota(dist[:, :], pattern=[[1, SEQ]], base=-(SEQ - P), channel_multiplier=-1,
                           allow_small_or_imprecise_dtypes=True))
            pool.affine_select(out=dist[:, :], in_=dist[:, :], compare_op=ALU.is_ge, fill=NEG, base=SEQ - P,
                               pattern=[[-1, SEQ]], channel_multiplier=1).then_inc(k_const, 1)
            step(pool.iota(dist_c[:, :, :], pattern=[[-P, NT], [CMP_STRIDE, NCP]], base=CMP_BLOCK - 1,
                           channel_multiplier=-1, allow_small_or_imprecise_dtypes=True))
            pool.affine_select(out=dist_c[:, :, :], in_=dist_c[:, :, :], compare_op=ALU.is_ge, fill=NEG,
                               base=-(CMP_BLOCK - 1), pattern=[[P, NT], [-CMP_STRIDE, NCP]],
                               channel_multiplier=1).then_inc(k_const, 1)
            for dst, src in small_loads:
                pool.dma_start(dst, src).then_inc(d_small, 16)
            pool.iota(val_i[:, :], pattern=[[SEQ, 2], [P, NT]], base=0, channel_multiplier=1).then_inc(p_step, 1)
            steps[0] += 1
            pool.memset(sidx[0:CAP, :], NO_ROW).then_inc(lists_empty, 1)
            pool.wait_ge(lists_empty, 1)
            pool.dma_start(list_d.rearrange("(s n) a -> s (n a)", n=NCOL), sidx[0:CAP, :]).then_inc(lists_zeroed, 16)

            pool.wait_ge(on_free, NJ + AHEAD)
            pool.wait_ge(od_free, NJ + AHEAD)
            step(pool.memset(tri, 1.0))
            pool.affine_select(out=tri, in_=tri, compare_op=ALU.is_gt, fill=0.0, base=0,
                               pattern=[[1, P]], channel_multiplier=-1).then_inc(k_router, 1)
            pool.iota(key64, pattern=[[-1, NE]], base=NE, channel_multiplier=0,
                      allow_small_or_imprecise_dtypes=True).then_inc(k_router, 1)
            pool.iota(key8, pattern=[[-1, NG]], base=NG, channel_multiplier=0,
                      allow_small_or_imprecise_dtypes=True).then_inc(k_router, 1)
            pool.iota(thr7, pattern=[[CAP, NCMPR]], base=CAP, channel_multiplier=0,
                      allow_small_or_imprecise_dtypes=True).then_inc(k_router, 1)
            pool.iota(kr, pattern=[[1, MAX_EXTRA + 1]], base=0, channel_multiplier=0,
                      allow_small_or_imprecise_dtypes=True).then_inc(k_router, 1)
            pool.iota(slot_addr, pattern=[[NCOL, CAP]], base=0, channel_multiplier=0,
                      allow_small_or_imprecise_dtypes=True).then_inc(k_router, 1)

            pool.wait_ge(addr_ready, 1)
            pool.wait_ge(lists_zeroed, 16)
            for i in range(2 * NT):
                pool.indirect_dma_start(list_d, bass.IndirectOffsetOnAxis(addr_i[:, i:i + 1], 0), val_i[:, i:i + 1], None,
                                        bounds_check=CAP * NCOL - 1, oob_is_err=False).then_inc(lists_stored, 16)

            scatter_max = pool.to_reg(4 * SEQ - 1)

            def scatter_rows(column, b, copied, copies, full):
                pool.tensor_copy(scol[:, b:b + 1], sidx[:, column]).then_inc(copied, 1)
                pool.wait_ge(copied, copies)
                pool.sem_inc(copy_seen, 1)
                pool.indirect_dma_start(y_d, bass.IndirectOffsetOnAxis(scol[:, b:b + 1], 0), yb[b], None,
                                        bounds_check=scatter_max, oob_is_err=False).then_inc(full, 16)

            pool.wait_ge(idx_ready, 2)
            for b in range(2):
                pool.wait_ge(y_ready, b + 1)
                scatter_rows(slice(b, b + 1), b, idx_cp, b + 1, y_out[b])
            with pool.Fori(1, NE // 2) as g:
                for b in range(2):
                    pool.wait_ge(y_ready, g * 2 + (b + 1))
                    pool.wait_ge(y_out[b], g * 16)
                    scatter_rows(bass.ds(g * 2 + b, 1), b, idx_cp, g * 2 + (b + 1), y_out[b])

            for b in range(2):
                pool.wait_ge(y_out[b], 16 * (NE // 2))
            pool.wait_ge(over_ready, 2)
            n_blocks = pool.value_load(n_over[0:1, 0:1], min_val=0, max_val=MAX_EXTRA)

            def overflow_rows(k):
                pool.wait_ge(y_ready, k + (NE + 1))
                pool.wait_ge(y_out[0], k * 16 + 16 * (NE // 2))
                scatter_rows(bass.ds(k + NE, 1), 0, idx_cp, k + (NE + 1), y_out[0])
                pool.wait_ge(over_ready, 2)

            with pool.If(n_blocks > 0):
                overflow_rows(0)
            with pool.If(n_blocks > 1):
                with pool.Fori(1, MAX_EXTRA) as k:
                    with pool.If(k < n_blocks):
                        overflow_rows(k)

            for t in range(NT - 1):
                pool.wait_ge(f_ready, t + 1)
                pool.tensor_tensor(ytok[t][:, D:2 * D], ytok[t][:, 0:D], mods[:, 3, :], ALU.mult).then_inc(f_scaled, 1)

        @block.tensor
        def _(pe):

            def mm(out_, lhsT, rhs, start=True, stop=True):
                return pe.matmul(out_, lhsT, rhs, start=start, stop=stop, skip_group_check=True)

            lo, hi = slice(0, HD), slice(HD, P)
            pe.wait_ge(k_ident, 2)
            def ada_columns(i):
                pe.wait_ge(acc_ready, i + 1)
                for c_ in range(DC):
                    ins = mm(ps[i % 2 * HD:(i % 2 + 1) * HD, SB + i // 2, c_:c_ + 1], ada_acc[:, i % 2, c_::DC], ones[:, 0:1])
                ins.then_inc(bank_full, 1)

            ada_columns(0)
            ada_columns(1)
            for c_ in range(DC):
                if c_ >= 2:
                    pe.wait_ge(tbank_free, c_ - 1)
                for t in range(NT):
                    pe.wait_ge(xn_ready, t + 1)
                    ins = pe.transpose(ps[:, TB + c_ % 2, t * P:(t + 1) * P], xn(t)[:, c_::DC], ident[:, :])
                ins.then_inc(tbank_full, 1)
            ada_columns(2)
            ada_columns(3)
            pe.wait_ge(d_kv, 16)
            for i, o in enumerate((0, 128, 256, 512)):
                pe.wait_ge(bank_free, i + 1)
                for c_ in range(DC):
                    if i == 0:
                        pe.wait_ge(h_ready, c_ + 1)
                    ins = mm(ps[:, SB + i, :], w_kv[:, c_, o:o + P], hT[:, c_, :], c_ == 0, c_ == DC - 1)
                ins.then_inc(bank_full, 1)
            pe.wait_ge(d_small, 16 * N_SMALL)
            for w in range(2):
                pe.transpose(ps[:, TB + w, 0:16], pos_in[:, w, :], ident[0:16, 0:16]).then_inc(tbank_full, 1)
            for t in range(NT):
                pe.wait_ge(bank_free, 4 + t + 1)
                for o, n, at in ((384, 128, 0), (640, 152, 128)):
                    for c_ in range(DC):
                        ins = mm(ps[:, SB + t, at:at + n], hT[:, c_, t * P:(t + 1) * P], w_kv[:, c_, o:o + n],
                                 c_ == 0, c_ == DC - 1)
                ins.then_inc(bank_full, 1)
            pe.wait_ge(d_w1, 32)
            pe.wait_ge(tbank_free, PRE_T)
            for w in range(2):
                pe.wait_ge(bank_free, 8 + w + 1)
                for b in range(16):
                    ins = mm(ps[:, SB + w, 0:3 * NCMP].rearrange("p (h n) -> p h n", h=3), cmp_w1[:, w, b, :],
                             ckp[:, w, :, b:b + 8 * (NCMP - 1) + 1:8], b == 0, b == 15)
                ins.then_inc(bank_full, 1)

            def project(name, u):
                if name == "DV":
                    for t in range(NT):
                        for c_ in range(DC):
                            ins = mm(ps[:, SB + u % NBANK, t * P:(t + 1) * P], hT[:, c_, t * P:(t + 1) * P],
                                     w_slot[:, c_, 256:384], c_ == 0, c_ == DC - 1)
                else:
                    o = {"DQ": 0, "DK": 128, "NQ": 384}[name]
                    for c_ in range(DC):
                        ins = mm(ps[:, SB + u % NBANK, :], w_slot[:, c_, o:o + P], hT[:, c_, :], c_ == 0, c_ == DC - 1)
                ins.then_inc(bank_full, 1)

            pe.wait_ge(d_win, 48)
            for i, name in enumerate(("DQ", "DK")):
                pe.wait_ge(bank_free, PRE_PROJ + i - NBANK + 1)
                project(name, PRE_PROJ + i)
            pe.wait_ge(gelu_ready, 2)
            pe.wait_ge(bank_free, 13)
            for h, rows in enumerate((lo, hi)):
                ins = mm(ps[rows, SB, 0:NCMP], cmp_w2[:, 0, :], cmp_g[:, 0, h * NCMP:(h + 1) * NCMP])
            ins.then_inc(bank_full, 1)
            pe.wait_ge(bank_free, 14)
            for h in range(2):
                ins = mm(ps[0:NCMP, SB + 1, h * HD:(h + 1) * HD], cmp_g[:, 1, h * NCMP:(h + 1) * NCMP], cmp_w2[:, 1, :])
            ins.then_inc(bank_full, 1)
            for half in range(2):
                pe.wait_ge(adacc_ready, half + 1 + AHEAD)
                pe.wait_ge(bank_free, 15 + half)
                mm(ps[:, SB + 2 + half, :], ones[:, :], ada_acc[:, half, :]).then_inc(bank_full, 1)
            pe.wait_ge(bank_full, PRE_USES)
            pe.sem_inc(values_done, AHEAD)
            pe.wait_ge(bank_free, PRE_USES)

            def head_step(j, last):
                at = LAST_USE if last else USE

                def bank(u):
                    return SB + u % NBANK

                def scores(m, q, k):
                    u = at[MAPS[m][1]]
                    for i in range(NT):
                        bank_wait(pe, j, u + i)
                        mm(ps[:, bank(u + i), 0:LEN[i]], q[:, i * P:(i + 1) * P], k[:, 0:LEN[i]]).then_inc(bank_full, 1)

                def heads(name):
                    bank_wait(pe, j, at[name])
                    project(name, at[name])

                def turn(unit, buf, k_tiles):
                    pe.wait_ge(p_ready, j * 6 + (unit + 1))
                    for k in k_tiles:
                        pe.wait_ge(tbank_free, j * T_USES + (PRE_T + T_FIRST[unit] + k - 1))
                        for i in range(k, NT):
                            ins = pe.transpose(ps[:, TB + k % 2, (i - k) * P:(i - k + 1) * P],
                                               prob[:, buf, QOFF[i] + k * P:QOFF[i] + (k + 1) * P], ident[:, :])
                        ins.then_inc(tbank_full, 1)

                def values(bank_, heads_, first):
                    for k in range(NT):
                        for unit, rows, v in heads_:
                            pe.wait_ge(tbank_free, j * T_USES + (PRE_T + T_FIRST[unit] + k + 1))
                            ins = mm(ps[rows, bank_, k * P:SEQ], v(k), probT[unit % 3][:, TOFF[k]:TOFF[k] + TLEN[k]],
                                     first and k == 0, k == NT - 1)
                    ins.then_inc(values_done, 1)

                def nsa_values(w, units, first):
                    values(ON, [(units[0], lo, lambda k: vsw[:, w, k, lo]), (units[1], hi, lambda k: vsw[:, w, k, hi])], first)

                pe.wait_ge(bank_free, j * USES + (PRE_USES + USE["DK"] + 1 - USES))
                scores(M_A0, qd[:, 0, :], kd)
                scores(M_A1, qd[:, 1, :], kd)
                pe.wait_ge(d_nv, j * 48 + 48)
                heads("NQ")
                heads("DV")
                pe.wait_ge(bank_free, j * USES + (PRE_USES + at["NQ"] + 1))
                bank_wait(pe, j, at["CMP"])
                for hd in range(2):
                    for i in range(NT):
                        ins = mm(ps[:, bank(at["CMP"]), (hd * NT + i) * NCP:(hd * NT + i + 1) * NCP],
                                 qn[:, hd, i * P:(i + 1) * P], kcp[:, :])
                ins.then_inc(bank_full, 1)
                scores(M_S0, qn[:, 0, :], kslc)
                turn(T_A, 0, (0, 1))
                scores(M_S1, qn[:, 1, :], kslc)
                turn(T_A, 0, (2, 3))
                pe.wait_ge(od_free, j + AHEAD)
                pe.wait_ge(bank_free, j * USES + (PRE_USES + at["DV"] + 1))
                values(OD, [(T_A, slice(0, P), lambda k: vd[:, k, :])], True)
                if not last:
                    pe.wait_ge(d_win, j * 32 + 80)
                    heads("DQ")
                turn(T_S0, 2, (0, 1))
                scores(M_W0, qn[:, 0, :], kwin)
                turn(T_S0, 2, (2, 3))
                pe.wait_ge(sq_ready, j + 1)
                bank_wait(pe, j, at["SUB"])
                mm(ps[:, bank(at["SUB"]), :], ones[:, :], sqv).then_inc(bank_full, 1)
                turn(T_S1, 0, (0, 1))
                scores(M_W1, qn[:, 1, :], kwin)
                turn(T_S1, 0, (2, 3))
                pe.wait_ge(on_free, j + AHEAD)
                nsa_values(0, (T_S0, T_S1), True)
                if not last:
                    heads("DK")

                def ada_row(half):
                    if not last:
                        u = at["ADA0"] + half
                        pe.wait_ge(adacc_ready, j * 2 + (half + 3 + AHEAD))
                        bank_wait(pe, j, u)
                        mm(ps[:, bank(u), :], ones[:, :], ada_acc[:, half, :]).then_inc(bank_full, 1)

                turn(T_W0, 1, (0, 1))
                ada_row(0)
                turn(T_W0, 1, (2, 3))
                pe.wait_ge(p_ready, j * 6 + (T_C + 1))
                for hd in range(2):
                    pe.wait_ge(tbank_free, j * T_USES + (PRE_T + T_FIRST[T_C] + hd - 1))
                    for i in range(NT):
                        ins = pe.transpose(ps[0:NCP, TB + hd, i * P:(i + 1) * P], pc[:, hd, i, :], ident[:, :])
                    ins.then_inc(tbank_full, 1)
                for hd, rows in enumerate((lo, hi)):
                    pe.wait_ge(tbank_free, j * T_USES + (PRE_T + T_FIRST[T_C] + hd + 1))
                    ins = mm(ps[rows, ON, :], vcp[:, hd, :], probT[T_C % 3][:, hd * SEQ:(hd + 1) * SEQ], False, True)
                ins.then_inc(values_done, 1)
                turn(T_W1, 2, (0, 1))
                ada_row(1)
                turn(T_W1, 2, (2, 3))
                nsa_values(1, (T_W0, T_W1), False)

            with pe.Fori(0, NJ - 1) as j:
                head_step(j, False)
            head_step(NJ - 1, True)

            pe.wait_ge(bank_free, ALL_USES)
            pe.wait_ge(od_free, NJ + AHEAD)
            pe.wait_ge(on_free, NJ + AHEAD)
            pe.wait_ge(d_wo, 48)

            def mixer(t, halves=(0, 1)):
                for n in halves:
                    for c_ in range(DC):
                        ins = mm(ps[:, 2 * t + n, :], ov[:, c_, t * P:(t + 1) * P], wo[:, c_, n * 512:(n + 1) * 512],
                                 c_ == 0, c_ == DC - 1)
                if halves[-1] == 1:
                    ins.then_inc(mix_full, 1)

            def turn_h2(t):
                pe.wait_ge(h2_ready, t + 1)
                for c_ in range(DC):
                    ins = pe.transpose(ps[:, 2 * t + c_ // 4, (c_ % 4) * P:(c_ % 4 + 1) * P], h2_chunk(t, c_), ident[:, :])
                ins.then_inc(h2T_full, 1)

            def logits(t):
                pe.wait_ge(h2T_ready, t + 1)
                for c_ in range(DC):
                    ins = mm(ps[:, 2 * t, 0:NR], h2T[t % 2][:, c_, :], w_r[:, c_, :], c_ == 0, c_ == DC - 1)
                ins.then_inc(rout_full, 1)

            mixer(0)
            mixer(1)
            for t in range(2, NT):
                turn_h2(t - 2)
                mixer(t, (0,))
                logits(t - 2)
                mixer(t, (1,))
            turn_h2(NT - 2)
            logits(NT - 2)
            turn_h2(NT - 1)
            logits(NT - 1)
            pe.wait_ge(m_ready, 1)
            pe.wait_ge(k_router, 6)
            mm(ps[:, 0, 0:NT * NE], tri, msum.rearrange("p t e -> p (t e)"), True, False)
            pe.wait_ge(earlier_ready, 1)
            mm(ps[:, 0, NE:NT * NE], ones[:, :], earlier[:, 0:NT - 1, :].rearrange("p t e -> p (t e)"), False, True).then_inc(rank_full, 1)
            mm(ps[:, 1, 0:NE], ones[:, :], earlier[:, NT - 1, :]).then_inc(rank_full, 1)

            def gather(b):
                for t in range(NT):
                    for h, rows in enumerate((lo, hi)):
                        ins = mm(ps[rows, 0, :].rearrange("p (c q) -> p c q", c=4), sel1[b][:, t, :],
                                 ov[:, 4 * h:4 * h + 4, t * P:(t + 1) * P], t == 0, t == NT - 1)
                ins.then_inc(xg_full, 1)

            def turn_rows():
                for i in range(4):
                    ins = pe.transpose(ps[:, 1, i * P:(i + 1) * P], xg[:, i * P:(i + 1) * P], ident[:, :])
                ins.then_inc(xT_full, 1)

            def gate_up(b, room, done):
                for c_ in range(DC):
                    for h, rows in enumerate((lo, hi)):
                        ins = mm(ps[rows, 2 + b, :].rearrange("p (g n) -> p g n", g=2), xT[b][:, c_ % 4 * P + c_ // 4 * CAP:c_ % 4 * P + (c_ // 4 + 1) * CAP],
                                 gu_w[room][:, :, c_, h * 256:(h + 1) * 256], c_ == 0, c_ == DC - 1)
                ins.then_inc(done, 1)

            def turn_hidden(b, done):
                for jj in range(2):
                    ins = pe.transpose(ps[:, 4 + b, jj * P:(jj + 1) * P], hid[b][:, jj::2], ident[:, :])
                ins.then_inc(done, 1)

            def down(b, room, done):
                for i in range(4):
                    hf, jj = i // 2, i % 2
                    for n, rows in enumerate((lo, hi)):
                        ins = mm(ps[rows, 6 + b, :], hidT[b][:, jj * P + hf * CAP:jj * P + (hf + 1) * CAP],
                                 dn_w[room][:, hf, jj, n * 512:(n + 1) * 512], i == 0, i == 3)
                ins.then_inc(done, 1)

            def expert(e, b, room, use, following, down_first=False):
                def gather_next():
                    pe.wait_ge(sel_ready, e + 2)
                    gather(following)

                def turn_next():
                    pe.wait_ge(xg_ready, e + 2)
                    turn_rows()

                pe.wait_ge(xT_ready, e + 1)
                pe.wait_ge(d_gu[room], use * 32 + 32)
                gate_up(b, room, gu_done)
                if not down_first:
                    gather_next()
                pe.wait_ge(hid_ready, e + 1)
                turn_hidden(b, hT_full)
                if not down_first:
                    turn_next()
                pe.wait_ge(hidT_ready, e + 1)
                pe.wait_ge(d_wd[room], use * 32 + 32)
                down(b, room, d_done)
                if down_first:
                    gather_next()
                    turn_next()

            pe.wait_ge(sel_ready, 1)
            gather(0)
            pe.wait_ge(xg_ready, 1)
            turn_rows()
            for e in range(9):
                expert(e, e % 2, e % 3, e // 3, 1 - e % 2)
            with pe.Fori(0, (NE - 10) // 2) as g:
                for i in range(2):
                    expert(g * 2 + (9 + i), 1 - i, i, g + 3, i)
            expert(NE - 1, 1, 0, NE // 2 - 2, 0)
            pe.wait_ge(over_ready, 2)
            n_blocks = pe.value_load(n_over[0:1, 0:1], min_val=0, max_val=MAX_EXTRA)

            def overflow_block(k):
                pe.wait_ge(y_ready, k + NE)
                expert(k + NE, 0, 1, k + (NE // 2 - 2), 0, down_first=True)
                pe.wait_ge(over_ready, 2)

            with pe.If(n_blocks > 0):
                overflow_block(0)
            with pe.If(n_blocks > 1):
                with pe.Fori(1, MAX_EXTRA) as k:
                    with pe.If(k < n_blocks):
                        overflow_block(k)

        @block.scalar
        def _(act):
            act.sem_inc(on_free, AHEAD)

            def cols(v):
                return v.rearrange("a (p n) -> (a p) n", p=P)

            for dst, src in ((gpc, g_pre_mix), (bsh, b_ada[0:1, 0:D]), (bsc, b_ada[0:1, D:2 * D])):
                act.dma_start(dst, cols(src)).then_inc(d_cols, 16)
            act.wait_ge(d_c, 16)
            act.activation(cexp, craw, ACT.Exp, scale=-1.0).then_inc(cexp_ready, 1)
            act.wait_ge(d_x, 16)
            for t in range(NT):
                act.activation(xn(t), xs[:, t, :], ACT.Square, accum_out=ssq[:, t:t + 1]).then_inc(ssq_ready, 1)
            act.wait_ge(ms_ready, 1)
            act.activation(rstd, ssq, ACT.Sqrt).then_inc(rt_ready, 1)
            act.wait_ge(rstd_ready, 1)
            for t in range(NT):
                act.wait_ge(ssq_ready, t + 1)
                act.activation(xn(t), xs[:, t, :], ACT.Copy, scale=rstd[:, t:t + 1]).then_inc(xn_ready, 1)
            for c_ in range(DC):
                act.wait_ge(tbank_full, c_ + 1)
                act.activation(hT[:, c_, :], ps[:, TB + c_ % 2, :], ACT.Copy).then_inc(tbank_free, 1)
            act.wait_ge(k_zero, 4)
            for w in range(2):
                act.wait_ge(tbank_full, DC + w + 1)
                act.activation(ckp[:, w, 2, 0:16], ps[:, TB + w, 0:16], ACT.Copy).then_inc(tbank_free, 1)
            act.wait_ge(lam_ready, 2)
            act.activation(lame, lam2, ACT.Exp).then_inc(lame_ready, 1)
            act.wait_ge(bank_free, 12)
            act.activation(gates[:, :, :], gates[:, :, :], ACT.Exp, scale=-1.0).then_inc(gexp_ready, 1)
            for w in range(2):
                act.wait_ge(bank_free, 12 + w + 1)
                act.activation(cmp_g[:, w, 0:62], cmp_h[:, w, 0:62], ACT.Gelu_apprx_tanh,
                               bias=cmp_h[:, w, 62:63]).then_inc(gelu_ready, 1)
            act.wait_ge(bank_full, 12)
            load_gu(act, 0, 0)
            act.wait_ge(bank_full, PRE_USES)

            def head_step(j, last):
                at = LAST_USE if last else USE

                def exps(m):
                    act.wait_ge(neg_ready, j * 6 + (m + 1))
                    for i in range(NT):
                        p_ = prob[:, MAPS[m][2], QOFF[i]:QOFF[i] + LEN[i]]
                        ins = act.activation(p_, p_, ACT.Exp, bias=nmx[:, m, i:i + 1], accum_out=lsum[:, m, i:i + 1])
                    ins.then_inc(exp_done, 1)

                def buffer_used(unit):
                    act.wait_ge(values_done, j * V_STEP + (AHEAD + (0, 0, 0, V_A, V_S, V_S)[unit]))

                def take(unit, k_tiles=range(NT)):
                    buffer_used(unit)
                    for k in k_tiles:
                        act.wait_ge(tbank_full, j * T_USES + (PRE_T + T_FIRST[unit] + k + 1))
                        act.activation(probT[unit % 3][:, TOFF[k]:TOFF[k] + TLEN[k]], ps[:, TB + k % 2, 0:TLEN[k]],
                                       ACT.Copy).then_inc(tbank_free, 1)

                exps(M_A0)
                exps(M_A1)
                act.wait_ge(cmp_sub, j + 1)
                for hd in range(2):
                    p_ = pc[:, hd, :, :]
                    ins = act.activation(p_, p_, ACT.Exp, scale=slope[:, 1 + hd:2 + hd])
                ins.then_inc(cmp_exp, 1)
                take(T_A, (0, 1))
                exps(M_S0)
                take(T_A, (2, 3))
                act.wait_ge(values_done, j * V_STEP + (AHEAD + V_A))
                act.wait_ge(od_free, j + AHEAD)
                act.activation(sqv, ps[:, OD, :], ACT.Square).then_inc(sq_ready, 1)
                exps(M_S1)
                take(T_S0)
                exps(M_W0)
                take(T_S1)
                act.wait_ge(bank_free, j * USES + (PRE_USES + at["SUB"] + 1))
                act.activation(sqv, sqv, ACT.Sqrt).then_inc(subrt_ready, 1)
                exps(M_W1)
                take(T_W0)
                buffer_used(T_C)
                for hd in range(2):
                    act.wait_ge(tbank_full, j * T_USES + (PRE_T + T_FIRST[T_C] + hd + 1))
                    act.activation(probT[T_C % 3][0:NCP, hd * SEQ:(hd + 1) * SEQ], ps[0:NCP, TB + hd, :],
                                   ACT.Copy).then_inc(tbank_free, 1)
                take(T_W1)
                act.wait_ge(values_done, j * V_STEP + (AHEAD + V_W))
                act.activation(ovf[:, bass.ds(j * SEQ + 4 * SEQ, SEQ)], ps[:, ON, :], ACT.Copy).then_inc(on_free, 1)

            with act.Fori(0, NJ - 1) as j:
                head_step(j, False)
            head_step(NJ - 1, True)

            def take_h2T(t):
                act.wait_ge(h2T_full, t + 1)
                if t >= 2:
                    act.wait_ge(rout_full, t - 1)
                act.activation(h2T[t % 2], ps[:, 2 * t:2 * t + 2, :].rearrange("p a (c n) -> p (a c) n", c=4),
                               ACT.Copy).then_inc(h2T_ready, 1)

            def root_mean(out_, sums):
                return act.activation(out_, sums, ACT.Sqrt, scale=1.0 / D, bias=epsc)

            act.wait_ge(k_const, N_CONST)
            act.wait_ge(mods_ready, 4)
            for t in range(NT):
                act.wait_ge(mix_full, t + 1)
                act.activation(sqj, ps[:, 2 * t:2 * t + 2, :], ACT.Square, accum_out=ssq2[:, t:t + 1]).then_inc(mixsq, 1)
                act.wait_ge(mixsq, t + 1)
                root_mean(rstd2[:, t:t + 1], ssq2[:, t:t + 1]).then_inc(mixrt, 1)
                if t:
                    take_h2T(t - 1)
                act.wait_ge(x1_ready, t + 1)
                act.activation(sqj, xs[:, t, :].rearrange("p (a b) -> p a b", a=2), ACT.Square,
                               accum_out=ssq2[:, 4 + t:5 + t]).then_inc(x1sq, 1)
                act.wait_ge(x1sq, t + 1)
                root_mean(rstd2[:, 4 + t:5 + t], ssq2[:, 4 + t:5 + t]).then_inc(x1rt, 1)
            take_h2T(NT - 1)
            act.wait_ge(eg_in, 1)
            act.activation(eg, eg, ACT.Exp).then_inc(eg_out, 1)
            act.wait_ge(e2_in, 1)
            act.activation(rt[:, 4, :], rt[:, 4, :], ACT.Exp).then_inc(e2_out, 1)

            def take_rows(e, b):
                act.wait_ge(xg_full, e + 1)
                act.activation(xg, ps[:, 0, :], ACT.Copy).then_inc(xg_ready, 1)
                act.wait_ge(xT_full, e + 1)
                act.activation(xT[b], ps[:, 1, :], ACT.Copy).then_inc(xT_ready, 1)

            def expert(e, b, following, buffer_free, down_first=False):
                act.wait_ge(gu_done, e + 1)
                act.activation(sg[b], ps[:, 2 + b, 0:256], ACT.Silu).then_inc(sg_ready, 1)
                if not down_first:
                    take_rows(e + 1, following)
                act.wait_ge(d_done, e + 1)
                if buffer_free is not None:
                    act.wait_ge(y_out[b], buffer_free)
                act.activation(yb[b], ps[:, 6 + b, :], ACT.Copy).then_inc(y_ready, 1)
                if down_first:
                    take_rows(e + 1, following)

            act.wait_ge(addr_ready, 1)
            take_rows(0, 0)
            for b in range(2):
                expert(b, b, 1 - b, None)
            with act.Fori(1, NE // 2) as g:
                for b in range(2):
                    expert(g * 2 + b, b, 1 - b, g * 16)
            act.wait_ge(over_ready, 2)
            n_blocks = act.value_load(n_over[0:1, 0:1], min_val=0, max_val=MAX_EXTRA)

            def overflow_block(k):
                expert(k + NE, 0, 0, k * 16 + 16 * (NE // 2), down_first=True)

            with act.If(n_blocks > 0):
                overflow_block(0)
            with act.If(n_blocks > 1):
                with act.Fori(1, MAX_EXTRA) as k:
                    with act.If(k < n_blocks):
                        overflow_block(k)

            def root(t):
                act.wait_ge(f_ready, t + 1)
                act.activation(fsqj, ytok[t][:, 0:D], ACT.Square, accum_out=ssq3[:, t:t + 1]).then_inc(fsq, 1)
                act.wait_ge(fsq, t + 1)
                root_mean(rstd3[:, t:t + 1], ssq3[:, t:t + 1]).then_inc(frt, 1)

            act.activation(rstd3[:, 0:1], epsc, ACT.Sqrt).then_inc(root_warm, 1)
            act.wait_ge(root_warm, 1)
            for t in range(NT):
                act.wait_ge(y_back[t], 32)
                y0 = ytok[t][:, 0:D]
                act.activation(y0, y0, ACT.Copy, scale=wts[:, t, 0:1]).then_inc(y0_ready, 1)
                if t:
                    root(t - 1)
            root(NT - 1)

        @block.vector
        def _(dve):
            dve.sem_inc(adacc_ready, AHEAD)
            dve.sem_inc(od_free, AHEAD)
            steps = [0]

            def step(ins):
                steps[0] += 1
                ins.then_inc(v_step, 1)
                dve.wait_ge(v_step, steps[0])

            def mean_square(ap, n):
                return dve.tensor_scalar(ap, ap, 1.0 / n, EPS, ALU.mult, ALU.add)

            dve.wait_ge(cexp_ready, 1)
            step(dve.tensor_scalar(cexp, cexp, 1.0, None, ALU.add))
            step(dve.reciprocal(cexp, cexp))
            step(dve.tensor_tensor(cs, craw, cexp, ALU.mult))

            def weigh(buf, w, advance, last):
                advance(dve.tensor_scalar(ada_acc[:, buf, :], w[:, 0, :], cs[:, 0:1], None, ALU.mult))
                for c_ in range(1, DC):
                    ins = dve.scalar_tensor_tensor(ada_acc[:, buf, :], w[:, c_, :], cs[:, c_:c_ + 1],
                                                   ada_acc[:, buf, :], ALU.mult, ALU.add)
                    if c_ < DC - 1:
                        advance(ins)
                ins.then_inc(last, 1)

            for i, s in enumerate((d_ada0, d_win, d_ada, d_ada3)):
                dve.wait_ge(s, 16)
                if i >= 2:
                    dve.wait_ge(bank_full, i - 1)
                weigh(i % 2, ada_early[i].rearrange("p (c n) -> p c n", c=DC), step, acc_ready)
                if i == 0:
                    dve.wait_ge(ssq_ready, NT)
                    mean_square(ssq, D).then_inc(ms_ready, 1)
                    dve.wait_ge(rt_ready, 1)
                    dve.reciprocal(rstd, rstd).then_inc(rstd_ready, 1)
            dve.wait_ge(d_cols, 48)
            dve.wait_ge(bank_full, 4)
            step(dve.tensor_tensor(bsc, bsc, ps[:, SB + 1, 0:DC], ALU.add))
            dve.scalar_tensor_tensor(scc, bsc, 1.0, gpc, ALU.add, ALU.mult).then_inc(cols_ready, 1)
            dve.tensor_tensor(shc, ps[:, SB, 0:DC], bsh, ALU.add).then_inc(cols_ready, 1)
            dve.wait_ge(cols_ready, 2)
            for c_ in range(DC):
                dve.wait_ge(tbank_free, c_ + 1)
                dve.tensor_scalar(hT[:, c_, :], hT[:, c_, :], scc[:, c_:c_ + 1], shc[:, c_:c_ + 1], ALU.mult,
                                  ALU.add).then_inc(h_ready, 1)
            for i in range(4):
                dve.sem_inc(bank_free, 1)
            dve.wait_ge(d_small, 16 * N_SMALL)
            for i in range(2):
                dve.tensor_tensor_reduce(lam_junk[:, i, :], lam_in[:, 2 * i, :], lam_in[:, 2 * i + 1, :], 1.0, 0.0,
                                         ALU.mult, ALU.add, lam2[:, i:i + 1]).then_inc(lam_ready, 1)
            step(dve.tensor_scalar(gsub, gsub, 1.0 - LAMBDA_INIT, None, ALU.mult))

            dve.wait_ge(k_zero, 4)
            for w in range(2):
                dve.wait_ge(bank_full, 4 + w + 1)
                for h, rows in enumerate((slice(0, HD), slice(HD, P))):
                    for par, to in enumerate((slice(0, HD), slice(HD, P))):
                        ins = dve.tensor_copy(ckp[to, w, h, :], ps[rows, SB + w, par::2])
                ins.then_inc(bank_free, 1)
            for i, k_ in ((2, kslc), (3, kwin)):
                dve.wait_ge(bank_full, 4 + i + 1)
                dve.tensor_copy(k_[:, :], ps[:, SB + i, :]).then_inc(bank_free, 1)
            dve.wait_ge(d_ada, 32)
            weigh(0, ada_slot, step, adacc_ready)
            gv = gates[:, :, :].rearrange("p h (n t) -> p h n t", t=NT)
            for t in range(NT):
                dve.wait_ge(bank_full, 8 + t + 1)
                dve.tensor_copy(vsw[:, :, t, :], ps[:, SB + t, 0:256].rearrange("p (w n) -> p w n", w=2))
                dve.tensor_copy(gv[:, :, :, t], ps[:, SB + t, 256:280].rearrange("p (h n) -> p h n", h=2)).then_inc(bank_free, 1)
            dve.wait_ge(d_ada, 48)
            weigh(1, ada_slot, step, adacc_ready)
            for w in range(2):
                dve.wait_ge(bank_full, 12 + w + 1)
                dve.tensor_copy(cmp_h[:, w, 0:63], ps[:, SB + w, 0:63]).then_inc(bank_free, 1)
            dve.wait_ge(gexp_ready, 1)
            step(dve.tensor_scalar(gates[:, :, :], gates[:, :, :], 1.0, None, ALU.add))
            step(dve.reciprocal(gates[:, :, :], gates[:, :, :]))
            dve.wait_ge(lame_ready, 1)
            step(dve.tensor_tensor(lamd, lame[:, 0:1], lame[:, 1:2], ALU.subtract))
            step(dve.tensor_scalar(nlam, lamd, -1.0, -LAMBDA_INIT, ALU.mult, ALU.add))

            def drain(name, u):
                src = ps[:, SB + u % NBANK, :]
                if name in ("DQ", "NQ"):
                    q, (c0, c1) = (qd, (0, 0)) if name == "DQ" else (qn, (1, 2))
                    dve.tensor_scalar(q[0:HD, 0, :], src[0:HD], qsc[0:HD, c0:c0 + 1], None, ALU.mult)
                    ins = dve.tensor_scalar(q[HD:P, 1, :], src[HD:P], qsc[HD:P, c1:c1 + 1], None, ALU.mult)
                elif name == "DK":
                    ins = dve.tensor_copy(kd[:, :], src)
                else:
                    ins = dve.tensor_copy(vd[:, :, :].rearrange("p t n -> p (t n)"), src)
                ins.then_inc(bank_free, 1)

            dve.wait_ge(k_const, N_CONST)
            step(dve.tensor_tensor(qsc, qsc, qs_r, ALU.mult))
            for i, name in enumerate(("DQ", "DK")):
                dve.wait_ge(bank_full, PRE_PROJ + i + 1)
                drain(name, PRE_PROJ + i)
            dve.wait_ge(bank_full, 17)
            dve.tensor_copy(kcp[:, 0:NCMP], ps[:, SB, 0:NCMP]).then_inc(bank_free, 1)
            dve.wait_ge(bank_full, 18)
            dve.tensor_copy(vcp[0:NCMP, :, :], ps[0:NCMP, SB + 1, 0:P].rearrange("p (h n) -> p h n", h=2)).then_inc(bank_free, 1)
            for half in range(2):
                dve.wait_ge(bank_full, 19 + half)
                dve.tensor_copy(modsf[:, half * 512:(half + 1) * 512], ps[:, SB + 2 + half, :]).then_inc(bank_free, 1)

            def head_step(j, last):
                at = LAST_USE if last else USE
                n = [0]

                def lstep(ins):
                    n[0] += 1
                    ins.then_inc(v_loop, 1)
                    dve.wait_ge(v_loop, j * V_LOOP + n[0])

                def full(u):
                    dve.wait_ge(bank_full, j * USES + (PRE_USES + u + 1))

                def self_read(u):
                    dve.wait_ge(bank_free, j * USES + (PRE_USES + u + 1))

                def bank(u):
                    return SB + u % NBANK

                def heads(name):
                    full(at[name])
                    drain(name, at[name])

                def biased(m, buf_free):
                    col_, name, buf = MAPS[m]
                    u = at[name]
                    dve.wait_ge(tbank_full, j * T_USES + (PRE_T + buf_free))
                    for i in range(NT):
                        full(u + i)
                        dve.sem_inc(scores_seen, 1)
                        dve.tensor_tensor_reduce(prob[:, buf, QOFF[i]:QOFF[i] + LEN[i]], ps[:, bank(u + i), 0:LEN[i]],
                                                 dist[:, SEQ - LEN[i]:SEQ], slope[:, col_:col_ + 1], -3.0e38, ALU.add,
                                                 ALU.max, mx[:, m, i:i + 1]).then_inc(bank_free, 1)
                    self_read(u + NT - 1)
                    dve.tensor_scalar(nmx[:, m, :], mx[:, m, :], -1.0, None, ALU.mult).then_inc(neg_ready, 1)

                def weighted(m, g_):
                    buf = MAPS[m][2]
                    dve.wait_ge(exp_done, j * 6 + (m + 1))
                    lstep(dve.tensor_scalar(rl[:, m, :], lsum[:, m, :], SUM_FLOOR, None, ALU.max))
                    lstep(dve.reciprocal(rl[:, m, :], rl[:, m, :]))
                    lstep(dve.tensor_tensor(rl[:, m, :], rl[:, m, :], g_, ALU.mult))
                    for i in range(NT):
                        p_ = prob[:, buf, QOFF[i]:QOFF[i] + LEN[i]]
                        ins = dve.tensor_scalar(p_, p_, rl[:, m, i:i + 1], None, ALU.mult)
                    ins.then_inc(p_ready, 1)

                dve.tensor_tensor(slope, slope, sl_r, ALU.mult).then_inc(v_loop, 1)
                n[0] += 1
                lstep(dve.tensor_copy(gcur.rearrange("p h b t -> p h (b t)"), gates[:, :, bass.ds(j * 12, 12)]))
                biased(M_A0, T_FIRST[T_W0] + NT - T_USES)
                biased(M_A1, T_FIRST[T_W0] + NT - T_USES)
                dve.wait_ge(exp_done, j * 6 + 2)
                lstep(dve.tensor_scalar(rl[:, 0:2, :], lsum[:, 0:2, :], SUM_FLOOR, None, ALU.max))
                lstep(dve.reciprocal(rl[:, 0:2, :], rl[:, 0:2, :]))
                lstep(dve.tensor_scalar(rl[:, 1, :], rl[:, 1, :], nlam, None, ALU.mult))
                for i in range(NT):
                    p1 = prob[:, 1, QOFF[i]:QOFF[i] + LEN[i]]
                    ins = dve.tensor_scalar(p1, p1, rl[:, 1, i:i + 1], None, ALU.mult)
                lstep(ins)
                for i in range(NT):
                    p0, p1 = (prob[:, b, QOFF[i]:QOFF[i] + LEN[i]] for b in range(2))
                    ins = dve.scalar_tensor_tensor(p0, p0, rl[:, 0, i:i + 1], p1, ALU.mult, ALU.add)
                ins.then_inc(p_ready, 1)
                heads("NQ")
                if not last:
                    dve.wait_ge(d_ada, j * 32 + 64)
                    weigh(0, ada_slot, lstep, adacc_ready)
                heads("DV")
                full(at["CMP"])
                for hd in range(2):
                    ins = dve.tensor_tensor(pc[:, hd, :, :], ps[:, bank(at["CMP"]), hd * P:(hd + 1) * P].rearrange(
                        "p (t n) -> p t n", t=NT), dist_c[:, :, :], ALU.add)
                ins.then_inc(bank_free, 1)
                self_read(at["CMP"])
                pc8 = pc[:, :, :, :].rearrange("p h t n -> p (h t) n")
                lstep(dve.tensor_reduce(cmx, pc8, AX, ALU.max))
                lstep(dve.tensor_scalar(cmx, cmx, MAX_FLOOR, None, ALU.max))
                dve.tensor_tensor(pc8, pc8, cmx.unsqueeze(2).to_broadcast([P, 8, NCP]), ALU.subtract).then_inc(cmp_sub, 1)
                biased(M_S0, 0)
                biased(M_S1, T_FIRST[T_A] + NT)
                weighted(M_S0, gcur[:, 0, 1, :])
                weighted(M_S1, gcur[:, 1, 1, :])
                if not last:
                    lstep(dve.tensor_tensor(qsc, qsc, qs_r, ALU.mult))
                    heads("DQ")
                biased(M_W0, T_FIRST[T_A] + NT)
                full(at["SUB"])
                dve.tensor_scalar(sqv, ps[:, bank(at["SUB"]), :], 1.0 / P, EPS, ALU.mult, ALU.add).then_inc(bank_free, 1)
                biased(M_W1, T_FIRST[T_S0] + NT)
                weighted(M_W0, gcur[:, 0, 2, :])
                dve.wait_ge(cmp_exp, j + 1)
                lstep(dve.tensor_reduce(cl, pc8, AX, ALU.add))
                lstep(dve.tensor_scalar(cl, cl, SUM_FLOOR, None, ALU.max))
                lstep(dve.reciprocal(cl, cl))
                clv = cl.rearrange("p (h t) -> p h t", h=2)
                lstep(dve.tensor_tensor(clv, clv, gcur[:, :, 0, :], ALU.mult))
                dve.tensor_tensor(pc8, pc8, cl.unsqueeze(2).to_broadcast([P, 8, NCP]), ALU.mult).then_inc(p_ready, 1)
                weighted(M_W1, gcur[:, 1, 2, :])

                def ada_row(half):
                    full(at["ADA0"] + half)
                    dve.tensor_copy(modsf[:, bass.ds(j * D + (D + half * 512), 512)],
                                    ps[:, bank(at["ADA0"] + half), :]).then_inc(bank_free, 1)

                if not last:
                    dve.wait_ge(d_ada, j * 32 + 80)
                    weigh(1, ada_slot, lstep, adacc_ready)
                    heads("DK")
                    ada_row(0)
                dve.wait_ge(subrt_ready, j + 1)
                lstep(dve.reciprocal(sqv, sqv))
                dve.scalar_tensor_tensor(ovf[:, bass.ds(j * SEQ, SEQ)], ps[:, OD, :], gsub, sqv, ALU.mult,
                                         ALU.mult).then_inc(od_free, 1)
                if not last:
                    ada_row(1)
                assert last or n[0] == V_LOOP, n[0]

            with dve.Fori(0, NJ - 1) as j:
                head_step(j, False)
            head_step(NJ - 1, True)

            dve.wait_ge(d_bc, 16 * 3)
            dve.wait_ge(bank_free, ALL_USES)
            step(dve.tensor_tensor(modsf, modsf, b_rows, ALU.add))
            dve.tensor_tensor(mods[:, 0, :], mods[:, 0, :], g_rows[0], ALU.mult).then_inc(mods_ready, 1)
            dve.scalar_tensor_tensor(mods[:, 2, :], mods[:, 2, :], 1.0, g_rows[1], ALU.add, ALU.mult).then_inc(mods_ready, 1)
            dve.wait_ge(d_bc_last, 16)
            dve.tensor_tensor(mods[:, 3, :], mods[:, 3, :], g_rows[2], ALU.mult).then_inc(mods_ready, 2)
            dve.wait_ge(mods_ready, 4)

            mixv = [ps[:, 2 * t:2 * t + 2, :] for t in range(NT)]
            for t in range(NT):
                dve.wait_ge(mixsq, t + 1)
                step(dve.tensor_tensor(tmpx.rearrange("p (a b) -> p a b", a=2), mixv[t],
                                       mods[:, 0, :].rearrange("p (a b) -> p a b", a=2), ALU.mult))
                dve.wait_ge(mixrt, t + 1)
                step(dve.reciprocal(rstd2[:, t:t + 1], rstd2[:, t:t + 1]))
                dve.scalar_tensor_tensor(xs[:, t, :], tmpx, rstd2[:, t:t + 1], xs[:, t, :], ALU.mult, ALU.add).then_inc(x1_ready, 1)
                dve.wait_ge(x1_ready, t + 1)
                step(dve.tensor_tensor(h2[t], xs[:, t, :].rearrange("p (q c) -> p q c", c=DC),
                                       mods[:, 2, :].rearrange("p (q c) -> p q c", c=DC), ALU.mult))
                dve.wait_ge(x1rt, t + 1)
                step(dve.reciprocal(rstd2[:, 4 + t:5 + t], rstd2[:, 4 + t:5 + t]))
                dve.scalar_tensor_tensor(h2[t], h2[t], rstd2[:, 4 + t:5 + t],
                                         mods[:, 1, :].rearrange("p (q c) -> p q c", c=DC), ALU.mult, ALU.add).then_inc(h2_ready, 1)

            for t in range(NT):
                dve.wait_ge(rout_full, t + 1)
                dve.tensor_tensor(lg[:, t, :], ps[:, 2 * t, 0:NR], bias_r[:, :], ALU.add).then_inc(lg_ready, 1)
            dve.wait_ge(lg_ready, NT)
            dve.wait_ge(k_router, 6)
            b8, b64 = [P, NT, NG], [P, NT, NE]
            mg, v1, v2 = rt[:, 0, :], rt[:, 2, :], rt[:, 3, :]
            e2 = rt[:, 4, :]

            def wide(ap, shape):
                return ap.unsqueeze(2).to_broadcast(shape)

            def first_max(onehot, vals, mval, keyrow, shape, kk_):
                step(dve.tensor_tensor(onehot, vals, wide(mval, shape), ALU.is_equal))
                step(dve.tensor_tensor(onehot, onehot, keyrow.unsqueeze(1).to_broadcast(shape), ALU.mult))
                step(dve.tensor_reduce(kk_, onehot, AX, ALU.max))
                step(dve.tensor_tensor(onehot, onehot, wide(kk_, shape), ALU.is_equal))

            step(dve.tensor_reduce(mg, lg[:, :, 0:NG], AX, ALU.max))
            dve.tensor_tensor(eg, lg[:, :, 0:NG], wide(mg, b8), ALU.subtract).then_inc(eg_in, 1)
            first_max(ohg, lg[:, :, 0:NG], mg, key8, b8, rt[:, 1, :])
            b88 = [P, NT, NG, NE // NG]
            le4, lem4, sel4 = (a.rearrange("p t (g e) -> p t g e", g=NG) for a in (lg[:, :, NG:NR], lem, sel))
            oh4 = ohg.unsqueeze(3).to_broadcast(b88)
            step(dve.tensor_tensor(lem4, le4, oh4, ALU.mult))
            step(dve.tensor_scalar(sel4, oh4, 1.0, -NEG, ALU.subtract, ALU.mult))
            step(dve.tensor_tensor(lem4, lem4, sel4, ALU.add))
            step(dve.tensor_reduce(v1, lem, AX, ALU.max))
            first_max(oh[0], lem, v1, key64, b64, rt[:, 5, :])
            step(dve.scalar_tensor_tensor(lem, oh[0], 4.0 * NEG, lem, ALU.mult, ALU.add))
            step(dve.tensor_reduce(v2, lem, AX, ALU.max))
            first_max(oh[1], lem, v2, key64, b64, rt[:, 6, :])
            dve.tensor_tensor(msum, oh[0], oh[1], ALU.add).then_inc(m_ready, 1)
            dve.tensor_tensor(e2, v2, v1, ALU.subtract).then_inc(e2_in, 1)
            dve.wait_ge(m_ready, 1)
            dve.tensor_copy(earlier[:, 0, :], msum[:, 0, :]).then_inc(v_step, 1)
            steps[0] += 1
            step(dve.tensor_tensor(earlier[:, 1, :], msum[:, 0, :], msum[:, 1, :], ALU.add))
            step(dve.tensor_tensor(earlier[:, 2, :], earlier[:, 1, :], msum[:, 2, :], ALU.add))
            dve.tensor_tensor(earlier[:, 3, :], earlier[:, 2, :], msum[:, 3, :], ALU.add).then_inc(earlier_ready, 1)
            dve.wait_ge(eg_out, 1)
            step(dve.tensor_reduce(pgrp, eg, AX, ALU.add))
            dve.wait_ge(e2_out, 1)
            step(dve.tensor_scalar(mg, e2, 1.0, None, ALU.add))
            step(dve.tensor_tensor(mg, mg, pgrp, ALU.mult))
            step(dve.reciprocal(wts[:, :, 0], mg))
            step(dve.tensor_tensor(wts[:, :, 1], wts[:, :, 0], e2, ALU.mult))

            step(dve.tensor_scalar(e8, rt[:, 5:7, :], -1.0, float(NE), ALU.mult, ALU.add))
            b2 = [P, 2, NT, NE]

            def of_chosen(out_, table):
                step(dve.tensor_tensor(pick, oh2, table, ALU.mult))
                step(dve.tensor_reduce(out_.rearrange("p (k t) -> p k t", k=2), pick, AX, ALU.add))

            def one_hots(b, count, done):
                av = addr_f.rearrange("p (k t) -> p k t", k=2)
                moved_on(dve.tensor_tensor(sel2, av.unsqueeze(3).to_broadcast([P, 2, NT, CAP]),
                                           slot_addr.unsqueeze(1).unsqueeze(1).to_broadcast([P, 2, NT, CAP]),
                                           ALU.is_equal), count)
                dve.tensor_tensor(sel1[b], sel2[:, 0], sel2[:, 1], ALU.add).then_inc(done, 1)

            def moved_on(ins, count):
                ins.then_inc(v_moe, 1)
                dve.wait_ge(v_moe, count)

            def next_column(count):
                moved_on(dve.tensor_scalar(addr_f, addr_f, 1.0, None, ALU.subtract), count)

            dve.wait_ge(rank_full, 1)
            of_chosen(rank8, ps[:, 0, 0:NT * NE].rearrange("p (t e) -> p t e", t=NT).unsqueeze(1).to_broadcast(b2))
            e8f = e8.rearrange("p k t -> p (k t)")
            step(dve.scalar_tensor_tensor(addr_f, rank8, float(NCOL), e8f, ALU.mult, ALU.add))
            one_hots(0, 1, sel_ready)
            dve.wait_ge(rank_full, 2)
            step(dve.tensor_copy(cnt, ps[:, 1, 0:NE]))
            thr3 = thr7.unsqueeze(2).to_broadcast([P, NCMPR, NE])
            cmp3 = cmpx[:, 0:NCMPR * NE].rearrange("p (m e) -> p m e", m=NCMPR)
            step(dve.tensor_tensor(cmp3, cnt.unsqueeze(1).to_broadcast([P, NCMPR, NE]), thr3, ALU.is_gt))
            step(dve.tensor_reduce(extra_row, cmp3.rearrange("p m e -> p e m"), AX, ALU.add))
            step(dve.tensor_tensor_scan(cum, ones[:, 0:NE], extra_row, 0.0, ALU.mult, ALU.add))
            step(dve.tensor_tensor(base_e, cum, extra_row, ALU.subtract))
            of_chosen(base8, base_e.unsqueeze(1).unsqueeze(1).to_broadcast(b2))
            step(dve.tensor_tensor(over8, rank8.unsqueeze(2).to_broadcast([P, 8, NCMPR]),
                                   thr7.unsqueeze(1).to_broadcast([P, 8, NCMPR]), ALU.is_ge))
            step(dve.tensor_reduce(blk8, over8, AX, ALU.add))
            dve.scalar_tensor_tensor(rank8, blk8, -float(CAP), rank8, ALU.mult, ALU.add).then_inc(v_step, 1)
            steps[0] += 1
            step(dve.scalar_tensor_tensor(base8, base8, float(NE - 1), blk8, ALU.add, ALU.add))
            dve.tensor_scalar(blk8, blk8, 1.0, None, ALU.min).then_inc(v_step, 1)
            steps[0] += 1
            step(dve.tensor_tensor(base8, base8, e8f, ALU.subtract))
            step(dve.tensor_tensor(base8, base8, blk8, ALU.mult))
            step(dve.tensor_tensor(base8, base8, e8f, ALU.add))
            step(dve.scalar_tensor_tensor(addr_f, rank8, float(NCOL), base8, ALU.mult, ALU.add))
            dve.tensor_copy(addr_i[:, :], addr_f).then_inc(addr_ready, 1)

            dve.wait_ge(addr_ready, 1)
            next_column(2)
            oe = cmpx[0:1, 0:(MAX_EXTRA + 1) * NE].rearrange("p (k e) -> p k e", e=NE)
            step(dve.tensor_tensor(oe, cum[0:1, :].unsqueeze(1).to_broadcast([1, MAX_EXTRA + 1, NE]),
                                   kr.unsqueeze(2).to_broadcast([1, MAX_EXTRA + 1, NE]), ALU.is_le))
            step(dve.tensor_reduce(small[0:1, OVF:OVF + MAX_EXTRA + 1], oe, AX, ALU.add))
            dve.tensor_scalar(over_e[0:1, :], small[0:1, OVF:OVF + MAX_EXTRA + 1], float(NE - 1), None, ALU.min).then_inc(over_ready, 1)
            dve.tensor_copy(n_over[0:1, 0:1], cum[0:1, NE - 1:NE]).then_inc(over_ready, 1)
            def expert(e, b, following):
                dve.wait_ge(xg_full, e + 1)
                one_hots(following, e * 2 + 3, sel_ready)
                next_column(e * 2 + 4)
                dve.wait_ge(sg_ready, e + 1)
                dve.tensor_tensor(hid[b], sg[b], ps[:, 2 + b, 256:512], ALU.mult).then_inc(hid_ready, 1)
                dve.wait_ge(hT_full, e + 1)
                dve.tensor_copy(hidT[b], ps[:, 4 + b, 0:256]).then_inc(hidT_ready, 1)

            expert(0, 0, 1)
            dve.wait_ge(lists_loaded, 32)
            dve.tensor_scalar(sidx[0:CAP, :], sidx[0:CAP, :], 2.0, None, ALU.mult).then_inc(idx_ready, 1)
            dve.tensor_scalar(sidx[CAP:P, :], sidx[CAP:P, :], 2.0, 1.0, ALU.mult, ALU.add).then_inc(idx_ready, 1)
            expert(1, 1, 0)
            with dve.Fori(1, NE // 2) as g:
                for b in range(2):
                    expert(g * 2 + b, b, 1 - b)
            dve.wait_ge(over_ready, 2)
            n_blocks = dve.value_load(n_over[0:1, 0:1], min_val=0, max_val=MAX_EXTRA)

            def overflow_block(k):
                expert(k + NE, 0, 0)

            with dve.If(n_blocks > 0):
                overflow_block(0)
            with dve.If(n_blocks > 1):
                with dve.Fori(1, MAX_EXTRA) as k:
                    with dve.If(k < n_blocks):
                        overflow_block(k)

            def finish(t):
                dve.wait_ge(frt, t + 1)
                step(dve.reciprocal(rstd3[:, t:t + 1], rstd3[:, t:t + 1]))
                dve.wait_ge(f_scaled, t + 1)
                dve.scalar_tensor_tensor(xs[:, t, :], ytok[t][:, D:2 * D], rstd3[:, t:t + 1], xs[:, t, :], ALU.mult,
                                         ALU.add).then_inc(o_ready, 1)

            for t in range(NT):
                y0, y1 = ytok[t][:, 0:D], ytok[t][:, D:2 * D]
                dve.wait_ge(y0_ready, t + 1)
                dve.scalar_tensor_tensor(y0, y1, wts[:, t, 1:2], y0, ALU.mult, ALU.add).then_inc(f_ready, 1)
                if t:
                    finish(t - 1)
            dve.wait_ge(f_ready, NT)
            dve.tensor_tensor(ytok[NT - 1][:, D:2 * D], ytok[NT - 1][:, 0:D], mods[:, 3, :], ALU.mult).then_inc(f_scaled, 1)
            finish(NT - 1)


_INS = ['x', 'c', 'w_ada', 'b_ada', 'g_pre_mix', 'g_post_mix', 'g_pre_ffn', 'g_post_ffn', 'w_in',
        'lam_q1', 'lam_k1', 'lam_q2', 'lam_k2', 'g_subln', 'cmp_pos_k', 'cmp_pos_v', 'cmp_w1_k', 'cmp_w1_v',
        'cmp_w2_k', 'cmp_w2_v', 'w_out', 'w_router_grp', 'b_router_grp', 'w_router_exp', 'b_router_exp',
        'w_exp_gate', 'w_exp_up', 'w_exp_down']


def kernel(**inputs):
    import numpy as _np
    import concourse.bacc as _bacc
    from concourse import mybir as _mybir
    from concourse.bass_utils import run_bass_kernel_spmd as _run

    nc = _bacc.Bacc("TRN2", target_bir_lowering=False, num_devices=1)
    arrays, args = {}, []
    for name in _INS:
        a = _np.ascontiguousarray(inputs[name])
        arrays[f"in_{name}_dram"] = a
        args.append(nc.dram_tensor(f"in_{name}_dram", a.shape, _mybir.dt.from_np(a.dtype), kind="ExternalInput").ap())
    args.append(nc.dram_tensor("out_dram", (1, SEQ, D), F32, kind="ExternalOutput").ap())
    build(nc, *args)
    r = _run(nc, [arrays], core_ids=[0])
    return r.results[0]["out_dram"]
```
